# Optimizing a Trainium2 kernel written in Bass

```python
import jax, jax.numpy as jnp
from jax import lax
import numpy as np

D_MODEL = 1024
BATCH = 1
SEQ = 128
DEPTH = 1
DEC_BATCH = 1
DEC_SEQ = 512
PAST_LEN = 128

GRID_W = 64
SSD_EXPAND = 2
SSD_D_INNER = SSD_EXPAND * D_MODEL
SSD_HEADDIM = 64
SSD_HEADS = SSD_D_INNER // SSD_HEADDIM
SSD_GROUPS = 8
D_STATE = 128
CONV_W = 5
CHUNK = 128
XBC_DIM = SSD_D_INNER + 2 * SSD_GROUPS * D_STATE
N_HEADS = 16
N_KV_HEADS = 4
HEAD_DIM = D_MODEL // N_HEADS
Q_BLOCK = 128
ROPE_THETA = 10000.0
N_KEYS = 128
N_EXPERTS = N_KEYS * N_KEYS
PEER_HEADS = 8
PEER_TOPK = 16
PEER_DQ = 256
TOK_BLOCK = 128
EPS = 1e-6

IN_SIZES = (SSD_D_INNER, XBC_DIM, SSD_HEADS, SSD_HEADS, N_HEADS * HEAD_DIM,
            N_KV_HEADS * HEAD_DIM, N_KV_HEADS * HEAD_DIM, D_MODEL, D_MODEL)
IN_DIM = SSD_D_INNER + XBC_DIM + 2 * SSD_HEADS + N_HEADS * HEAD_DIM + 2 * N_KV_HEADS * HEAD_DIM + 2 * D_MODEL

kernel_name = "hybrid_ssd_gqa_peer_diffusion_step"

def rmsnorm(x, w):
    xf = x.astype(jnp.float32)
    y = xf * lax.rsqrt(jnp.mean(xf * xf, axis=-1, keepdims=True) + EPS)
    return (y * w.astype(jnp.float32)).astype(x.dtype)

def modulate(x, shift, scale):
    return x * (1 + scale) + shift

def depthwise_conv(x, w, b):
    pad = CONV_W // 2
    y = lax.conv_general_dilated(x, w.astype(x.dtype)[:, None, :], window_strides=(1,),
                                 padding=[(pad, pad)], dimension_numbers=('NWC', 'WIO', 'NWC'),
                                 feature_group_count=x.shape[-1])
    return y + b

def ssd_scan(x, dt, a_log, b_in, c_in, init_state):
    f32 = jnp.float32
    dtype = x.dtype
    bsz, t, h, p = x.shape
    nc = t // CHUNK
    rep = h // b_in.shape[2]
    A = -jnp.exp(a_log.astype(f32))
    Bh = jnp.repeat(b_in.astype(f32), rep, axis=2).reshape(bsz, nc, CHUNK, h, -1)
    Ch = jnp.repeat(c_in.astype(f32), rep, axis=2).reshape(bsz, nc, CHUNK, h, -1)
    dtf = dt.astype(f32)
    xdt = (x.astype(f32) * dtf[..., None]).reshape(bsz, nc, CHUNK, h, p)
    a_cs = jnp.cumsum((dtf * A).reshape(bsz, nc, CHUNK, h), axis=2)
    seg = a_cs[:, :, :, None, :] - a_cs[:, :, None, :, :]
    lower = jnp.tril(jnp.ones((CHUNK, CHUNK), dtype=bool))[None, None, :, :, None]
    decay_in = jnp.exp(jnp.where(lower, seg, -jnp.inf))
    scores = jnp.einsum('bclhn,bcshn->bclsh', Ch, Bh)
    y_diag = jnp.einsum('bclsh,bcshp->bclhp', scores * decay_in, xdt)
    decay_to_end = jnp.exp(a_cs[:, :, -1:, :] - a_cs)
    chunk_states = jnp.einsum('bclhn,bclh,bclhp->bchpn', Bh, decay_to_end, xdt)
    chunk_decay = jnp.exp(a_cs[:, :, -1, :])

    def step(s, inp):
        st, dc = inp
        return s * dc[:, :, None, None] + st, s

    final, prev = lax.scan(step, init_state.astype(f32),
                           (jnp.moveaxis(chunk_states, 1, 0), jnp.moveaxis(chunk_decay, 1, 0)))
    prev = jnp.moveaxis(prev, 0, 1)
    y_off = jnp.einsum('bclhn,bchpn,bclh->bclhp', Ch, prev, jnp.exp(a_cs))
    y = (y_diag + y_off).reshape(bsz, t, h, p)
    return y.astype(dtype), final.astype(dtype)

def rope_1d(v, pos):
    half = v.shape[-1] // 2
    inv = ROPE_THETA ** (-jnp.arange(half, dtype=jnp.float32) / half)
    ang = pos.astype(jnp.float32)[:, None] * inv
    cos = jnp.cos(ang)[None, :, None, :]
    sin = jnp.sin(ang)[None, :, None, :]
    vf = v.astype(jnp.float32)
    v1, v2 = vf[..., :half], vf[..., half:]
    return jnp.concatenate([v1 * cos - v2 * sin, v1 * sin + v2 * cos], axis=-1).astype(v.dtype)

def axial_rope(v, row_pos, col_pos):
    hd2 = v.shape[-1] // 2
    return jnp.concatenate([rope_1d(v[..., :hd2], row_pos), rope_1d(v[..., hd2:], col_pos)], axis=-1)

def attend(q, k, v):
    bsz, tq = q.shape[:2]
    nq = tq // Q_BLOCK
    g = N_HEADS // N_KV_HEADS
    qb = q.reshape(bsz, nq, Q_BLOCK, N_KV_HEADS, g, HEAD_DIM).transpose(1, 0, 2, 3, 4, 5)
    scale = HEAD_DIM ** -0.5

    def blk(qi):
        s = jnp.einsum('bqkgd,bskd->bkgqs', qi, k).astype(jnp.float32) * scale
        p = jax.nn.softmax(s, axis=-1).astype(v.dtype)
        return jnp.einsum('bkgqs,bskd->bqkgd', p, v)

    o = lax.map(blk, qb)
    return o.transpose(1, 0, 2, 3, 4, 5).reshape(bsz, tq, N_HEADS * HEAD_DIM)

def peer(x, w_pq, sub_keys, u_tab, v_tab):
    bsz, t, d = x.shape
    xb = x.reshape(-1, TOK_BLOCK, d)

    def blk(xi):
        q = (xi @ w_pq).reshape(TOK_BLOCK, PEER_HEADS, 2, PEER_DQ // 2)
        s = jnp.einsum('thcd,hckd->thck', q, sub_keys).astype(jnp.float32)
        top_s, top_i = lax.top_k(s, PEER_TOPK)
        cand_s = (top_s[:, :, 0, :, None] + top_s[:, :, 1, None, :]).reshape(TOK_BLOCK, PEER_HEADS, -1)
        cand_i = (top_i[:, :, 0, :, None] * N_KEYS + top_i[:, :, 1, None, :]).reshape(TOK_BLOCK, PEER_HEADS, -1)
        best_s, pos = lax.top_k(cand_s, PEER_TOPK)
        idx = jnp.take_along_axis(cand_i, pos, axis=-1)
        gate = jax.nn.softmax(best_s, axis=-1).astype(xi.dtype)
        act = jax.nn.gelu(jnp.einsum('td,thkd->thk', xi, u_tab[idx]))
        return jnp.einsum('thk,thkd->td', gate * act, v_tab[idx])

    return lax.map(blk, xb).reshape(bsz, t, d)

def token_mixer(h, init_f, init_b, ctx_k, ctx_v, pos, lp):
    bsz, t, _ = h.shape
    proj = h @ lp['w_in']
    idx, acc = [], 0
    for s in IN_SIZES[:-1]:
        acc += s
        idx.append(acc)
    z, xbc, dt_f, dt_b, q, k, v, g_a, g_b = jnp.split(proj, idx, axis=-1)

    xbc = jax.nn.silu(depthwise_conv(xbc, lp['conv_w'], lp['conv_b']))
    xs, bm, cm = jnp.split(xbc, [SSD_D_INNER, SSD_D_INNER + SSD_GROUPS * D_STATE], axis=-1)
    xs = xs.reshape(bsz, t, SSD_HEADS, SSD_HEADDIM)
    bm = bm.reshape(bsz, t, SSD_GROUPS, D_STATE)
    cm = cm.reshape(bsz, t, SSD_GROUPS, D_STATE)
    dt_f = jax.nn.softplus(dt_f + lp['dt_bias_f'])
    dt_b = jax.nn.softplus(dt_b + lp['dt_bias_b'])
    if init_f is None:
        init_f = jnp.zeros((bsz, SSD_HEADS, SSD_HEADDIM, D_STATE), h.dtype)
        init_b = jnp.zeros((bsz, SSD_HEADS, SSD_HEADDIM, D_STATE), h.dtype)
    y_f, s_f = ssd_scan(xs, dt_f, lp['a_log_f'], bm, cm, init_f)
    fl = lambda a: jnp.flip(a, axis=1)
    y_b, s_b = ssd_scan(fl(xs), fl(dt_b), lp['a_log_b'], fl(bm), fl(cm), init_b)
    y = y_f + fl(y_b) + lp['d_skip'][:, None] * xs
    y = rmsnorm(y.reshape(bsz, t, SSD_D_INNER) * jax.nn.silu(z), lp['ssd_norm_w'])
    y_a = y @ lp['w_ssd_out']

    q = rmsnorm(q.reshape(bsz, t, N_HEADS, HEAD_DIM), lp['q_norm_w'])
    k = rmsnorm(k.reshape(bsz, t, N_KV_HEADS, HEAD_DIM), lp['k_norm_w'])
    v = v.reshape(bsz, t, N_KV_HEADS, HEAD_DIM)
    if ctx_k is None:
        keys, vals = k, v
    else:
        q = axial_rope(q, pos[0], pos[1])
        keys = jnp.concatenate([axial_rope(k, pos[0], pos[1]), ctx_k], axis=1)
        vals = jnp.concatenate([v, ctx_v], axis=1)
    y_b2 = attend(q, keys, vals) @ lp['w_attn_out']

    merged = jax.nn.sigmoid(g_a) * y_a + jax.nn.sigmoid(g_b) * y_b2
    return merged @ lp['w_o'], s_f, s_b, k, v

def layer(x, mod, init_f, init_b, ctx_k, ctx_v, pos, lp):
    shift1, scale1, gate1, shift2, scale2, gate2 = jnp.split(mod, 6, axis=-1)
    h = modulate(rmsnorm(x, lp['norm1_w']), shift1, scale1)
    mix, s_f, s_b, k, v = token_mixer(h, init_f, init_b, ctx_k, ctx_v, pos, lp)
    x = x + gate1 * mix
    h = modulate(rmsnorm(x, lp['norm2_w']), shift2, scale2)
    x = x + gate2 * peer(h, lp['w_pq'], lp['peer_keys'], lp['peer_u'], lp['peer_v'])
    return x, s_f, s_b, k, v

def setup_inputs(seed: int = 0) -> dict:
    key = jax.random.key(seed)
    ks = jax.random.split(key, 40)
    f32 = jnp.float32
    nrm = lambda i, shape, s: jax.random.normal(ks[i], shape, f32) * s
    dt0 = jnp.exp(jax.random.uniform(ks[30], (DEPTH, SSD_HEADS), f32, np.log(1e-3), np.log(1e-1)))
    dt1 = jnp.exp(jax.random.uniform(ks[31], (DEPTH, SSD_HEADS), f32, np.log(1e-3), np.log(1e-1)))
    inv_sp = lambda d: d + jnp.log(-jnp.expm1(-d))
    return {
        "x_prompt": nrm(0, (BATCH, SEQ, D_MODEL), 1.0),
        "x_sample": nrm(1, (DEC_BATCH, DEC_SEQ, D_MODEL), 1.0),
        "cache_k": nrm(2, (DEC_BATCH, DEPTH, PAST_LEN, N_KV_HEADS, HEAD_DIM), 1.0),
        "cache_v": nrm(3, (DEC_BATCH, DEPTH, PAST_LEN, N_KV_HEADS, HEAD_DIM), 1.0),
        "state_ssm_fwd": nrm(4, (DEC_BATCH, DEPTH, SSD_HEADS, SSD_HEADDIM, D_STATE), 0.5),
        "state_ssm_bwd": nrm(5, (DEC_BATCH, DEPTH, SSD_HEADS, SSD_HEADDIM, D_STATE), 0.5),
        "c": nrm(6, (DEC_BATCH, D_MODEL), 1.0),
        "c_ctx": nrm(7, (D_MODEL,), 1.0),
        "w_ada": nrm(8, (DEPTH, D_MODEL, 6 * D_MODEL), 0.5 * D_MODEL ** -0.5),
        "b_ada": nrm(9, (DEPTH, 6 * D_MODEL), 0.01),
        "norm1_w": 1.0 + nrm(10, (DEPTH, D_MODEL), 0.02),
        "norm2_w": 1.0 + nrm(11, (DEPTH, D_MODEL), 0.02),
        "w_in": nrm(12, (DEPTH, D_MODEL, IN_DIM), D_MODEL ** -0.5),
        "conv_w": nrm(13, (DEPTH, CONV_W, XBC_DIM), CONV_W ** -0.5),
        "conv_b": nrm(14, (DEPTH, XBC_DIM), 0.01),
        "a_log_f": jnp.log(jax.random.uniform(ks[15], (DEPTH, SSD_HEADS), f32, 1.0, 16.0)),
        "a_log_b": jnp.log(jax.random.uniform(ks[16], (DEPTH, SSD_HEADS), f32, 1.0, 16.0)),
        "dt_bias_f": inv_sp(dt0),
        "dt_bias_b": inv_sp(dt1),
        "d_skip": 1.0 + nrm(17, (DEPTH, SSD_HEADS), 0.1),
        "ssd_norm_w": 1.0 + nrm(18, (DEPTH, SSD_D_INNER), 0.02),
        "w_ssd_out": nrm(19, (DEPTH, SSD_D_INNER, D_MODEL), SSD_D_INNER ** -0.5),
        "q_norm_w": 1.0 + nrm(20, (DEPTH, HEAD_DIM), 0.02),
        "k_norm_w": 1.0 + nrm(21, (DEPTH, HEAD_DIM), 0.02),
        "w_attn_out": nrm(22, (DEPTH, N_HEADS * HEAD_DIM, D_MODEL), (N_HEADS * HEAD_DIM) ** -0.5),
        "w_o": nrm(23, (DEPTH, D_MODEL, D_MODEL), D_MODEL ** -0.5),
        "w_pq": nrm(24, (DEPTH, D_MODEL, PEER_HEADS * PEER_DQ), D_MODEL ** -0.5),
        "peer_keys": nrm(25, (DEPTH, PEER_HEADS, 2, N_KEYS, PEER_DQ // 2), (PEER_DQ // 2) ** -0.5),
        "peer_u": nrm(26, (DEPTH, N_EXPERTS, D_MODEL), D_MODEL ** -0.5),
        "peer_v": nrm(27, (DEPTH, N_EXPERTS, D_MODEL), 0.5),
        "final_norm_w": 1.0 + nrm(28, (D_MODEL,), 0.02),
    }

def reference(x_prompt, x_sample, cache_k, cache_v, state_ssm_fwd, state_ssm_bwd, c, c_ctx,
              w_ada, b_ada, norm1_w, norm2_w, w_in, conv_w, conv_b, a_log_f, a_log_b,
              dt_bias_f, dt_bias_b, d_skip, ssd_norm_w, w_ssd_out, q_norm_w, k_norm_w,
              w_attn_out, w_o, w_pq, peer_keys, peer_u, peer_v, final_norm_w):
    n_lat = x_sample.shape[1]
    rows = n_lat // GRID_W
    row_pos = jnp.repeat(jnp.arange(rows), GRID_W)
    col_pos = jnp.tile(jnp.arange(GRID_W), rows)
    pos = (row_pos, col_pos)

    xp, xs = x_prompt, x_sample
    new_k, new_v, new_sf, new_sb = [], [], [], []
    for l in range(DEPTH):
        lp = {
            'norm1_w': norm1_w[l], 'norm2_w': norm2_w[l], 'w_in': w_in[l],
            'conv_w': conv_w[l], 'conv_b': conv_b[l], 'a_log_f': a_log_f[l], 'a_log_b': a_log_b[l],
            'dt_bias_f': dt_bias_f[l], 'dt_bias_b': dt_bias_b[l], 'd_skip': d_skip[l],
            'ssd_norm_w': ssd_norm_w[l], 'w_ssd_out': w_ssd_out[l], 'q_norm_w': q_norm_w[l],
            'k_norm_w': k_norm_w[l], 'w_attn_out': w_attn_out[l], 'w_o': w_o[l],
            'w_pq': w_pq[l], 'peer_keys': peer_keys[l], 'peer_u': peer_u[l], 'peer_v': peer_v[l],
        }
        mod_ctx = jax.nn.silu(c_ctx) @ w_ada[l] + b_ada[l]
        mod_lat = (jax.nn.silu(c) @ w_ada[l] + b_ada[l])[:, None, :]
        xp, sf, sb, kc, vc = layer(xp, mod_ctx, None, None, None, None, None, lp)
        new_k.append(kc); new_v.append(vc); new_sf.append(sf); new_sb.append(sb)
        xs, _, _, _, _ = layer(xs, mod_lat, state_ssm_fwd[:, l], state_ssm_bwd[:, l],
                               cache_k[:, l], cache_v[:, l], pos, lp)
    y_prompt = rmsnorm(xp, final_norm_w)
    y_sample = rmsnorm(xs, final_norm_w)
    new_cache_k = jnp.stack(new_k, axis=1)
    new_cache_v = jnp.stack(new_v, axis=1)
    new_state_fwd = jnp.stack(new_sf, axis=1)
    new_state_bwd = jnp.stack(new_sb, axis=1)
    return (y_prompt, y_sample, new_cache_k, new_cache_v, new_state_fwd, new_state_bwd)


_drawn_inputs = setup_inputs


def setup_inputs(seed=0):
    import zlib

    import numpy as np

    out = dict(_drawn_inputs(seed))
    spreads = {}
    factors = {'cache_k': 8.0,
     'cache_v': 7.157,
     'norm2_w': 4.781,
     'conv_b': 3.44,
     'd_skip': 7.59,
     'ssd_norm_w': 8.0,
     'q_norm_w': 8.0,
     'k_norm_w': 12.875,
     'final_norm_w': 7.391}
    for name, (base, spread) in spreads.items():
        noise = np.random.default_rng([zlib.crc32(name.encode()), seed]).standard_normal(out[name].shape)
        drawn = base * np.exp(spread * noise) if base else spread * noise
        out[name] = __import__('jax').numpy.asarray(drawn.astype(out[name].dtype))
    for name, factor in factors.items():
        out[name] = (out[name] * factor).astype(out[name].dtype)
    return out
```

```python
from contextlib import ExitStack

import concourse.bass as bass
from concourse import mybir

F32 = mybir.dt.float32
F32R = mybir.dt.float32r
U32 = mybir.dt.uint32
ALU = mybir.AluOpType
ACT = mybir.ActivationFunctionType
AX = mybir.AxisListType

P = 128
D = 1024
KD = D // P
T = 640
NT = T // P
TH = T // 2
EPS = 1e-6
UC = 256
HEADS, HP, NS, GROUPS = 32, 64, 128, 8
HPG = HEADS // GROUPS
DI = HEADS * HP
NH, NKV, HD = 16, 4, 64
PAST = 128
PH, TOPK, NKEYS = 8, 16, 128
SLOTS = PH * TOPK

N_TOK = 14
N_MERGE = 12
N_SSD = 16
N_SO = 8
N_O = 4
N_PQ = 8
N_EXP = 128
U_TOK = 0
U_MERGE = U_TOK + N_TOK
U_SSD = U_MERGE + N_MERGE
U_SO = U_SSD + N_SSD
U_O = U_SO + N_SO
U_PQ = U_O + N_O
U_EXP = U_PQ + N_PQ
N_UNITS = U_EXP + N_EXP


class Shared:
    pass


def group(t):
    return 0 if t == 0 else 1



class Stream:

    def __init__(self, nc, K):
        self.nc, self.K = nc, K

    def load(self, sp, n, slot):
        K = self.K
        if not (isinstance(n, int) and n < 2):
            sp.wait_ge(K.w_lo_done, n - 1)
        src = K.w_stream[bass.ds(n, 1), :, :].rearrange("o p c -> p (o c)")
        sp.dma_start(K.raw[slot][:, :], src).then_inc(K.w_loaded[slot], 16)

    def hi(self, act, n, slot):
        K = self.K
        act.wait_ge(K.w_loaded[slot], (n - slot + 2) * 8)
        act.wait_ge(K.hilo_free, n + 1)
        self.nc.scalar.activation(K.whi[slot][:, :], K.raw[slot][:, :], ACT.Copy).then_inc(K.w_hi_done, 1)

    def lo(self, dve, n, slot):
        K = self.K
        dve.wait_ge(K.w_hi_done, n + 1)
        self.nc.vector.tensor_tensor(K.wlo[slot][:, :], K.raw[slot][:, :], K.whi[slot][:, :].bitcast(F32),
                                     ALU.subtract).then_inc(K.w_lo_done, 1)

    def ready(self, pe, n):
        pe.wait_ge(self.K.w_lo_done, n + 1)


def mm3(nc, out, lhs, rhs, first, last):
    (lh, ll), (rh, rl) = lhs, rhs
    nc.tensor.matmul(out, lh, rh, start=first, stop=False)
    nc.tensor.matmul(out, lh, rl, start=False, stop=False)
    return nc.tensor.matmul(out, ll, rh, start=False, stop=last)



def phase_modulate(nc, K, ctx):
    S = Stream(nc, K)
    sem = K.phase_semaphores(ctx)
    sb = lambda n, s, d=F32: ctx.enter_context(nc.sbuf_tensor(n, s, d))
    ada = [K.raw[0], K.raw[1]]
    cT = sb("cT", [P, KD, 2])
    silu_c = sb("silu_c", [P, KD, 2])
    xt = sb("xt", [P, NT, D])
    xn = sb("xn", [P, 2, D])
    hf = sb("hf", [P, 2, KD, P])
    sq = sb("sq", [P, D])
    ssq = sb("ssq", [P, NT])
    rstd = sb("rstd", [P, NT])
    b_col = sb("b_col", [P, 48])
    b_row = sb("b_row", [2, 2 * D])
    n1 = sb("n1", [P, KD])
    n2 = sb("n2", [P, KD])
    g_row = sb("g_row", [2, 2 * D])
    modc = sb("modc", [P, 48, 2])
    ps_mod = ctx.enter_context(nc.psum_tensor("ps_mod", [P, 48, 2], F32))
    ps_gate = ctx.enter_context(nc.psum_tensor("ps_gate", [2, 2 * D], F32))
    ps_x = [ctx.enter_context(nc.psum_tensor(f"ps_x{i}", [P, 4, P], F32)) for i in range(2)]

    small = sem("m_small"); c_in = sem("m_c_in"); x_in = sem("m_x_in")
    ada_in = [sem("m_ada_in0"), sem("m_ada_in1")]; ada_used = sem("m_ada_used")
    silu_done = sem("m_silu"); ident_done = sem("m_ident"); iota_done = sem("m_iota"); zeroed = sem("m_zeroed")
    sq_done = sem("m_sq"); ms_done = sem("m_ms"); rt_done = sem("m_rt"); rstd_done = sem("m_rstd")
    xn_done = sem("m_xn"); xT_done = sem("m_xT"); hf_done = sem("m_hf"); hhi_done = sem("m_hhi"); hlo_done = sem("m_hlo")
    mod_done = sem("m_mod"); gate_done = sem("m_gate"); modc_done = sem("m_modc"); scale_done = sem("m_scale")
    grow_done = sem("m_grow"); g_out = sem("m_g_out")
    ADA = [(0, 8, False), (8, 4, True), (12, 8, False), (20, 4, True)]

    with nc.Block() as block:
        def split(dve, t):
            dve.wait_ge(hf_done, KD * (t + 1))
            nc.vector.tensor_copy(K.hT[0][:, :, t * P:(t + 1) * P], hf[:, t % 2, :, :]).then_inc(hhi_done, 1)
            dve.wait_ge(hhi_done, t + 1)
            nc.vector.tensor_tensor(K.hT[1][:, :, t * P:(t + 1) * P], hf[:, t % 2, :, :],
                                    K.hT[0][:, :, t * P:(t + 1) * P].bitcast(F32), ALU.subtract).then_inc(hlo_done, 1)

        @block.sync
        def _(sp):
            sp.dma_start(cT[:, :, :], K.c_cols).then_inc(c_in, 16)
            for u in range(2):
                sp.dma_start(ada[u][:, :], K.w_ada[u]).then_inc(ada_in[u], 16)
            sp.dma_start(xt[:, :, :], K.x.rearrange("(t p) d -> p t d", p=P)).then_inc(x_in, 16)
            with sp.Fori(1, 12) as i:
                for s in range(2):
                    sp.wait_ge(ada_used, 2 * i + s - 1)
                    sp.dma_start(ada[s][:, :], K.w_ada[bass.ds(2 * i + s, 1), :, :].rearrange("o p c -> p (o c)")).then_inc(ada_in[s], 16)
            sp.wait_ge(ada_used, 24)
            S.load(sp, 0, 0)
            S.load(sp, 1, 1)
            S.load(sp, 2, 0)
            sp.wait_ge(grow_done, 1)
            sp.dma_start(K.gates, g_row[:, :]).then_inc(g_out, 16)
            sp.wait_ge(g_out, 16)

        @block.gpsimd
        def _(pool):
            nc.gpsimd.memset(K.ident[:, :], 0.0).then_inc(zeroed, 1)
            nc.gpsimd.memset(K.ones[:, :], 1.0).then_inc(zeroed, 1)
            pool.wait_ge(zeroed, 2)
            nc.gpsimd.affine_select(out=K.ident[:, :], in_=K.ident[:, :], compare_op=ALU.not_equal, fill=1.0, base=0,
                                    pattern=[[-1, P]], channel_multiplier=1).then_inc(ident_done, 1)
            nc.gpsimd.affine_select(out=K.tri_le[:, :], in_=K.ones[:, :], compare_op=ALU.is_ge, fill=0.0, base=0,
                                    pattern=[[1, P]], channel_multiplier=-1).then_inc(iota_done, 1)
            nc.gpsimd.affine_select(out=K.tri_gt[:, :], in_=K.ones[:, :], compare_op=ALU.is_gt, fill=0.0, base=0,
                                    pattern=[[-1, P]], channel_multiplier=1).then_inc(iota_done, 1)
            nc.gpsimd.affine_select(out=K.tri_ge[:, :], in_=K.ones[:, :], compare_op=ALU.is_ge, fill=0.0, base=0,
                                    pattern=[[-1, P]], channel_multiplier=1).then_inc(iota_done, 1)
            nc.gpsimd.affine_select(out=K.tri_lt[:, :], in_=K.ones[:, :], compare_op=ALU.is_gt, fill=0.0, base=0,
                                    pattern=[[1, P]], channel_multiplier=-1).then_inc(iota_done, 1)
            nc.gpsimd.iota(K.iota[:, :], pattern=[[1, P]], base=0, channel_multiplier=0,
                           allow_small_or_imprecise_dtypes=True).then_inc(iota_done, 1)

        @block.scalar
        def _(act):
            act.dma_start(b_col[:, :], K.b_ada_cols).then_inc(small, 16)
            act.dma_start(n1[:, :], K.norm1_cols).then_inc(small, 16)
            act.dma_start(n2[:, :], K.norm2_cols).then_inc(small, 16)
            act.dma_start(b_row[:, 0:D], K.b_ada[:, 2 * D:3 * D].partition_broadcast(2).rearrange("a o d -> a (o d)")).then_inc(small, 16)
            act.dma_start(b_row[:, D:2 * D], K.b_ada[:, 5 * D:6 * D].partition_broadcast(2).rearrange("a o d -> a (o d)")).then_inc(small, 16)
            act.wait_ge(c_in, 16)
            nc.scalar.activation(silu_c[:, :, :], cT[:, :, :], ACT.Silu).then_inc(silu_done, 1)
            act.wait_ge(x_in, 16)
            for t in range(NT):
                if t:
                    act.wait_ge(sq_done, t)
                nc.scalar.activation(sq[:, :], xt[:, t, :], ACT.Square, accum_out=ssq[:, t:t + 1]).then_inc(sq_done, 1)
            act.wait_ge(ms_done, 1)
            nc.scalar.activation(rstd[:, :], ssq[:, :], ACT.Sqrt).then_inc(rt_done, 1)
            act.wait_ge(scale_done, 4)
            for t in range(NT):
                for h in range(2):
                    act.wait_ge(xT_done, 2 * t + h + 1)
                    if t >= 2 and h == 0:
                        act.wait_ge(hlo_done, t - 1)
                    for k in range(4):
                        kd = 4 * h + k
                        nc.scalar.activation(hf[:, t % 2, kd, :], ps_x[h][:, k, :], ACT.Identity,
                                             scale=K.mul1[:, kd, group(t):group(t) + 1],
                                             bias=K.add1[:, kd, group(t):group(t) + 1]).then_inc(hf_done, 1)
            S.hi(act, 0, 0)

        @block.vector
        def _(dve):
            dve.wait_ge(sq_done, NT)
            nc.vector.tensor_scalar(ssq[:, :], ssq[:, :], 1.0 / D, EPS, ALU.mult, ALU.add).then_inc(ms_done, 1)
            dve.wait_ge(rt_done, 1)
            nc.vector.reciprocal(rstd[:, :], rstd[:, :]).then_inc(rstd_done, 1)
            dve.wait_ge(rstd_done, 1)
            for t in range(NT):
                if t >= 2:
                    dve.wait_ge(xT_done, 2 * t - 2)
                nc.vector.tensor_scalar(xn[:, t % 2, :], xt[:, t, :], rstd[:, t:t + 1], None, ALU.mult).then_inc(xn_done, 1)
                if t == 1:
                    dve.wait_ge(small, 80)
                    dve.wait_ge(mod_done, 1)
                    nc.vector.tensor_tensor(modc[:, 0:16, :], ps_mod[:, 0:16, :],
                                            b_col[:, 0:16].unsqueeze(2).to_broadcast([P, 16, 2]), ALU.add).then_inc(modc_done, 1)
                    dve.wait_ge(modc_done, 1)
                    nc.vector.tensor_copy(K.add1[:, :, :], modc[:, 0:8, :]).then_inc(scale_done, 1)
                    nc.vector.tensor_scalar(K.mul1[:, :, :], modc[:, 8:16, :], 1.0, None, ALU.add).then_inc(scale_done, 1)
                    dve.wait_ge(scale_done, 2)
                    for g in range(2):
                        nc.vector.tensor_tensor(K.mul1[:, :, g], K.mul1[:, :, g], n1[:, :], ALU.mult).then_inc(scale_done, 1)
                if t >= 1:
                    split(dve, t - 1)
            split(dve, NT - 1)
            dve.wait_ge(mod_done, 2)
            nc.vector.tensor_tensor(modc[:, 24:40, :], ps_mod[:, 24:40, :],
                                    b_col[:, 24:40].unsqueeze(2).to_broadcast([P, 16, 2]), ALU.add).then_inc(modc_done, 1)
            dve.wait_ge(modc_done, 2)
            nc.vector.tensor_copy(K.add2[:, :, :], modc[:, 24:32, :]).then_inc(scale_done, 1)
            nc.vector.tensor_scalar(K.mul2[:, :, :], modc[:, 32:40, :], 1.0, None, ALU.add).then_inc(scale_done, 1)
            dve.wait_ge(scale_done, 6)
            for g in range(2):
                nc.vector.tensor_tensor(K.mul2[:, :, g], K.mul2[:, :, g], n2[:, :], ALU.mult).then_inc(scale_done, 1)
            dve.wait_ge(gate_done, 2)
            nc.vector.tensor_tensor(g_row[:, :], ps_gate[:, :], b_row[:, :], ALU.add).then_inc(grow_done, 1)
            S.lo(dve, 0, 0)

        @block.tensor
        def _(pe):
            pe.sem_inc(K.hilo_free, 2)
            pe.wait_ge(silu_done, 1)
            for n, (u0, cnt, row) in enumerate(ADA):
                with pe.Fori(0, cnt // 2) as i:
                    for s in range(2):
                        pe.wait_ge(ada_in[s], (i + (u0 // 2 + 1)) * 16)
                        w = ada[s][:, :].rearrange("p (k c) -> p k c", k=KD)
                        if row:
                            for k in range(KD):
                                mm = nc.tensor.matmul(ps_gate[:, bass.ds(i * 512 + ((0 if u0 < 12 else D) + s * UC), UC)],
                                                      silu_c[:, k, :], w[:, k, :], start=(k == 0), stop=(k == KD - 1))
                            mm.then_inc(ada_used, 1)
                        else:
                            for m in range(2):
                                for k in range(KD):
                                    mm = nc.tensor.matmul(ps_mod[:, bass.ds(i * 4 + (2 * (u0 + s) + m), 1), :].rearrange("p o c -> p (o c)"),
                                                          w[:, k, m * P:(m + 1) * P], silu_c[:, k, :],
                                                          start=(k == 0), stop=(k == KD - 1))
                            mm.then_inc(ada_used, 1)
                pe.drain().then_inc(gate_done if row else mod_done, 1)
                if n == 0:
                    pe.wait_ge(ident_done, 1)
                    for t in range(NT):
                        pe.wait_ge(xn_done, t + 1)
                        for h in range(2):
                            if t:
                                pe.wait_ge(hf_done, KD * (t - 1) + 4 * (h + 1))
                            for k in range(4):
                                kd = 4 * h + k
                                mm = nc.tensor.transpose(ps_x[h][:, k, :], xn[:, t % 2, kd * P:(kd + 1) * P], K.ident[:, :])
                            mm.then_inc(xT_done, 1)


def project_features(nc, pe, w, act, out):
    wh, wl = (x[:, :].rearrange("p (k c) -> p k c", k=KD) for x in w)
    ah, al = act
    for m in range(2):
        for k in range(KD):
            cols = slice(m * P, (m + 1) * P)
            for lhs, rhs, first, last in ((wh, ah, k == 0, False), (wh, al, False, False), (wl, ah, False, k == KD - 1)):
                for h in range(2):
                    mm = nc.tensor.matmul(out[2 * m + h], lhs[:, k, cols], rhs[:, k, h * TH:(h + 1) * TH],
                                          start=first, stop=last)
    return mm



def phase_tokens(nc, K, ctx):
    S = Stream(nc, K)
    sem = K.phase_semaphores(ctx)
    sb = lambda n, s, d=F32: ctx.enter_context(nc.sbuf_tensor(n, s, d))
    ob = [sb(f"t_ob{t}", [P, 2 * UC]) for t in range(NT)]
    ps = [ctx.enter_context(nc.psum_tensor(f"t_ps{t}", [P, 2 * UC], F32)) for t in range(NT)]
    ps_dt = ctx.enter_context(nc.psum_tensor("t_psdt", [P, NT, 64], F32))
    ps_cum = [ctx.enter_context(nc.psum_tensor(f"t_cum{i}", [P, 3, NT * HEADS], F32)) for i in range(2)]
    dtw = sb("dtw", [P, KD * 64])
    dtwh, dtwl = sb("dtwh", [P, KD, 64], F32R), sb("dtwl", [P, KD, 64], F32R)
    bias = sb("dt_bias", [P, 64])
    xdt = sb("xdt", [P, NT, 64]); ax = sb("ax", [P, NT, 64]); ex = sb("ex", [P, NT, 64])
    sr = sb("sr", [P, NT, 64]); s2 = sb("s2", [P, NT, 64]); pl = sb("pl", [P, NT, 64])
    nega = sb("nega", [P, 64])

    dtw_in = sem("t_dtw_in"); par_in = sem("t_par_in"); dtw_hi = sem("t_dtw_hi"); dtw_lo = sem("t_dtw_lo")
    mm_done = sem("t_mm"); ev_done = sem("t_ev"); out_done = [sem(f"t_out{t}") for t in range(NT)]
    dt_mm = sem("t_dt_mm"); chain = sem("t_chain"); ex_done = sem("t_ex"); ax_done = sem("t_ax")
    na_done = sem("t_na"); dtA_done = sem("t_dtA"); cum_mm = sem("t_cum_mm"); cum_exp = sem("t_cum_exp")

    with nc.Block() as block:
        def one_pair(act, i, func):
            for t in range(NT):
                tile_out(act, i, t, func)
                if t == 0:
                    S.hi(act, 2 * i + 2, 0)
                if t == 2:
                    S.hi(act, 2 * i + 3, 1)

        def tile_out(act, i, t, func):
            act.wait_ge(mm_done, NT * i + (t + 1))
            if not isinstance(i, int):
                act.wait_ge(out_done[t], i * 16)
            nc.scalar.activation(ob[t][:, :], ps[t][:, :], func).then_inc(ev_done, 1)

        @block.sync
        def _(sp):
            sp.dma_start(dtw[:, :], K.w_dt).then_inc(dtw_in, 16)
            sp.dma_start(bias[:, 0:32], K.dt_bias_f.partition_broadcast(P).rearrange("p o h -> p (o h)")).then_inc(par_in, 16)
            sp.dma_start(bias[:, 32:64], K.dt_bias_b.partition_broadcast(P).rearrange("p o h -> p (o h)")).then_inc(par_in, 16)
            sp.dma_start(nega[:, 0:32], K.a_log_f.partition_broadcast(P).rearrange("p o h -> p (o h)")).then_inc(par_in, 16)
            sp.dma_start(nega[:, 32:64], K.a_log_b.partition_broadcast(P).rearrange("p o h -> p (o h)")).then_inc(par_in, 16)
            with sp.Fori(0, N_TOK // 2) as i:
                for s in range(2):
                    S.load(sp, 2 * i + (U_TOK + s + 3), (s + 1) % 2)

        @block.gpsimd
        def _(pool):
            with pool.Fori(0, 4) as i:
                for t in range(NT):
                    pool.wait_ge(ev_done, i * NT + (t + 1))
                    pool.dma_start(K.z_dram[t * P:(t + 1) * P, bass.ds(i * 512, 512)], ob[t][:, :]).then_inc(out_done[t], 16)
            with pool.Fori(0, 3) as i:
                for t in range(NT):
                    pool.wait_ge(ev_done, i * NT + (4 * NT + t + 1))
                    pool.dma_start(K.qkv_dram[t * P:(t + 1) * P, bass.ds(i * 512, 512)], ob[t][:, :]).then_inc(out_done[t], 16)
            for t in range(NT):
                pool.wait_ge(out_done[t], 7 * 16)

        @block.scalar
        def _(act):
            act.wait_ge(dtw_in, 16)
            nc.scalar.activation(dtwh[:, :, :], dtw[:, :].rearrange("p (k c) -> p k c", k=KD), ACT.Copy).then_inc(dtw_hi, 1)
            S.hi(act, 1, 1)
            act.wait_ge(par_in, 64)
            nc.scalar.activation(nega[:, :], nega[:, :], ACT.Exp).then_inc(na_done, 1)
            act.wait_ge(ax_done, 1)
            nc.scalar.activation(ex[:, :, :], ax[:, :, :], ACT.Exp, scale=-1.0).then_inc(ex_done, 1)
            for t in range(NT):
                tile_out(act, 0, t, ACT.Silu)
                if t == 0:
                    S.hi(act, 2, 0)
                if t == 2:
                    S.hi(act, 3, 1)
            act.wait_ge(cum_mm, 2)
            for j in range(2):
                nc.scalar.activation(K.decay[:, 3 * j:3 * j + 3, :], ps_cum[j][:, :, :], ACT.Exp).then_inc(cum_exp, 1)
            with act.Fori(1, 4) as i:
                one_pair(act, i, ACT.Silu)
            with act.Fori(4, 7) as i:
                one_pair(act, i, ACT.Copy)

        @block.vector
        def _(dve):
            dve.wait_ge(dtw_hi, 1)
            nc.vector.tensor_tensor(dtwl[:, :, :], dtw[:, :].rearrange("p (k c) -> p k c", k=KD),
                                    dtwh[:, :, :].bitcast(F32), ALU.subtract).then_inc(dtw_lo, 1)
            S.lo(dve, 1, 1)
            dve.wait_ge(par_in, 64)
            dve.wait_ge(dt_mm, 1)
            k = [0]

            def link(ins):
                k[0] += 1
                ins.then_inc(chain, 1)
                dve.wait_ge(chain, k[0])

            b3 = bias[:, :].unsqueeze(1).to_broadcast([P, NT, 64])
            link(nc.vector.tensor_tensor(xdt[:, :, :], ps_dt[:, :, :], b3, ALU.add))
            nc.vector.scalar_tensor_tensor(ax[:, :, :], xdt[:, :, :], -1.0, xdt[:, :, :], ALU.mult, ALU.max).then_inc(ax_done, 1)
            dve.wait_ge(ex_done, 1)
            link(nc.vector.tensor_scalar(s2[:, :, :], ex[:, :, :], 2.0, None, ALU.add))
            link(nc.vector.reciprocal(pl[:, :, :], s2[:, :, :]))
            link(nc.vector.tensor_tensor(sr[:, :, :], ex[:, :, :], pl[:, :, :], ALU.mult))
            link(nc.vector.tensor_tensor(s2[:, :, :], sr[:, :, :], sr[:, :, :], ALU.mult))
            link(nc.vector.tensor_scalar(pl[:, :, :], s2[:, :, :], 2.0 / 17, None, ALU.mult))
            for c in (15, 13, 11, 9, 7, 5, 3):
                link(nc.vector.scalar_tensor_tensor(pl[:, :, :], pl[:, :, :], 2.0 / c, s2[:, :, :], ALU.add, ALU.mult))
            link(nc.vector.scalar_tensor_tensor(pl[:, :, :], pl[:, :, :], 2.0, sr[:, :, :], ALU.add, ALU.mult))
            link(nc.vector.scalar_tensor_tensor(K.dt[:, :, :], xdt[:, :, :], 0.0, pl[:, :, :], ALU.max, ALU.add))
            dve.wait_ge(na_done, 1)
            link(nc.vector.tensor_scalar(nega[:, :], nega[:, :], -1.0, None, ALU.mult))
            nc.vector.tensor_tensor(K.dtA[:, :, :], K.dt[:, :, :], nega[:, :].unsqueeze(1).to_broadcast([P, NT, 64]),
                                    ALU.mult).then_inc(dtA_done, 1)
            S.lo(dve, 2, 0)
            S.lo(dve, 3, 1)
            dve.wait_ge(cum_exp, 2)
            for row, d in ((1, 0), (4, 1)):
                v = K.decay[:, row, :].rearrange("p (c h) -> p c h", c=NT)
                link(nc.vector.tensor_tensor(v, v, K.dt[:, :, d * 32:(d + 1) * 32], ALU.mult))
            with dve.Fori(1, 7) as i:
                S.lo(dve, 2 * i + 2, 0)
                S.lo(dve, 2 * i + 3, 1)

        @block.tensor
        def _(pe):
            def unit(n, i, s):
                S.ready(pe, n)
                wh, wl = (x[s][:, :].rearrange("p (k c) -> p k c", k=KD) for x in (K.whi, K.wlo))
                for t in range(NT):
                    if s == 0 and not isinstance(i, int):
                        pe.wait_ge(ev_done, NT * i + (t - NT + 1))
                    tc = slice(t * P, (t + 1) * P)
                    for k in range(KD):
                        mm = mm3(nc, ps[t][:, s * UC:(s + 1) * UC], (K.hT[0][:, k, tc], K.hT[1][:, k, tc]),
                                 (wh[:, k, :], wl[:, k, :]), k == 0, k == KD - 1)
                    if s == 1:
                        mm.then_inc(mm_done, 1)
                pe.drain().then_inc(K.hilo_free, 1)

            pe.wait_ge(dtw_lo, 1)
            for t in range(NT):
                tc = slice(t * P, (t + 1) * P)
                for k in range(KD):
                    mm = mm3(nc, ps_dt[:, t, :], (K.hT[0][:, k, tc], K.hT[1][:, k, tc]),
                             (dtwh[:, k, :], dtwl[:, k, :]), k == 0, k == KD - 1)
            mm.then_inc(dt_mm, 1)
            unit(0, 0, 0)
            unit(1, 0, 1)
            pe.wait_ge(dtA_done, 1)
            for j, tris in enumerate(((K.tri_le, K.tri_gt, K.ones), (K.tri_ge, K.tri_lt, K.ones))):
                for r, tri in enumerate(tris):
                    mm = nc.tensor.matmul(ps_cum[j][:, r, :], tri[:, :], K.dtA[:, :, j * 32:(j + 1) * 32],
                                          start=True, stop=True)
                mm.then_inc(cum_mm, 1)
            with pe.Fori(1, 7) as i:
                unit(2 * i, i, 0)
                unit(2 * i + 1, i, 1)



def phase_qk(nc, K, ctx):
    sem = K.phase_semaphores(ctx)
    sb = lambda n, s, d=F32: ctx.enter_context(nc.sbuf_tensor(n, s, d))
    NQ, NK = NH * HD, NKV * HD
    NHK = NH + NKV
    st = [sb(f"q_st{i}", [P, NQ + NK]) for i in range(2)]
    sq = sb("q_sq", [P, NQ + NK])
    qn = sb("q_n", [P, NQ + NK])
    qr = [sb(f"q_r{i}", [P, NQ]) for i in range(2)]
    kd = [sb(f"k_d{i}", [P, NKV, 2, HD]) for i in range(2)]
    ck = sb("q_ck", [P, NK])
    ss = sb("q_ss", [P, NHK]); wq = sb("q_w", [P, HD]); wk = sb("k_w", [P, HD])
    cs = sb("q_cs", [P, 2, 4, 32])
    t1 = sb("q_t1", [P, NHK, 2, 16]); t2 = sb("q_t2", [P, NHK, 2, 16])
    ps = [ctx.enter_context(nc.psum_tensor(f"q_ps{i}", [P, 12, P], F32)) for i in range(2)]
    st_in = [sem(f"q_st_in{i}") for i in range(2)]
    par_in = sem("q_par_in"); ck_in = sem("q_ck_in"); v_in = sem("q_v_in")
    chain = sem("q_chain"); ms_done = sem("q_ms"); rt_done = sem("q_rt"); st_read = sem("q_st_read")
    k0_done = sem("q_k0"); src_done = sem("q_src"); tr_done = sem("q_tr"); ev_done = sem("q_ev"); outs = sem("q_outs")
    bc = lambda ap: ap.partition_broadcast(P).rearrange("p o h -> p (o h)")

    with nc.Block() as block:
        @block.sync
        def _(sp):
            for t in range(NT):
                if t >= 2:
                    sp.wait_ge(st_read, t - 1)
                sp.dma_start(st[t % 2][:, :], K.qkv_dram[t * P:(t + 1) * P, 0:NQ + NK]).then_inc(st_in[t % 2], 16)
                if t == 0:
                    sp.dma_start(wq[:, :], bc(K.q_norm_w)).then_inc(par_in, 16)
                    sp.dma_start(wk[:, :], bc(K.k_norm_w)).then_inc(par_in, 16)
                    sp.dma_start(cs[:, :, :, :], K.rope).then_inc(par_in, 16)
                    sp.dma_start(ck[:, :], K.cache_k).then_inc(ck_in, 16)
            sp.wait_ge(outs, 32)
            sp.wait_ge(v_in, 32)

        @block.gpsimd
        def _(pool):
            pool.dma_start(K.vals[:, 0:NT, :], K.qkv_dram[:, NQ + NK:].rearrange("(t p) c -> p t c", p=P)).then_inc(v_in, 16)
            pool.dma_start(K.vals[:, NT, :], K.cache_v).then_inc(v_in, 16)
            pool.dma_start(K.out_new_v, K.qkv_dram[0:P, NQ + NK:]).then_inc(outs, 16)
            pool.wait_ge(k0_done, 1)
            pool.dma_start(K.out_new_k, qn[:, NQ:]).then_inc(outs, 16)

        @block.vector
        def _(dve):
            k = [0]

            def link(ins):
                k[0] += 1
                ins.then_inc(chain, 1)
                dve.wait_ge(chain, k[0])

            heads = lambda ap: ap.rearrange("p (h d) -> p h d", d=HD)
            row = lambda w, n: w[:, :].unsqueeze(1).to_broadcast([P, n, HD])
            for t in range(NT):
                s = t % 2
                x = st[s]
                dve.wait_ge(st_in[s], (t // 2 + 1) * 16)
                link(nc.vector.tensor_tensor(sq[:, :], x[:, :], x[:, :], ALU.mult))
                link(nc.vector.tensor_reduce(ss[:, :], heads(sq[:, :]), axis=AX.X, op=ALU.add))
                nc.vector.tensor_scalar(ss[:, :], ss[:, :], 1.0 / HD, EPS, ALU.mult, ALU.add).then_inc(ms_done, 1)
                dve.wait_ge(rt_done, t + 1)
                link(nc.vector.reciprocal(ss[:, :], ss[:, :]))
                if t == 1:
                    dve.wait_ge(outs, 32)
                nc.vector.tensor_tensor(heads(qn[:, :]), heads(x[:, :]), ss[:, :].unsqueeze(2).to_broadcast([P, NHK, HD]),
                                        ALU.mult).then_inc(st_read, 1)
                dve.wait_ge(st_read, t + 1)
                if t == 0:
                    dve.wait_ge(par_in, 48)
                link(nc.vector.tensor_tensor(heads(qn[:, 0:NQ]), heads(qn[:, 0:NQ]), row(wq, NH), ALU.mult))
                ins = nc.vector.tensor_tensor(heads(qn[:, NQ:]), heads(qn[:, NQ:]), row(wk, NKV), ALU.mult)
                if t == 0:
                    ins.then_inc(k0_done, 1)
                    dve.wait_ge(k0_done, 1)
                    link(nc.vector.tensor_copy(qr[0][:, :], qn[:, 0:NQ]))
                    for c in range(2):
                        nc.vector.tensor_copy(kd[0][:, :, c, :], heads(qn[:, NQ:])).then_inc(src_done, 1)
                else:
                    link(ins)
                    if t >= 2:
                        dve.wait_ge(tr_done, t - 1)
                    axes = qn[:, :].rearrange("p (h a f d) -> p h a f d", h=NHK, a=2, f=2)
                    a, b = axes[:, :, :, 0, :], axes[:, :, :, 1, :]
                    cos, sin = (cs[:, j, t - 1, :].rearrange("p (a d) -> p a d", a=2).unsqueeze(1).to_broadcast([P, NHK, 2, 16])
                                for j in range(2))
                    qo = qr[s][:, :].rearrange("p (h a f d) -> p h a f d", h=NH, a=2, f=2)
                    for f, (c1, c2, op) in enumerate(((cos, sin, ALU.subtract), (sin, cos, ALU.add))):
                        link(nc.vector.tensor_tensor(t1[:, :, :, :], a, c1, ALU.mult))
                        link(nc.vector.tensor_tensor(t2[:, :, :, :], b, c2, ALU.mult))
                        link(nc.vector.tensor_tensor(qo[:, :, :, f, :], t1[:, 0:NH], t2[:, 0:NH], op))
                        for c in range(2):
                            ko = kd[s][:, :, c, :].rearrange("p h (a f d) -> p h a f d", a=2, f=2)
                            link(nc.vector.tensor_tensor(ko[:, :, :, f, :], t1[:, NH:], t2[:, NH:], op))
                    nc.vector.tensor_copy(ss[:, 0:1], ss[:, 0:1]).then_inc(src_done, 2)
            dve.wait_ge(ck_in, 16)
            dve.wait_ge(tr_done, NT - 1)
            for c in range(2):
                nc.vector.tensor_copy(kd[1][:, :, c, :], heads(ck[:, :])).then_inc(src_done, 1)

        @block.scalar
        def _(act):
            def evacuate(t):
                act.wait_ge(tr_done, t + 1)
                cols = slice(t * P, (t + 1) * P)
                if t < NT:
                    nc.scalar.activation(K.QT[:, :, cols], ps[t % 2][:, 0:8, :], ACT.Copy).then_inc(ev_done, 1)
                nc.scalar.activation(K.KT[:, :, cols], ps[t % 2][:, 8:12, :], ACT.Copy).then_inc(ev_done, 1)

            for t in range(NT):
                act.wait_ge(ms_done, t + 1)
                nc.scalar.activation(ss[:, :], ss[:, :], ACT.Sqrt).then_inc(rt_done, 1)
                if t:
                    evacuate(t - 1)
            evacuate(NT - 1)
            evacuate(NT)

        @block.tensor
        def _(pe):
            for t in range(NT + 1):
                s = t % 2
                pe.wait_ge(src_done, 2 * (t + 1))
                if t >= 2:
                    pe.wait_ge(ev_done, 2 * (t - 1))
                if t < NT:
                    for i in range(8):
                        nc.tensor.transpose(ps[s][:, i, :], qr[s][:, i * P:(i + 1) * P], K.ident[:, :])
                for i in range(NKV):
                    mm = nc.tensor.transpose(ps[s][:, 8 + i, :], kd[t % 2][:, i, :, :].rearrange("p c d -> p (c d)"), K.ident[:, :])
                mm.then_inc(tr_done, 1)



def phase_attention(nc, K, ctx):
    sem = K.phase_semaphores(ctx)
    sb = lambda n, s, d=F32: ctx.enter_context(nc.sbuf_tensor(n, s, d))
    SCALE = float(HD) ** -0.5
    STEPS = [(h, qt) for h in range(NH) for qt in range(NT)]
    J = len(STEPS)
    KW = TH
    prob = [sb(f"a_p{i}", [P, 2 * KW]) for i in range(3)]
    PT = [sb(f"a_pT{i}", [P, NT, T]) for i in range(2)]
    nb = sb("a_nb", [P, J]); nmax = sb("a_nmax", [P, J]); sm = sb("a_sum", [P, J]); rc = sb("a_rc", [P, J])
    ps_s = [ctx.enter_context(nc.psum_tensor(f"a_ps{i}", [P, 2, 512], F32)) for i in range(2)]
    ps_t = ctx.enter_context(nc.psum_tensor("a_pst", [P, 8, P], F32))
    ps_o = ctx.enter_context(nc.psum_tensor("a_pso", [P, 2, 512], F32))
    sc_done = sem("a_sc"); mx_done = sem("a_mx"); nb_done = sem("a_nb"); exp_done = sem("a_exp"); rc_done = sem("a_rc")
    pn_done = sem("a_pn"); pT_done = sem("a_pT"); ptev = sem("a_ptev"); pv_done = sem("a_pv"); oev = sem("a_oev")

    def scores(j):
        return ps_s[j % 2][:, :, 0:KW] if STEPS[j][1] else ps_s[j % 2][:, 0, 0:P]

    def probs(j):
        return prob[j % 3][:, :].rearrange("p (a c) -> p a c", a=2) if STEPS[j][1] else prob[j % 3][:, 0:P]

    with nc.Block() as block:
        @block.tensor
        def _(pe):
            def qk(j):
                h, qt = STEPS[j]
                rows = slice(64 * (h % 2), 64 * (h % 2) + 64)
                if j >= 2:
                    pe.wait_ge(exp_done, j - 1)
                q = K.QT[rows, h // 2, qt * P:(qt + 1) * P]
                if qt == 0:
                    mm = nc.tensor.matmul(ps_s[j % 2][:, 0, 0:P], q, K.KT[rows, h // 4, 0:P], start=True, stop=True)
                else:
                    for a in range(2):
                        mm = nc.tensor.matmul(ps_s[j % 2][:, a, 0:KW], q, K.KT[rows, h // 4, P + a * KW:P + (a + 1) * KW],
                                              start=True, stop=True)
                mm.then_inc(sc_done, 1)

            def transposes(j):
                pe.wait_ge(pn_done, j + 1)
                if j:
                    pe.wait_ge(ptev, j)
                for kt in range(NT if STEPS[j][1] else 1):
                    mm = nc.tensor.transpose(ps_t[:, kt, :], prob[j % 3][:, kt * P:(kt + 1) * P], K.ident[:, :])
                mm.then_inc(pT_done, 1)

            def pv(h):
                rows = slice(64 * (h % 2), 64 * (h % 2) + 64)
                kv = slice((h // 4) * HD, (h // 4 + 1) * HD)
                pe.wait_ge(ptev, NT * (h + 1))
                if h:
                    pe.wait_ge(oev, 2 * h)
                nc.tensor.matmul(ps_o[rows, 0, 0:P], K.vals[:, 0, kv], PT[h % 2][:, 0, 0:P], start=True, stop=True)
                for kt in range(NT):
                    mm = nc.tensor.matmul(ps_o[rows, 1, 0:4 * P], K.vals[:, kt + 1, kv], PT[h % 2][:, kt, P:T],
                                          start=(kt == 0), stop=(kt == NT - 1))
                mm.then_inc(pv_done, 1)

            for j in range(J + 2):
                if j < J:
                    qk(j)
                if j >= 2:
                    transposes(j - 2)
                    if STEPS[j - 2][1] == NT - 1:
                        pv(STEPS[j - 2][0])

        @block.vector
        def _(dve):
            def normalise(j):
                dve.wait_ge(exp_done, j + 1)
                nc.vector.reciprocal(rc[:, j:j + 1], sm[:, j:j + 1]).then_inc(rc_done, 1)
                dve.wait_ge(rc_done, j + 1)
                nc.vector.tensor_scalar(probs(j), probs(j), rc[:, j:j + 1], None, ALU.mult).then_inc(pn_done, 1)

            def output(h):
                rows = slice(64 * (h % 2), 64 * (h % 2) + 64)
                dve.wait_ge(pv_done, h + 1)
                nc.vector.tensor_copy(K.QT[rows, h // 2, 0:P], ps_o[rows, 0, 0:P]).then_inc(oev, 1)
                nc.vector.tensor_copy(K.QT[rows, h // 2, P:T], ps_o[rows, 1, 0:4 * P]).then_inc(oev, 1)

            for j in range(J):
                dve.wait_ge(sc_done, j + 1)
                nc.vector.tensor_reduce(nmax[:, j:j + 1], scores(j), axis=AX.XY if STEPS[j][1] else AX.X, op=ALU.max,
                                        negate=True).then_inc(mx_done, 1)
                dve.wait_ge(mx_done, j + 1)
                nc.vector.tensor_scalar(nb[:, j:j + 1], nmax[:, j:j + 1], SCALE, None, ALU.mult).then_inc(nb_done, 1)
                if j:
                    normalise(j - 1)
                if j >= NT + 3 and (j - 3) % NT == 0:
                    output((j - 3) // NT - 1)
            normalise(J - 1)
            output(NH - 1)

        @block.scalar
        def _(act):
            def evacuate(j):
                h, qt = STEPS[j]
                act.wait_ge(pT_done, j + 1)
                if h >= 2 and qt == 0:
                    act.wait_ge(pv_done, h - 1)
                n = NT if qt else 1
                nc.scalar.activation(PT[h % 2][:, 0:n, qt * P:(qt + 1) * P], ps_t[:, 0:n, :], ACT.Copy).then_inc(ptev, 1)

            for j in range(J):
                act.wait_ge(nb_done, j + 1)
                if j >= 3:
                    act.wait_ge(pT_done, j - 2)
                nc.scalar.activation(probs(j), scores(j), ACT.Exp, bias=nb[:, j:j + 1], scale=SCALE,
                                     accum_out=sm[:, j:j + 1]).then_inc(exp_done, 1)
                if j >= 2:
                    evacuate(j - 2)
            evacuate(J - 2)
            evacuate(J - 1)



def phase_merge(nc, K, ctx):
    S = Stream(nc, K)
    sem = K.phase_semaphores(ctx)
    sb = lambda n, s, d=F32: ctx.enter_context(nc.sbuf_tensor(n, s, d))
    oT = [sb(f"g_oT{i}", [P, KD, T], F32R) for i in range(2)]
    mergedT = sb("mergedT", [P, KD, T])
    merged_out = sem("g_merged_out")
    sg = [sb(f"g_sg{i}", [P, 4, TH]) for i in range(2)]
    ps = [[ctx.enter_context(nc.psum_tensor(f"g_ps{s}{i}", [P, TH], F32)) for i in range(4)] for s in range(2)]
    oh_done = sem("g_oh"); ol_done = sem("g_ol")
    mm_done = [sem("g_mm0"), sem("g_mm1")]
    bank_read = [sem("g_read0"), sem("g_read1")]
    out_done = [sem("g_out0"), sem("g_out1")]

    with nc.Block() as block:
        @block.sync
        def _(sp):
            with sp.Fori(0, N_MERGE // 2) as i:
                for s in range(2):
                    S.load(sp, 2 * i + (U_MERGE + s + 3), (s + 1) % 2)

        @block.gpsimd
        def _(pool):
            for i in range(4, 6):
                for s in range(2):
                    pool.wait_ge(bank_read[s], 4 * (i + 1))
                    pool.dma_start(K.sga_dram[2 * (2 * (i - 4) + s):2 * (2 * (i - 4) + s) + 2, :, :].rearrange("m p t -> p m t"),
                                   sg[s][:, :, :].rearrange("p (m a) t -> p m (a t)", a=2)).then_inc(out_done[s], 16)
                if i == 4:
                    pool.wait_ge(bank_read[1], 16)
                    pool.dma_start(K.merged_dram.rearrange("m p t -> p m t"), mergedT[:, :, :]).then_inc(merged_out, 16)
            for s in range(2):
                pool.wait_ge(out_done[s], 32)
            pool.wait_ge(merged_out, 16)

        @block.tensor
        def _(pe):
            def unit(i, s, act):
                n = 2 * i + (U_MERGE + s)
                S.ready(pe, n)
                if not isinstance(i, int):
                    pe.wait_ge(bank_read[s], 4 * i)
                project_features(nc, pe, (K.whi[s], K.wlo[s]), act, [p[:, :] for p in ps[s]]).then_inc(mm_done[s], 1)
                pe.drain().then_inc(K.hilo_free, 1)

            unit(0, 0, K.hT)
            pe.wait_ge(ol_done, 4)
            unit(0, 1, oT)
            with pe.Fori(1, 4) as i:
                unit(i, 0, K.hT)
                unit(i, 1, oT)
            with pe.Fori(4, 6) as i:
                unit(i, 0, K.hT)
                unit(i, 1, K.hT)

        @block.scalar
        def _(act):
            for q in range(4):
                nc.scalar.activation(oT[0][:, 2 * q:2 * q + 2, :], K.QT[:, 2 * q:2 * q + 2, :], ACT.Copy).then_inc(oh_done, 1)

            def sigmoids(i, s):
                act.wait_ge(mm_done[s], i + 1)
                for b in range(4):
                    nc.scalar.activation(sg[s][:, b, :], ps[s][b][:, :], ACT.Sigmoid).then_inc(bank_read[s], 1)

            def pair(i):
                if not isinstance(i, int):
                    act.wait_ge(bank_read[1], 4 * i)
                sigmoids(i, 0)
                S.hi(act, 2 * i + (U_MERGE + 2), 0)
                S.hi(act, 2 * i + (U_MERGE + 3), 1)

            pair(0)
            with act.Fori(1, 4) as i:
                pair(i)
            for i in range(4, 6):
                for s in range(2):
                    if i == 4:
                        act.wait_ge(bank_read[1], 16)
                    else:
                        act.wait_ge(out_done[s], 16)
                    sigmoids(i, s)
                    S.hi(act, 2 * i + (U_MERGE + 2 + s), s)

        @block.vector
        def _(dve):
            for q in range(4):
                dve.wait_ge(oh_done, q + 1)
                nc.vector.tensor_tensor(oT[1][:, 2 * q:2 * q + 2, :], K.QT[:, 2 * q:2 * q + 2, :],
                                        oT[0][:, 2 * q:2 * q + 2, :].bitcast(F32), ALU.subtract).then_inc(ol_done, 1)
            with dve.Fori(0, 4) as i:
                S.lo(dve, 2 * i + (U_MERGE + 2), 0)
                dve.wait_ge(mm_done[1], i + 1)
                dve.wait_ge(bank_read[0], 4 * i + 4)
                for b in range(4):
                    nc.vector.tensor_tensor(mergedT[:, bass.ds(2 * i + b // 2, 1), (b % 2) * TH:(b % 2 + 1) * TH],
                                            ps[1][b][:, :].unsqueeze(1), sg[0][:, b, :].unsqueeze(1), ALU.mult).then_inc(bank_read[1], 1)
                S.lo(dve, 2 * i + (U_MERGE + 3), 1)
            with dve.Fori(4, 6) as i:
                for s in range(2):
                    S.lo(dve, 2 * i + (U_MERGE + 2 + s), s)



def phase_ssd(nc, K, ctx):
    S = Stream(nc, K)
    sem = K.phase_semaphores(ctx)
    sb = lambda n, s, d=F32: ctx.enter_context(nc.sbuf_tensor(n, s, d))
    pb = lambda n, s: ctx.enter_context(nc.psum_tensor(n, s, F32))
    CW = 5
    PAD = CW // 2
    WC = P + PAD + 4 * P
    WI = WC + 2 * PAD
    XW = HPG * HP
    c0 = lambda c: 0 if c == 0 else P + PAD + (c - 1) * P
    ORDER = [4, 3, 2, 1, 0]
    cin = sb("s_cin", [P, 4, WI])
    xc = [sb(f"s_xc{i}", [P, 4, WC]) for i in range(2)]
    xb = sb("s_xb", [P, NT, XW + NS])
    xs = [sb(f"s_xs{i}", [P, 2, XW]) for i in range(2)]
    st = sb("s_st", [P, NT, 2, XW])
    pv = sb("s_pv", [P, 4, 2, XW])
    rT = sb("s_rT", [P, 2, HPG, P])
    E = sb("s_E", [P, HPG, P])
    stl = sb("s_stl", [P, P]); stu = sb("s_stu", [P, P])
    A = sb("s_A", [P, HPG, P]); B = sb("s_B", [P, HPG, P])
    M = [sb(f"s_M{i}", [P, HPG, P]) for i in range(2)]
    t3 = sb("s_t3", [P, 2, XW]); xd = sb("s_xd", [P, XW])
    yb = [sb(f"s_yb{i}", [P, XW]) for i in range(2)]
    cw = sb("s_cw", [P, 32, CW]); cb = sb("s_cb", [P, 32]); dsk = sb("s_dsk", [P, HEADS])
    ps_p = [pb(f"s_pp{i}", [P, TH]) for i in range(4)]
    ps_tr = pb("s_ptr", [P, XW + NS]); ps_T = pb("s_pT", [P, HPG, P]); ps_so = pb("s_pso", [P, 2, XW])
    ps_y = pb("s_py", [P, XW])
    ps_sc = ps_tr[:, 0:P]

    par_in = sem("s_par"); zero = sem("s_zero")
    pj_mm, cin_done, conv_done, silu_done = sem("s_pj"), sem("s_cin_done"), sem("s_conv"), sem("s_silu")
    tr_mm, xb_done, xs_done, st_mm, st_done = sem("s_tr"), sem("s_xb_done"), sem("s_xs_done"), sem("s_stmm"), sem("s_st_done")
    pv_in, pv_done, pv_step, s_out = sem("s_pv_in"), sem("s_pv_done"), sem("s_pv_step"), sem("s_s_out")
    rT_done, T_mm, sc_mm, E_done, ml_done = sem("s_rT_done"), sem("s_T"), sem("s_sc"), sem("s_E_done"), sem("s_ml")
    A_done, B_done, PM, M_done = sem("s_A_done"), sem("s_B_done"), sem("s_PM"), sem("s_M_done")
    y_mm, xd_done, t3_done, y_step, y_done = sem("s_y"), sem("s_xd_done"), sem("s_t3_done"), sem("s_y_step"), sem("s_y_done")
    y_out = [sem("s_y_out0"), sem("s_y_out1")]
    cv = sem("s_cv")
    first = lambda g: isinstance(g, int) and g == 0

    heads = lambda ap: ap.rearrange("p (h d) -> p h d", d=HP)

    def per_head(ap, n):
        return ap.unsqueeze(len(ap.shape)).to_broadcast(list(ap.shape) + [n])

    def decay(row, c, g):
        return K.decay[:, row, bass.ds(4 * g + c * HEADS, HPG)]

    with nc.Block() as block:
        @block.sync
        def _(sp):
            sp.dma_start(cw[:, :, :], K.conv_w_cols).then_inc(par_in, 16)
            sp.dma_start(cb[:, :], K.conv_b_cols).then_inc(par_in, 16)
            sp.dma_start(dsk[:, :], K.d_skip.partition_broadcast(P).rearrange("p o h -> p (o h)")).then_inc(par_in, 16)

            def group_dmas(g, loads):
                if not first(g):
                    sp.wait_ge(y_mm, 5 * g)
                sp.dma_start(pv[:, 0, 0, :], K.state_f[:, bass.ds(4 * g, HPG), :].rearrange("p h d -> p (h d)")).then_inc(pv_in, 16)
                sp.dma_start(pv[:, 3, 1, :], K.state_b[:, bass.ds(4 * g, HPG), :].rearrange("p h d -> p (h d)")).then_inc(pv_in, 16)
                if loads:
                    S.load(sp, 2 * g + (U_SSD + 5), 1)
                sp.wait_ge(st_done, 5 * g + 5)
                sp.dma_start(K.out_new_sf[:, bass.ds(4 * g, HPG), :], heads(st[:, 0, 0, :])).then_inc(s_out, 16)
                sp.dma_start(K.out_new_sb[:, bass.ds(4 * g, HPG), :], heads(st[:, 0, 1, :])).then_inc(s_out, 16)
                for c in range(NT):
                    sp.wait_ge(y_done, 5 * g + (c + 1))
                    sp.dma_start(K.y_dram[c * P:(c + 1) * P, bass.ds(g * XW, XW)], yb[c % 2][:, :]).then_inc(y_out[c % 2], 16)
                    if c == 2 and loads:
                        S.load(sp, 2 * g + (U_SSD + 6), 0)

            S.load(sp, U_SSD + 3, 1)
            S.load(sp, U_SSD + 4, 0)
            with sp.Fori(0, 7) as g:
                group_dmas(g, True)
            group_dmas(7, False)
            sp.wait_ge(s_out, 8 * 32)
            sp.wait_ge(y_out[0], 24 * 16)
            sp.wait_ge(y_out[1], 16 * 16)

        @block.gpsimd
        def _(pool):
            nc.gpsimd.memset(cin[:, :, :], 0.0).then_inc(zero, 1)
            pool.wait_ge(par_in, 48)

            def build_rT(g, c):
                if not (first(g) and c == 0):
                    pool.wait_ge(T_mm, 5 * g + c)
                for d, tri in ((0, K.tri_le), (1, K.tri_ge)):
                    ins = nc.gpsimd.tensor_tensor(rT[:, d], per_head(K.dtA[:, c, bass.ds(4 * g + d * HEADS, HPG)], P),
                                                  tri[:, :].unsqueeze(1).to_broadcast([P, HPG, P]), ALU.mult)
                ins.then_inc(rT_done, 1)

            def carry(g, n, to, frm, d, c):
                pool.wait_ge(st_done, 5 * g + (ORDER.index(c) + 1))
                if n:
                    pool.wait_ge(pv_done, 6 * g + n)
                row = 2 if d == 0 else 5
                nc.gpsimd.tensor_tensor(heads(pv[:, to - 1, d, :]), heads(pv[:, frm - 1, d, :]), per_head(decay(row, c, g), HP),
                                        ALU.mult).then_inc(pv_step, 1)
                pool.wait_ge(pv_step, 6 * g + (n + 1))
                nc.gpsimd.tensor_tensor(pv[:, to - 1, d, :], pv[:, to - 1, d, :], st[:, c, d, :], ALU.add).then_inc(pv_done, 1)

            def skip(g, c):
                if c == 0:
                    pool.wait_ge(xb_done, 5 * g + 5)
                if not (first(g) and c == 0):
                    pool.wait_ge(y_done, 5 * g + c)
                nc.gpsimd.tensor_tensor(heads(xd[:, :]), heads(xb[:, c, 0:XW]), per_head(dsk[:, bass.ds(4 * g, HPG)], HP),
                                        ALU.mult).then_inc(xd_done, 1)

            def forward_part(g, c):
                pool.wait_ge(ml_done, 5 * g + (c + 1))
                if not (first(g) and c == 0):
                    pool.wait_ge(M_done, 5 * g + c)
                nc.gpsimd.tensor_tensor(A[:, :, :], stl[:, :].unsqueeze(1).to_broadcast([P, HPG, P]),
                                        per_head(K.dt[:, c, bass.ds(4 * g, HPG)], P), ALU.mult).then_inc(A_done, 1)

            def group_work(g):
                build_rT(g, 0)
                pool.wait_ge(pv_in, 32 * g + 32)
                carry(g, 0, 3, 4, 1, 4)
                carry(g, 1, 2, 3, 1, 3)
                carry(g, 2, 1, 2, 1, 2)
                carry(g, 3, 2, 1, 0, 1)
                skip(g, 0)
                forward_part(g, 0)
                build_rT(g, 1)
                carry(g, 4, 3, 2, 0, 2)
                carry(g, 5, 4, 3, 0, 3)
                for c in range(1, NT):
                    forward_part(g, c)
                    if c + 1 < NT:
                        build_rT(g, c + 1)
                    skip(g, c)

            for g in range(GROUPS):
                group_work(g)

        def piece(pe, g, p):
            m, half = p // 2, p % 2
            unit = m // 2
            n = 2 * g + (U_SSD + unit)
            if p % 4 == 0:
                S.ready(pe, n)
            if half == 0 and not (first(g) and m < 2):
                pe.wait_ge(cin_done, 4 * g + (m - 1))
            wh, wl = (x[unit][:, :].rearrange("p (k c) -> p k c", k=KD) for x in (K.whi, K.wlo))
            ah, al = K.hT
            cols = slice((m % 2) * P, (m % 2 + 1) * P)
            for k in range(4 * half, 4 * half + 4):
                for lhs, rhs, f, l in ((wh, ah, k == 0, False), (wh, al, False, False), (wl, ah, False, k == KD - 1)):
                    for h in range(2):
                        mm = nc.tensor.matmul(ps_p[2 * (m % 2) + h][:, :], lhs[:, k, cols], rhs[:, k, h * TH:(h + 1) * TH],
                                              start=f, stop=l)
            if half:
                mm.then_inc(pj_mm, 1)
            if p % 4 == 3:
                pe.drain().then_inc(K.hilo_free, 1)

        @block.tensor
        def _(pe):
            def transposes(g, s, a):
                c = ORDER[a]
                if a == 0:
                    pe.wait_ge(silu_done, g + 1)
                    if not first(g):
                        pe.wait_ge(ml_done, 5 * g)
                if not (first(g) and a == 0):
                    pe.wait_ge(xb_done, 5 * g + a)
                for m in range(3):
                    mm = nc.tensor.transpose(ps_tr[:, m * P:(m + 1) * P], xc[s][:, m, c0(c):c0(c) + P], K.ident[:, :])
                mm.then_inc(tr_mm, 1)

            def states(g, a):
                c = ORDER[a]
                pe.wait_ge(xs_done, 5 * g + (a + 1))
                if a:
                    pe.wait_ge(st_done, 5 * g + a)
                elif not first(g):
                    pe.wait_ge(t3_done, 4 * g)
                nc.tensor.matmul(ps_so[:, :, :], xb[:, c, XW:], xs[a % 2][:, :, :], start=True, stop=True).then_inc(st_mm, 1)

            def between(g, s, c):
                if not (first(g) and c == 0):
                    pe.wait_ge(E_done, 5 * g + c)
                pe.wait_ge(rT_done, 5 * g + (c + 1))
                nc.tensor.matmul(ps_T[:, :, :], K.tri_gt[:, :], rT[:, 0], start=True, stop=False)
                nc.tensor.matmul(ps_T[:, :, :], K.tri_lt[:, :], rT[:, 1], start=False, stop=True).then_inc(T_mm, 1)
                if not (first(g) and c == 0):
                    pe.wait_ge(ml_done, 5 * g + c)
                if c == 0:
                    pe.wait_ge(xb_done, 5 * g + 5)
                nc.tensor.matmul(ps_sc, xc[s][:, 2, c0(c):c0(c) + P], xc[s][:, 3, c0(c):c0(c) + P],
                                 start=True, stop=True).then_inc(sc_mm, 1)

            def outputs(g, s, c):
                if not (first(g) and c == 0):
                    pe.wait_ge(y_done, 5 * g + c)
                if c:
                    if c == 1:
                        pe.wait_ge(st_done, 5 * g + 5)
                    else:
                        pe.wait_ge(t3_done, 4 * g + (c - 1))
                    pe.wait_ge(pv_done, 6 * g + (c + 2))
                    nc.tensor.matmul(ps_so[:, :, :], xc[s][:, 3, c0(c):c0(c) + P], pv[:, c - 1], start=True, stop=True)
                pe.wait_ge(M_done, 5 * g + (c + 1))
                for h in range(HPG):
                    mm = nc.tensor.matmul(ps_y[:, h * HP:(h + 1) * HP], M[c % 2][:, h, :], xb[:, c, h * HP:(h + 1) * HP],
                                          start=True, stop=True)
                mm.then_inc(y_mm, 1)

            def group_work(g, s, ahead):
                for k in range(11):
                    if k < NT:
                        transposes(g, s, k)
                    if 1 <= k <= NT:
                        states(g, k - 1)
                    if NT <= k < 2 * NT:
                        between(g, s, k - NT)
                    if k > NT:
                        outputs(g, s, k - NT - 1)
                    if ahead and k < 8:
                        piece(pe, g + 1, k)

            for p in range(8):
                piece(pe, 0, p)
            with pe.Fori(0, 3) as i:
                group_work(2 * i, 0, True)
                group_work(2 * i + 1, 1, True)
            group_work(6, 0, True)
            group_work(7, 1, False)

        @block.scalar
        def _(act):
            act.wait_ge(zero, 1)

            def conv_input(g, m):
                act.wait_ge(pj_mm, 4 * g + (m + 1))
                if not first(g):
                    act.wait_ge(conv_done, 4 * g + (m - 3))
                b = ps_p[2 * (m % 2):2 * (m % 2) + 2]
                nc.scalar.activation(cin[:, m, PAD:PAD + P], b[0][:, 0:P], ACT.Copy)
                nc.scalar.activation(cin[:, m, 2 * PAD + P:2 * PAD + TH], b[0][:, P:TH], ACT.Copy)
                nc.scalar.activation(cin[:, m, 2 * PAD + TH:2 * PAD + T], b[1][:, :], ACT.Copy).then_inc(cin_done, 1)

            def silus(g, s):
                act.wait_ge(conv_done, 4 * g + 4)
                nc.scalar.activation(xc[s][:, :, :], xc[s][:, :, :], ACT.Silu).then_inc(silu_done, 1)

            def token_major(g, a):
                act.wait_ge(tr_mm, 5 * g + (a + 1))
                if a == 0 and not first(g):
                    act.wait_ge(y_mm, 5 * g)
                    act.wait_ge(xd_done, 5 * g)
                nc.scalar.activation(xb[:, ORDER[a], :], ps_tr[:, :], ACT.Copy).then_inc(xb_done, 1)

            def chunk_states(g, a):
                act.wait_ge(st_mm, 5 * g + (a + 1))
                if a == 0 and not first(g):
                    act.wait_ge(pv_done, 6 * g)
                if a == 4 and not first(g):
                    act.wait_ge(s_out, 32 * g)
                nc.scalar.activation(st[:, ORDER[a]], ps_so[:, :, :], ACT.Copy).then_inc(st_done, 1)

            def exps(g, c):
                act.wait_ge(T_mm, 5 * g + (c + 1))
                if not (first(g) and c == 0):
                    act.wait_ge(M_done, 5 * g + c)
                nc.scalar.activation(E[:, :, :], ps_T[:, :, :], ACT.Exp).then_inc(E_done, 1)

            def group_work(g, s, ahead, split):
                token_major(g, 0)
                token_major(g, 1)
                chunk_states(g, 0)
                if ahead:
                    conv_input(g + 1, 0)
                token_major(g, 2)
                chunk_states(g, 1)
                token_major(g, 3)
                chunk_states(g, 2)
                if ahead:
                    conv_input(g + 1, 1)
                if split:
                    S.hi(act, 2 * g + (U_SSD + 4), 0)
                token_major(g, 4)
                chunk_states(g, 3)
                chunk_states(g, 4)
                exps(g, 0)
                if ahead:
                    conv_input(g + 1, 2)
                exps(g, 1)
                exps(g, 2)
                if ahead:
                    conv_input(g + 1, 3)
                if split:
                    S.hi(act, 2 * g + (U_SSD + 5), 1)
                exps(g, 3)
                exps(g, 4)
                if ahead:
                    silus(g + 1, 1 - s)

            for m in range(4):
                conv_input(0, m)
            S.hi(act, U_SSD + 2, 0)
            S.hi(act, U_SSD + 3, 1)
            silus(0, 0)
            with act.Fori(0, 3) as i:
                group_work(2 * i, 0, True, True)
                group_work(2 * i + 1, 1, True, True)
            group_work(6, 0, True, True)
            group_work(7, 1, False, False)

        @block.vector
        def _(dve):
            dve.wait_ge(par_in, 48)
            n_cv = 4 * (CW - 1)

            def convolve(g, s, m):
                tile = bass.ds(2 * g + m, 1) if m < 2 else bass.ds(g + (16 if m == 2 else 24), 1)
                dve.wait_ge(cin_done, 4 * g + (m + 1))
                if m == 0 and not (isinstance(g, int) and g < 2):
                    dve.wait_ge(y_mm, 5 * g - 5)
                tap = lambda w: cw[:, tile, w:w + 1].rearrange("p o w -> p (o w)")
                out = xc[s][:, m, :]
                nc.vector.tensor_scalar(out, cin[:, m, 0:WC], tap(0), cb[:, tile], ALU.mult, ALU.add).then_inc(cv, 1)
                for w in range(1, CW):
                    dve.wait_ge(cv, n_cv * g + (4 * m + w))
                    nc.vector.scalar_tensor_tensor(out, cin[:, m, w:w + WC], tap(w), out, ALU.mult,
                                                   ALU.add).then_inc(cv if w < CW - 1 else conv_done, 1)

            def weighted(g, a):
                c = ORDER[a]
                dve.wait_ge(xb_done, 5 * g + (a + 1))
                if a >= 2:
                    dve.wait_ge(st_mm, 5 * g + (a - 1))
                elif not first(g):
                    dve.wait_ge(st_mm, 5 * g)
                for d, row in ((0, 1), (1, 4)):
                    ins = nc.vector.tensor_tensor(heads(xs[a % 2][:, d, :]), heads(xb[:, c, 0:XW]), per_head(decay(row, c, g), HP), ALU.mult)
                ins.then_inc(xs_done, 1)

            def mix(g, c):
                dve.wait_ge(sc_mm, 5 * g + (c + 1))
                if not (first(g) and c == 0):
                    dve.wait_ge(A_done, 5 * g + c)
                nc.vector.tensor_tensor(stl[:, :], ps_sc, K.tri_le[:, :], ALU.mult)
                nc.vector.tensor_tensor(stu[:, :], ps_sc, K.tri_ge[:, :], ALU.mult).then_inc(ml_done, 1)
                dve.wait_ge(ml_done, 5 * g + (c + 1))
                nc.vector.tensor_tensor(B[:, :, :], stu[:, :].unsqueeze(1).to_broadcast([P, HPG, P]),
                                        per_head(K.dt[:, c, bass.ds(4 * g + HEADS, HPG)], P), ALU.mult).then_inc(B_done, 1)
                dve.wait_ge(B_done, 5 * g + (c + 1))
                dve.wait_ge(A_done, 5 * g + (c + 1))
                nc.vector.tensor_tensor(B[:, :, :], B[:, :, :], A[:, :, :], ALU.add).then_inc(PM, 1)
                dve.wait_ge(PM, 5 * g + (c + 1))
                dve.wait_ge(E_done, 5 * g + (c + 1))
                if c >= 2:
                    dve.wait_ge(y_mm, 5 * g + (c - 1))
                elif not first(g):
                    dve.wait_ge(y_mm, 5 * g)
                nc.vector.tensor_tensor(M[c % 2][:, :, :], B[:, :, :], E[:, :, :], ALU.mult).then_inc(M_done, 1)

            def finish(g, c):
                dve.wait_ge(y_mm, 5 * g + (c + 1))
                dve.wait_ge(xd_done, 5 * g + (c + 1))
                per, before = (3, c // 2) if c % 2 == 0 else (2, c // 2)
                if not (first(g) and before == 0):
                    dve.wait_ge(y_out[c % 2], 16 * per * g + 16 * before)
                y = yb[c % 2]
                if c:
                    nc.vector.tensor_tensor(t3[:, :, :].rearrange("p a (h d) -> p a h d", h=HPG),
                                            ps_so[:, :, :].rearrange("p a (h d) -> p a h d", h=HPG),
                                            per_head(K.decay[:, 0:4:3, bass.ds(4 * g + c * HEADS, HPG)], HP), ALU.mult).then_inc(t3_done, 1)
                    nc.vector.tensor_tensor(y[:, :], ps_y[:, 0:XW], xd[:, :], ALU.add).then_inc(y_step, 1)
                    dve.wait_ge(t3_done, 4 * g + c)
                    dve.wait_ge(y_step, 8 * g + (2 * c - 1))
                    nc.vector.tensor_tensor(y[:, :], y[:, :], t3[:, 0, :], ALU.add).then_inc(y_step, 1)
                    dve.wait_ge(y_step, 8 * g + 2 * c)
                    nc.vector.tensor_tensor(y[:, :], y[:, :], t3[:, 1, :], ALU.add).then_inc(y_done, 1)
                    dve.wait_ge(y_done, 5 * g + (c + 1))
                else:
                    nc.vector.tensor_tensor(y[:, :], ps_y[:, 0:XW], xd[:, :], ALU.add).then_inc(y_done, 1)

            def group_work(g, s, ahead, split):
                weighted(g, 0)
                weighted(g, 1)
                if ahead:
                    convolve(g + 1, 1 - s, 0)
                weighted(g, 2)
                weighted(g, 3)
                if ahead:
                    convolve(g + 1, 1 - s, 1)
                if split:
                    S.lo(dve, 2 * g + (U_SSD + 4), 0)
                weighted(g, 4)
                mix(g, 0)
                if ahead:
                    convolve(g + 1, 1 - s, 2)
                mix(g, 1)
                finish(g, 0)
                mix(g, 2)
                finish(g, 1)
                if ahead:
                    convolve(g + 1, 1 - s, 3)
                if split:
                    S.lo(dve, 2 * g + (U_SSD + 5), 1)
                mix(g, 3)
                finish(g, 2)
                mix(g, 4)
                finish(g, 3)
                finish(g, 4)

            for m in range(4):
                convolve(0, 0, m)
            S.lo(dve, U_SSD + 2, 0)
            S.lo(dve, U_SSD + 3, 1)
            with dve.Fori(0, 3) as i:
                group_work(2 * i, 0, True, True)
                group_work(2 * i + 1, 1, True, True)
            group_work(6, 0, True, True)
            group_work(7, 1, False, False)



def phase_ssd_norm(nc, K, ctx):
    sem = K.phase_semaphores(ctx)
    sb = lambda n, s, d=F32: ctx.enter_context(nc.sbuf_tensor(n, s, d))
    KI = DI // P
    y = [sb(f"n_y{i}", [P, DI]) for i in range(2)]
    z = [sb(f"n_z{i}", [P, DI]) for i in range(2)]
    w = sb("n_w", [P, DI]); ss = sb("n_ss", [P, NT])
    ps = [ctx.enter_context(nc.psum_tensor(f"n_ps{i}", [P, 4, P], F32)) for i in range(4)]
    y_in = [sem(f"n_y_in{i}") for i in range(2)]
    w_in = sem("n_w_in"); gz_done = sem("n_gz"); sq_done = sem("n_sq"); ms_done = sem("n_ms"); rt_done = sem("n_rt")
    r_done = sem("n_r"); yn_done = sem("n_yn"); tr_done = sem("n_tr"); hi_done = sem("n_hi"); lo_done = sem("n_lo")

    with nc.Block() as block:
        @block.sync
        def _(sp):
            for t in range(NT):
                if t >= 2:
                    sp.wait_ge(tr_done, 4 * (t - 1))
                sp.dma_start(y[t % 2][:, :], K.y_dram[t * P:(t + 1) * P, :]).then_inc(y_in[t % 2], 16)
                sp.dma_start(z[t % 2][:, :], K.z_dram[t * P:(t + 1) * P, :]).then_inc(y_in[t % 2], 16)
                if t == 0:
                    sp.dma_start(w[:, :], K.ssd_norm_w.partition_broadcast(P).rearrange("p o d -> p (o d)")).then_inc(w_in, 16)

        @block.vector
        def _(dve):
            def lows(t):
                for b in range(4):
                    dve.wait_ge(hi_done, 4 * t + b + 1)
                    nc.vector.tensor_tensor(K.yT[1][:, 4 * b:4 * b + 4, t * P:(t + 1) * P], ps[b][:, :, :],
                                            K.yT[0][:, 4 * b:4 * b + 4, t * P:(t + 1) * P].bitcast(F32), ALU.subtract).then_inc(lo_done, 1)

            for t in range(NT):
                s = t % 2
                dve.wait_ge(y_in[s], 32 * (t // 2 + 1))
                nc.vector.tensor_tensor(y[s][:, :], y[s][:, :], z[s][:, :], ALU.mult).then_inc(gz_done, 1)
                dve.wait_ge(sq_done, t + 1)
                nc.vector.tensor_scalar(ss[:, t:t + 1], ss[:, t:t + 1], 1.0 / DI, EPS, ALU.mult, ALU.add).then_inc(ms_done, 1)
                if t:
                    lows(t - 1)
                dve.wait_ge(rt_done, t + 1)
                nc.vector.reciprocal(ss[:, t:t + 1], ss[:, t:t + 1]).then_inc(r_done, 1)
                dve.wait_ge(r_done, t + 1)
                if t == 0:
                    dve.wait_ge(w_in, 16)
                nc.vector.scalar_tensor_tensor(y[s][:, :], y[s][:, :], ss[:, t:t + 1], w[:, :], ALU.mult, ALU.mult).then_inc(yn_done, 1)
            lows(NT - 1)

        @block.scalar
        def _(act):
            def highs(t):
                for b in range(4):
                    act.wait_ge(tr_done, 4 * t + b + 1)
                    nc.scalar.activation(K.yT[0][:, 4 * b:4 * b + 4, t * P:(t + 1) * P], ps[b][:, :, :], ACT.Copy).then_inc(hi_done, 1)

            for t in range(NT):
                act.wait_ge(gz_done, t + 1)
                nc.scalar.activation(z[t % 2][:, :], y[t % 2][:, :], ACT.Square, accum_out=ss[:, t:t + 1]).then_inc(sq_done, 1)
                act.wait_ge(ms_done, t + 1)
                nc.scalar.activation(ss[:, t:t + 1], ss[:, t:t + 1], ACT.Sqrt).then_inc(rt_done, 1)
                if t:
                    highs(t - 1)
            highs(NT - 1)

        @block.tensor
        def _(pe):
            for t in range(NT):
                pe.wait_ge(yn_done, t + 1)
                for b in range(4):
                    if t:
                        pe.wait_ge(lo_done, 4 * (t - 1) + b + 1)
                    for i in range(4):
                        k = 4 * b + i
                        mm = nc.tensor.transpose(ps[b][:, i, :], y[t % 2][:, k * P:(k + 1) * P], K.ident[:, :])
                    mm.then_inc(tr_done, 1)



def phase_ssd_out(nc, K, ctx):
    S = Stream(nc, K)
    sem = K.phase_semaphores(ctx)
    sb = lambda n, s, d=F32: ctx.enter_context(nc.sbuf_tensor(n, s, d))
    sg = [sb(f"o_sg{i}", [P, 2, T]) for i in range(2)]
    mb = [sb(f"o_mb{i}", [P, 2, T]) for i in range(2)]
    ps = [[ctx.enter_context(nc.psum_tensor(f"o_ps{s}{i}", [P, TH], F32)) for i in range(4)] for s in range(2)]
    ld = [sem("o_ld0"), sem("o_ld1")]
    mm_done = sem("o_mm"); gated = sem("o_gated"); added = sem("o_added"); out = [sem("o_out0"), sem("o_out1")]

    def columns(c):
        return bass.ds(2 * c, 2)

    with nc.Block() as block:
        @block.sync
        def _(sp):
            def block_dmas(c, s):
                sp.dma_start(sg[s][:, :, :], K.sga_dram[columns(c), :, :].rearrange("m p t -> p m t")).then_inc(ld[s], 16)
                sp.dma_start(mb[s][:, :, :], K.merged_dram[columns(c), :, :].rearrange("m p t -> p m t")).then_inc(ld[s], 16)

            block_dmas(0, 0)
            block_dmas(1, 1)
            for c in range(4):
                S.load(sp, U_SO + 2 * c + 3, 1)
                S.load(sp, U_SO + 2 * c + 4, 0)
                sp.wait_ge(added, 4 * (c + 1))
                sp.dma_start(K.merged_dram[2 * c:2 * c + 2, :, :].rearrange("m p t -> p m t"), mb[c % 2][:, :, :]).then_inc(out[c % 2], 16)
                if c + 2 < 4:
                    sp.wait_ge(out[c % 2], 16)
                    block_dmas(c + 2, c % 2)
            for s in range(2):
                sp.wait_ge(out[s], 32)

        @block.tensor
        def _(pe):
            pe.sem_inc(K.so_free, 8)

            def unit(c, s, half):
                S.ready(pe, 2 * c + (U_SO + half))
                wh, wl = (x[half][:, :].rearrange("p (k c) -> p k c", k=KD) for x in (K.whi, K.wlo))
                for m in range(2):
                    for k in range(KD):
                        cols, kk = slice(m * P, (m + 1) * P), half * KD + k
                        for lhs, rhs, f, l in ((wh, K.yT[0], kk == 0, False), (wh, K.yT[1], False, False),
                                               (wl, K.yT[0], False, kk == 2 * KD - 1)):
                            for h in range(2):
                                mm = nc.tensor.matmul(ps[s][2 * m + h][:, :], lhs[:, k, cols], rhs[:, kk, h * TH:(h + 1) * TH],
                                                      start=f, stop=l)
                if half:
                    mm.then_inc(mm_done, 1)
                pe.drain().then_inc(K.hilo_free, 1)

            with pe.Fori(0, 2) as i:
                for s in range(2):
                    c = 2 * i + s
                    pe.wait_ge(K.so_free, 4 * c + 4)
                    unit(c, s, 0)
                    unit(c, s, 1)

        @block.scalar
        def _(act):
            with act.Fori(0, 4) as c:
                S.hi(act, 2 * c + (U_SO + 2), 0)
                S.hi(act, 2 * c + (U_SO + 3), 1)

        @block.vector
        def _(dve):
            with dve.Fori(0, 2) as i:
                for s in range(2):
                    c = 2 * i + s
                    S.lo(dve, 2 * c + (U_SO + 2), 0)
                    dve.wait_ge(mm_done, c + 1)
                    dve.wait_ge(ld[s], 32 * i + 32)
                    for b in range(4):
                        v = sg[s][:, b // 2, (b % 2) * TH:(b % 2 + 1) * TH]
                        nc.vector.tensor_tensor(v, v, ps[s][b][:, :], ALU.mult).then_inc(K.so_free, 1)
                    dve.wait_ge(K.so_free, 4 * c + 12)
                    for b in range(4):
                        v = mb[s][:, b // 2, (b % 2) * TH:(b % 2 + 1) * TH]
                        nc.vector.tensor_tensor(v, v, sg[s][:, b // 2, (b % 2) * TH:(b % 2 + 1) * TH], ALU.add).then_inc(added, 1)
                    S.lo(dve, 2 * c + (U_SO + 3), 1)



def phase_mix_out(nc, K, ctx):
    S = Stream(nc, K)
    sem = K.phase_semaphores(ctx)
    sb = lambda n, s, d=F32: ctx.enter_context(nc.sbuf_tensor(n, s, d))
    m32 = sb("x_m32", [P, KD, T])
    mT = [sb(f"x_mT{i}", [P, KD, T], F32R) for i in range(2)]
    x = sb("x_x", [P, NT, D]); g1 = sb("x_g1", [P, 2, D]); tmp = sb("x_tmp", [P, 2 * UC])
    xn = sb("x_n", [P, D]); hf = sb("x_hf", [P, KD, P]); ss = sb("x_ss", [P, NT])
    ps = [ctx.enter_context(nc.psum_tensor(f"x_ps{t}", [P, 2 * UC], F32)) for t in range(NT)]
    ps_x = [ctx.enter_context(nc.psum_tensor(f"x_px{i}", [P, 4, P], F32)) for i in range(2)]
    m_in = sem("x_m_in"); x_in = sem("x_x_in"); mh = sem("x_mh"); ml = sem("x_ml"); mm_done = sem("x_mm")
    scaled = sem("x_scaled"); res = sem("x_res"); sq_done = sem("x_sq"); ms_done = sem("x_ms"); rt_done = sem("x_rt")
    r_done = sem("x_r"); xn_done = sem("x_xn"); tr_done = sem("x_tr"); hf_done = sem("x_hf_done"); hh = sem("x_hh"); hl = sem("x_hl")
    x_out = sem("x_out")

    with nc.Block() as block:
        @block.sync
        def _(sp):
            sp.dma_start(m32[:, :, :], K.merged_dram.rearrange("m p t -> p m t")).then_inc(m_in, 16)
            sp.dma_start(x[:, :, :], K.x.rearrange("(t p) d -> p t d", p=P)).then_inc(x_in, 16)
            for g in range(2):
                sp.dma_start(g1[:, g, :], K.gates[g:g + 1, 0:D].partition_broadcast(P).rearrange("p o d -> p (o d)")).then_inc(x_in, 16)
            for n in range(U_O, U_PQ):
                S.load(sp, n + 3, (n + 3) % 2)
            sp.wait_ge(res, 2 * NT)
            sp.dma_start(K.x2_dram.rearrange("(t p) d -> p t d", p=P), x[:, :, :]).then_inc(x_out, 16)
            sp.wait_ge(x_out, 16)

        @block.tensor
        def _(pe):
            pe.wait_ge(ml, 4)
            for n in range(U_O, U_PQ):
                i, s = (n - U_O) // 2, n % 2
                S.ready(pe, n)
                wh, wl = (w[s][:, :].rearrange("p (k c) -> p k c", k=KD) for w in (K.whi, K.wlo))
                for t in range(NT):
                    if i and s == 0:
                        pe.wait_ge(scaled, t + 1)
                    tc = slice(t * P, (t + 1) * P)
                    for k in range(KD):
                        mm = mm3(nc, ps[t][:, s * UC:(s + 1) * UC], (mT[0][:, k, tc], mT[1][:, k, tc]),
                                 (wh[:, k, :], wl[:, k, :]), k == 0, k == KD - 1)
                    if s == 1:
                        mm.then_inc(mm_done, 1)
                pe.drain().then_inc(K.hilo_free, 1)
            for t in range(NT):
                pe.wait_ge(xn_done, t + 1)
                for h in range(2):
                    if t:
                        pe.wait_ge(hf_done, KD * (t - 1) + 4 * (h + 1))
                    for k in range(4):
                        mm = nc.tensor.transpose(ps_x[h][:, k, :], xn[:, (4 * h + k) * P:(4 * h + k + 1) * P], K.ident[:, :])
                    mm.then_inc(tr_done, 1)

        @block.scalar
        def _(act):
            act.wait_ge(m_in, 16)
            for q in range(4):
                nc.scalar.activation(mT[0][:, 2 * q:2 * q + 2, :], m32[:, 2 * q:2 * q + 2, :], ACT.Copy).then_inc(mh, 1)
            for n in range(U_O, U_PQ):
                S.hi(act, n + 2, n % 2)
            for t in range(NT):
                act.wait_ge(res, NT + t + 1)
                if t:
                    act.wait_ge(tr_done, 2 * t)
                nc.scalar.activation(xn[:, :], x[:, t, :], ACT.Square, accum_out=ss[:, t:t + 1]).then_inc(sq_done, 1)
                act.wait_ge(ms_done, t + 1)
                nc.scalar.activation(ss[:, t:t + 1], ss[:, t:t + 1], ACT.Sqrt).then_inc(rt_done, 1)
                for h in range(2):
                    act.wait_ge(tr_done, 2 * t + h + 1)
                    if t and h == 0:
                        act.wait_ge(hl, t)
                    for k in range(4):
                        kd = 4 * h + k
                        nc.scalar.activation(hf[:, kd, :], ps_x[h][:, k, :], ACT.Identity,
                                             scale=K.mul2[:, kd, group(t):group(t) + 1],
                                             bias=K.add2[:, kd, group(t):group(t) + 1]).then_inc(hf_done, 1)

        @block.vector
        def _(dve):
            for q in range(4):
                dve.wait_ge(mh, q + 1)
                nc.vector.tensor_tensor(mT[1][:, 2 * q:2 * q + 2, :], m32[:, 2 * q:2 * q + 2, :],
                                        mT[0][:, 2 * q:2 * q + 2, :].bitcast(F32), ALU.subtract).then_inc(ml, 1)
            dve.wait_ge(x_in, 48)
            for i in range(2):
                for t in range(NT):
                    n = NT * i + t
                    dve.wait_ge(mm_done, n + 1)
                    cols = slice(i * 512, (i + 1) * 512)
                    if n:
                        dve.wait_ge(res, n)
                    nc.vector.tensor_tensor(tmp[:, :], ps[t][:, :], g1[:, group(t), cols], ALU.mult).then_inc(scaled, 1)
                    dve.wait_ge(scaled, n + 1)
                    nc.vector.tensor_tensor(x[:, t, cols], x[:, t, cols], tmp[:, :], ALU.add).then_inc(res, 1)
                S.lo(dve, U_O + 2 * i + 2, 0)
                S.lo(dve, U_O + 2 * i + 3, 1)
            for t in range(NT):
                dve.wait_ge(sq_done, t + 1)
                nc.vector.tensor_scalar(ss[:, t:t + 1], ss[:, t:t + 1], 1.0 / D, EPS, ALU.mult, ALU.add).then_inc(ms_done, 1)
                dve.wait_ge(rt_done, t + 1)
                nc.vector.reciprocal(ss[:, t:t + 1], ss[:, t:t + 1]).then_inc(r_done, 1)
                dve.wait_ge(r_done, t + 1)
                nc.vector.tensor_scalar(xn[:, :], x[:, t, :], ss[:, t:t + 1], None, ALU.mult).then_inc(xn_done, 1)
                dve.wait_ge(hf_done, KD * (t + 1))
                tc = slice(t * P, (t + 1) * P)
                nc.vector.tensor_copy(K.h2T[0][:, :, tc], hf[:, :, :]).then_inc(hh, 1)
                dve.wait_ge(hh, t + 1)
                nc.vector.tensor_tensor(K.h2T[1][:, :, tc], hf[:, :, :], K.h2T[0][:, :, tc].bitcast(F32), ALU.subtract).then_inc(hl, 1)



def phase_route(nc, K, ctx):
    S = Stream(nc, K)
    sem = K.phase_semaphores(ctx)
    sb = lambda n, s, d=F32: ctx.enter_context(nc.sbuf_tensor(n, s, d))
    LOW = -3.0e38
    keys = sb("r_keys", [P, 2 * PH, NKEYS])
    q = [sb(f"r_q{i}", [P, 2, T]) for i in range(2)]
    sc = [sb(f"r_sc{i}", [P, NT, 2, NKEYS]) for i in range(2)]
    v16 = sb("r_v16", [P, NT, 2, TOPK]); i16 = sb("r_i16", [P, NT, 2, TOPK], U32); f16 = sb("r_f16", [P, NT, 2, TOPK])
    cand = sb("r_cand", [P, NT, TOPK, TOPK])
    bv = sb("r_bv", [P, NT, TOPK]); bi = sb("r_bi", [P, NT, TOPK], U32)
    ki = sb("r_ki", [P, 2, NT, TOPK], U32); kf = sb("r_kf", [P, 2, NT * TOPK])
    eq = sb("r_eq", [P, NT * TOPK, TOPK]); bs = sb("r_bs", [P, NT, TOPK]); be = sb("r_be", [P, NT, TOPK])
    sm = sb("r_sm", [P, NT])
    slots = sb("r_slots", [P, 3, NT, SLOTS])
    ps = [ctx.enter_context(nc.psum_tensor(f"r_ps{i}", [P, TH], F32)) for i in range(4)]
    ps_k = [ctx.enter_context(nc.psum_tensor(f"r_pk{i}", [P, 2, 2, NKEYS], F32)) for i in range(3)]
    ps_t = ctx.enter_context(nc.psum_tensor("r_pt", [P, 3, P], F32))
    k_in = sem("r_k_in"); mm_done = sem("r_mm"); q_done = sem("r_q_done"); sc_mm = sem("r_sc_mm"); sc_done = sem("r_sc_done")
    chain = sem("r_chain"); top_done = sem("r_top"); sub_done = sem("r_sub"); be_done = sem("r_be_done"); slot_done = sem("r_slot")
    tr_done = sem("r_tr"); ev_done = sem("r_ev"); gh = sem("r_gh")

    with nc.Block() as block:
        @block.sync
        def _(sp):
            sp.dma_start(keys[:, :, :], K.keys_t).then_inc(k_in, 16)
            with sp.Fori(0, PH // 2) as i:
                for s in range(2):
                    S.load(sp, 2 * i + (U_PQ + s + 3), (s + 1) % 2)

        @block.tensor
        def _(pe):
            pe.wait_ge(k_in, 16)

            def queries(h, s):
                S.ready(pe, h + U_PQ)
                if not (isinstance(h, int) and h == 0):
                    pe.wait_ge(q_done, 4 * h)
                project_features(nc, pe, (K.whi[s], K.wlo[s]), K.h2T, [p[:, :] for p in ps]).then_inc(mm_done, 1)
                pe.drain().then_inc(K.hilo_free, 1)

            def scores(h, s):
                pe.wait_ge(q_done, 4 * h + 4)
                if not (isinstance(h, int) and h == 0):
                    pe.wait_ge(sc_done, 3 * h)
                for t in range(NT):
                    for c in range(2):
                        mm = nc.tensor.matmul(ps_k[t // 2][:, t % 2, c, :], q[s][:, c, t * P:(t + 1) * P],
                                              keys[:, bass.ds(2 * h + c, 1), :].rearrange("p o k -> p (o k)"), start=True, stop=True)
                mm.then_inc(sc_mm, 1)

            queries(0, 0)
            with pe.Fori(0, 3) as i:
                queries(2 * i + 1, 1)
                scores(2 * i, 0)
                queries(2 * i + 2, 0)
                scores(2 * i + 1, 1)
            queries(7, 1)
            scores(6, 0)
            scores(7, 1)
            pe.wait_ge(slot_done, PH)
            for t in range(NT):
                if t:
                    pe.wait_ge(ev_done, t)
                for r in range(3):
                    mm = nc.tensor.transpose(ps_t[:, r, :], slots[:, r, t, :], K.ident[:, :])
                mm.then_inc(tr_done, 1)

        @block.scalar
        def _(act):
            def copies(h, s):
                act.wait_ge(mm_done, h + 1)
                if not (isinstance(h, int) and h < 2):
                    act.wait_ge(sc_mm, h - 1)
                for m in range(2):
                    for a in range(2):
                        nc.scalar.activation(q[s][:, m, a * TH:(a + 1) * TH], ps[2 * m + a][:, :], ACT.Copy).then_inc(q_done, 1)
                S.hi(act, h + (U_PQ + 2), s)

            def score_copies(h, s):
                act.wait_ge(sc_mm, h + 1)
                if not (isinstance(h, int) and h < 2):
                    act.wait_ge(top_done, h - 1)
                for b in range(3):
                    n = 2 if b < 2 else 1
                    nc.scalar.activation(sc[s][:, 2 * b:2 * b + n, :, :], ps_k[b][:, 0:n, :, :], ACT.Copy).then_inc(sc_done, 1)

            def gate_exp(h):
                act.wait_ge(sub_done, h + 1)
                nc.scalar.activation(be[:, :, :], bs[:, :, :], ACT.Exp).then_inc(be_done, 1)

            copies(0, 0)
            copies(1, 1)
            score_copies(0, 0)
            with act.Fori(0, 3) as i:
                copies(2 * i + 2, 0)
                score_copies(2 * i + 1, 1)
                gate_exp(2 * i)
                copies(2 * i + 3, 1)
                score_copies(2 * i + 2, 0)
                gate_exp(2 * i + 1)
            score_copies(7, 1)
            gate_exp(6)
            gate_exp(7)
            for t in range(NT):
                act.wait_ge(tr_done, t + 1)
                nc.scalar.activation(K.slotsT[:, :, t * P:(t + 1) * P], ps_t[:, :, :], ACT.Copy).then_inc(ev_done, 1)

        @block.vector
        def _(dve):
            LINKS = NT * 2 * 5 + NT * 5 + 12 + 2

            def search(h, s):
                k = [0]

                def link(ins):
                    k[0] += 1
                    ins.then_inc(chain, 1)
                    dve.wait_ge(chain, LINKS * h + k[0])

                def top16(values, best, index):
                    link(nc.vector.max(best[:, 0:8], values))
                    link(nc.vector.max_index(index[:, 0:8], best[:, 0:8], values))
                    link(nc.vector.match_replace(out=values, in_to_replace=best[:, 0:8], in_values=values, imm_value=LOW))
                    link(nc.vector.max(best[:, 8:16], values))
                    link(nc.vector.max_index(index[:, 8:16], best[:, 8:16], values))

                dve.wait_ge(sc_done, 3 * h + 3)
                for t in range(NT):
                    for c in range(2):
                        top16(sc[s][:, t, c, :], v16[:, t, c, :], i16[:, t, c, :])
                link(nc.vector.tensor_copy(f16[:, :, :, :], i16[:, :, :, :]))
                for t in range(NT):
                    ins = nc.vector.tensor_tensor(cand[:, t], v16[:, t, 0, :].unsqueeze(2).to_broadcast([P, TOPK, TOPK]),
                                                  v16[:, t, 1, :].unsqueeze(1).to_broadcast([P, TOPK, TOPK]), ALU.add)
                ins.then_inc(top_done, 1)
                dve.wait_ge(top_done, h + 1)
                for t in range(NT):
                    top16(cand[:, t].rearrange("p a b -> p (a b)"), bv[:, t, :], bi[:, t, :])
                nc.vector.tensor_tensor(bs[:, :, :], bv[:, :, :], bv[:, :, 0:1].to_broadcast([P, NT, TOPK]), ALU.subtract).then_inc(sub_done, 1)
                nc.vector.tensor_scalar(ki[:, 0], bi[:, :, :], 4, None, ALU.logical_shift_right)
                link(nc.vector.tensor_scalar(ki[:, 1], bi[:, :, :], 15, None, ALU.bitwise_and))
                link(nc.vector.tensor_copy(kf[:, :, :], ki[:, :, :, :].rearrange("p c t k -> p c (t k)")))
                slot = bass.ds(TOPK * h, TOPK)
                for c in range(2):
                    link(nc.vector.tensor_tensor(eq[:, :, :], kf[:, c, :].unsqueeze(2).to_broadcast([P, NT * TOPK, TOPK]),
                                                 K.iota[:, 0:TOPK].unsqueeze(1).to_broadcast([P, NT * TOPK, TOPK]), ALU.is_equal))
                    e4 = eq[:, :, :].rearrange("p (t k) e -> p t k e", t=NT)
                    link(nc.vector.tensor_tensor(e4, e4, f16[:, :, c, :].unsqueeze(2).to_broadcast([P, NT, TOPK, TOPK]), ALU.mult))
                    link(nc.vector.tensor_reduce(slots[:, c, :, slot], e4, axis=AX.X, op=ALU.add))
                dve.wait_ge(be_done, h + 1)
                link(nc.vector.tensor_reduce(sm[:, :], be[:, :, :], axis=AX.X, op=ALU.add))
                link(nc.vector.reciprocal(sm[:, :], sm[:, :]))
                while k[0] < LINKS:
                    link(nc.vector.tensor_copy(kf[:, 0, 0:1], kf[:, 0, 0:1]))
                nc.vector.tensor_tensor(slots[:, 2, :, slot], be[:, :, :], sm[:, :].unsqueeze(2).to_broadcast([P, NT, TOPK]),
                                        ALU.mult).then_inc(slot_done, 1)
                dve.wait_ge(slot_done, h + 1)

            S.lo(dve, U_PQ + 2, 0)
            S.lo(dve, U_PQ + 3, 1)
            for h in range(PH):
                search(h, h % 2)
                if h < PH - 2:
                    S.lo(dve, h + U_PQ + 4, h % 2)
            dve.wait_ge(ev_done, NT)
            nc.vector.tensor_copy(K.gate_hi[:, :], K.slotsT[:, 2, :]).then_inc(gh, 1)
            dve.wait_ge(gh, 1)
            nc.vector.tensor_tensor(K.gate_lo[:, :], K.slotsT[:, 2, :], K.gate_hi[:, :].bitcast(F32), ALU.subtract)



def phase_gates(nc, K, ctx):
    sem = K.phase_semaphores(ctx)
    sb = lambda n, s, d=F32: ctx.enter_context(nc.sbuf_tensor(n, s, d))
    TB, Q = 64, 4
    GPS = TB // Q
    stage = [sb(f"e_st{i}", [P, P, TB]) for i in range(2)]
    col = [sb(f"e_col{i}", [P, 4, Q]) for i in range(2)]
    oj = [sb(f"e_oj{i}", [P, Q, P], F32R) for i in range(2)]
    oi = [sb(f"e_oi{i}", [P, Q, 2, P], F32R) for i in range(2)]
    ps = [ctx.enter_context(nc.psum_tensor(f"e_ps{i}", [P, Q, P], F32)) for i in range(2)]
    col_done = sem("e_col"); hot_done = sem("e_hot"); mm_done = sem("e_mm"); ev_done = sem("e_ev")
    out = [sem("e_out0"), sem("e_out1")]

    with nc.Block() as block:
        @block.sync
        def _(sp):
            with sp.Fori(0, T // TB // 2) as b:
                for s in range(2):
                    sp.wait_ge(ev_done, 2 * GPS * b + (GPS * (s + 1)))
                    sp.dma_start(K.g_dram[bass.ds(2 * b + s, 1)].rearrange("o j i t -> j (o i t)"),
                                 stage[s][:, :, :].rearrange("p i t -> p (i t)")).then_inc(out[s], 16)
            for s in range(2):
                sp.wait_ge(out[s], 16 * (T // TB // 2))

        @block.vector
        def _(dve):
            dve.sem_inc(mm_done, 2)

            def one_hots(g, u):
                dve.wait_ge(mm_done, g + 1)
                tok = bass.ds(4 * g, Q)
                nc.vector.tensor_copy(col[u][:, 0:2, :], K.slotsT[:, 0:2, tok])
                nc.vector.tensor_copy(col[u][:, 2, :], K.gate_hi[:, tok].bitcast(F32))
                nc.vector.tensor_copy(col[u][:, 3, :], K.gate_lo[:, tok].bitcast(F32)).then_inc(col_done, 1)
                dve.wait_ge(col_done, g + 1)
                for t in range(Q):
                    c = lambda r: col[u][:, r, t:t + 1]
                    nc.vector.tensor_scalar(oj[u][:, t, :], K.iota[:, :], c(1), None, ALU.is_equal)
                    nc.vector.tensor_scalar(oi[u][:, t, 0, :], K.iota[:, :], c(0), c(2), ALU.is_equal, ALU.mult)
                    ins = nc.vector.tensor_scalar(oi[u][:, t, 1, :], K.iota[:, :], c(0), c(3), ALU.is_equal, ALU.mult)
                ins.then_inc(hot_done, 1)

            with dve.Fori(0, T // Q // 2) as i:
                for u in range(2):
                    one_hots(2 * i + u, u)

        @block.tensor
        def _(pe):
            pe.sem_inc(K.g_free, 2)

            def products(g, u):
                pe.wait_ge(hot_done, g + 1)
                pe.wait_ge(K.g_free, g + 1)
                for t in range(Q):
                    for part in range(2):
                        mm = nc.tensor.matmul(ps[u][:, t, :], oj[u][:, t, :], oi[u][:, t, part, :], start=(part == 0), stop=(part == 1))
                mm.then_inc(mm_done, 1)

            with pe.Fori(0, T // Q // 2) as i:
                for u in range(2):
                    products(2 * i + u, u)

        @block.scalar
        def _(act):
            def stage_part(b, s, g0, q, u):
                act.wait_ge(mm_done, g0 + 3)
                nc.scalar.activation(stage[s][:, :, bass.ds(Q * q, Q)].rearrange("p i t -> p t i"), ps[u][:, :, :],
                                     ACT.Copy).then_inc(ev_done, 1)
                act.wait_ge(ev_done, g0 + 1)
                act.sem_inc(K.g_free, 1)

            def fill(b, s):
                with act.Fori(0, GPS // 2) as i:
                    for u in range(2):
                        stage_part(b, s, b * (2 * GPS) + 2 * i + (GPS * s + u), 2 * i + u, u)

            fill(0, 0)
            fill(0, 1)
            with act.Fori(1, T // TB // 2) as b:
                for s in range(2):
                    act.wait_ge(out[s], 16 * b)
                    fill(b, s)



def phase_experts(nc, K, ctx):
    S = Stream(nc, K)
    sem = K.phase_semaphores(ctx)
    sb = lambda n, s, d=F32: ctx.enter_context(nc.sbuf_tensor(n, s, d))
    PAIRS = NKEYS // 2
    TB = 64
    NB = 4
    OUTS = [(t, d) for t in range(NT) for d in range(2)]
    NO = len(OUTS)
    G = [sb(f"p_g{i}", [P, T // TB, 2, TB]) for i in range(2)]
    A = sb("p_a", [P, 2, T]); W = sb("p_w", [P, 2, T])
    Wh = [sb(f"p_wh{i}", [P, 2, T], F32R) for i in range(2)]
    Wl = [sb(f"p_wl{i}", [P, 2, T], F32R) for i in range(2)]
    ps_a = [ctx.enter_context(nc.psum_tensor(f"p_pa{i}", [P, TH], F32)) for i in range(4)]
    ps_y = [ctx.enter_context(nc.psum_tensor(f"p_py{i}", [P, 512], F32)) for i in range(NB)]
    g_in = [sem("p_g_in0"), sem("p_g_in1")]
    a_mm = sem("p_a_mm"); a_done = sem("p_a_done"); w_done = sem("p_w_done"); wh_done = sem("p_wh_done"); wl_done = sem("p_wl_done")
    y_mm = sem("p_y_mm"); y_added = sem("p_y_added"); zeroed = sem("p_zero")
    is0 = lambda n: isinstance(n, int) and n == 0

    with nc.Block() as block:
        @block.sync
        def _(sp):
            def load_g(n, s):
                sp.dma_start(G[s][:, :, :, :], K.g_dram[:, :, bass.ds(2 * n, 2), :].rearrange("b j i t -> j b i t")).then_inc(g_in[s], 16)

            def pair(n, s, stream, gates):
                if stream:
                    S.load(sp, 2 * n + (U_EXP + 4), 0)
                if gates:
                    sp.wait_ge(w_done, n + 1)
                    load_g(n + 2, s)
                if stream:
                    S.load(sp, 2 * n + (U_EXP + 5), 1)

            load_g(0, 0)
            load_g(1, 1)
            S.load(sp, U_EXP + 3, 1)
            with sp.Fori(0, 30) as i:
                pair(2 * i, 0, True, True)
                pair(2 * i + 1, 1, True, True)
            pair(60, 0, True, True)
            pair(61, 1, False, True)
            S.load(sp, U_EXP + 126, 0)
            S.load(sp, U_EXP + 127, 1)

        @block.tensor
        def _(pe):
            def hidden(n, slot):
                S.ready(pe, U_EXP if is0(n) else 2 * n + (U_EXP - 1))
                if not is0(n):
                    pe.wait_ge(a_done, 4 * n)
                project_features(nc, pe, (K.whi[slot], K.wlo[slot]), K.h2T, [p[:, :] for p in ps_a]).then_inc(a_mm, 1)
                pe.drain().then_inc(K.hilo_free, 1)

            def output(n, s, slot, unit):
                S.ready(pe, unit)
                pe.wait_ge(wl_done, n + 1)
                vh, vl = (x[slot][:, :].rearrange("p (c d) -> p c d", c=2) for x in (K.whi, K.wlo))
                for o, (t, d) in enumerate(OUTS):
                    last = o - NB if o >= NB else max(x for x in range(NO) if x % NB == o) - NO
                    pe.wait_ge(y_added, NO * n + (NO + last + 1))
                    tc, dc = slice(t * P, (t + 1) * P), slice(d * 512, (d + 1) * 512)
                    for c in range(2):
                        mm = mm3(nc, ps_y[o % NB][:, :], (Wh[s][:, c, tc], Wl[s][:, c, tc]), (vh[:, c, dc], vl[:, c, dc]), c == 0, c == 1)
                    mm.then_inc(y_mm, 1)
                pe.drain().then_inc(K.hilo_free, 1)

            hidden(0, 0)
            with pe.Fori(0, 31) as i:
                for s in range(2):
                    n = 2 * i + s
                    hidden(n + 1, 1)
                    output(n, s, 0, 2 * n + (U_EXP + 2))
            hidden(63, 1)
            output(62, 0, 0, U_EXP + 126)
            output(63, 1, 1, U_EXP + 127)

        @block.scalar
        def _(act):
            def gelu(n, s):
                act.wait_ge(a_mm, n + 1)
                if not is0(n):
                    act.wait_ge(w_done, n)
                for m in range(2):
                    for h in range(2):
                        nc.scalar.activation(A[:, m, h * TH:(h + 1) * TH], ps_a[2 * m + h][:, :], ACT.Gelu_apprx_tanh).then_inc(a_done, 1)

            def w_hi(n, s):
                act.wait_ge(w_done, n + 1)
                if not (isinstance(n, int) and n < 2):
                    act.wait_ge(y_mm, NO * n - NO)
                nc.scalar.activation(Wh[s][:, :, :], W[:, :, :], ACT.Copy).then_inc(wh_done, 1)

            gelu(0, 0)
            S.hi(act, U_EXP + 2, 0)
            w_hi(0, 0)
            gelu(1, 1)
            S.hi(act, U_EXP + 3, 1)
            w_hi(1, 1)
            S.hi(act, U_EXP + 4, 0)
            with act.Fori(1, 31) as i:
                for s in range(2):
                    n = 2 * i + s
                    gelu(n, s)
                    S.hi(act, 2 * n + (U_EXP + 1), 1)
                    w_hi(n, s)
                    S.hi(act, 2 * n + (U_EXP + 2), 0)
            gelu(62, 0)
            S.hi(act, U_EXP + 125, 1)
            w_hi(62, 0)
            S.hi(act, U_EXP + 126, 0)
            gelu(63, 1)
            S.hi(act, U_EXP + 127, 1)
            w_hi(63, 1)

        @block.vector
        def _(dve):
            dve.sem_inc(y_added, NO)
            nc.vector.memset(K.y[:, :, :], 0.0).then_inc(zeroed, 1)
            dve.wait_ge(zeroed, 1)

            def weight(n, s):
                dve.wait_ge(a_done, 4 * n + 4)
                dve.wait_ge(g_in[s], 8 * (n - s) + 16)
                if not is0(n):
                    dve.wait_ge(wh_done, n)
                    dve.wait_ge(wl_done, n)
                for c in range(2):
                    ins = nc.vector.tensor_tensor(W[:, c, :].rearrange("p (b t) -> p b t", t=TB),
                                                  A[:, c, :].rearrange("p (b t) -> p b t", t=TB), G[s][:, :, c, :], ALU.mult)
                ins.then_inc(w_done, 1)

            def w_lo(n, s):
                dve.wait_ge(wh_done, n + 1)
                nc.vector.tensor_tensor(Wl[s][:, :, :], W[:, :, :], Wh[s][:, :, :].bitcast(F32), ALU.subtract).then_inc(wl_done, 1)

            def add(n, lo, hi):
                for o in range(lo, hi):
                    t, d = OUTS[o]
                    dve.wait_ge(y_mm, NO * n + (o + 1))
                    v = K.y[:, t, d * 512:(d + 1) * 512]
                    nc.vector.tensor_tensor(v, v, ps_y[o % NB][:, :], ALU.add).then_inc(y_added, 1)

            def step(n, s, first_unit, second_unit):
                add(n, 0, 1)
                weight(n + 1, 1 - s)
                S.lo(dve, first_unit, 1)
                add(n, 1, 3)
                w_lo(n + 1, 1 - s)
                add(n, 3, NO)
                if second_unit is not None:
                    S.lo(dve, second_unit, 0)

            weight(0, 0)
            S.lo(dve, U_EXP + 2, 0)
            w_lo(0, 0)
            with dve.Fori(0, 31) as i:
                for s in range(2):
                    n = 2 * i + s
                    step(n, s, 2 * n + (U_EXP + 3), 2 * n + (U_EXP + 4))
            step(62, 0, U_EXP + 127, None)
            add(63, 0, NO)



def phase_final(nc, K, ctx):
    sem = K.phase_semaphores(ctx)
    sb = lambda n, s, d=F32: ctx.enter_context(nc.sbuf_tensor(n, s, d))
    x = sb("f_x", [P, NT, D]); g2 = sb("f_g2", [P, 2, D]); w = sb("f_w", [P, D]); sq = sb("f_sq", [P, D]); ss = sb("f_ss", [P, NT])
    ld = sem("f_ld"); scaled = sem("f_scaled"); res = sem("f_res"); sq_done = sem("f_sq_done"); ms_done = sem("f_ms"); rt_done = sem("f_rt")
    r_done = sem("f_r"); o_done = sem("f_o"); out = sem("f_out")

    with nc.Block() as block:
        @block.sync
        def _(sp):
            sp.dma_start(x[:, :, :], K.x2_dram.rearrange("(t p) d -> p t d", p=P)).then_inc(ld, 16)
            for g in range(2):
                sp.dma_start(g2[:, g, :], K.gates[g:g + 1, D:2 * D].partition_broadcast(P).rearrange("p o d -> p (o d)")).then_inc(ld, 16)
            sp.dma_start(w[:, :], K.final_norm_w.partition_broadcast(P).rearrange("p o d -> p (o d)")).then_inc(ld, 16)
            for t in range(NT):
                sp.wait_ge(o_done, t + 1)
                sp.dma_start(K.out_y[t * P:(t + 1) * P, :], x[:, t, :]).then_inc(out, 16)
            sp.wait_ge(out, 16 * NT)

        @block.vector
        def _(dve):
            dve.wait_ge(ld, 64)
            for t in range(NT):
                nc.vector.tensor_tensor(K.y[:, t, :], K.y[:, t, :], g2[:, group(t), :], ALU.mult).then_inc(scaled, 1)
            for t in range(NT):
                dve.wait_ge(scaled, t + 1)
                nc.vector.tensor_tensor(x[:, t, :], x[:, t, :], K.y[:, t, :], ALU.add).then_inc(res, 1)
            dve.wait_ge(sq_done, NT)
            nc.vector.tensor_scalar(ss[:, :], ss[:, :], 1.0 / D, EPS, ALU.mult, ALU.add).then_inc(ms_done, 1)
            dve.wait_ge(rt_done, 1)
            nc.vector.reciprocal(ss[:, :], ss[:, :]).then_inc(r_done, 1)
            dve.wait_ge(r_done, 1)
            for t in range(NT):
                nc.vector.scalar_tensor_tensor(x[:, t, :], x[:, t, :], ss[:, t:t + 1], w[:, :], ALU.mult, ALU.mult).then_inc(o_done, 1)

        @block.scalar
        def _(act):
            for t in range(NT):
                act.wait_ge(res, t + 1)
                if t:
                    act.wait_ge(sq_done, t)
                nc.scalar.activation(sq[:, :], x[:, t, :], ACT.Square, accum_out=ss[:, t:t + 1]).then_inc(sq_done, 1)
            act.wait_ge(ms_done, 1)
            nc.scalar.activation(ss[:, :], ss[:, :], ACT.Sqrt).then_inc(rt_done, 1)



PHASES = [phase_modulate, phase_tokens]


def run_phase(nc, K, phase):
    K.sems = []

    def phase_semaphores(ctx):
        def sem(name):
            K.sems.append(ctx.enter_context(nc.semaphore(name)))
            return K.sems[-1]
        return sem

    K.phase_semaphores = phase_semaphores
    with ExitStack() as ctx:
        phase(nc, K, ctx)
        with nc.Block() as block:
            @block.gpsimd
            def _(pool):
                for s in K.sems:
                    pool.sem_clear(s)


def build(nc, K):
    ctx = ExitStack()
    with ctx:
        sb = lambda n, s, d=F32: ctx.enter_context(nc.sbuf_tensor(n, s, d))
        sem = lambda n: ctx.enter_context(nc.semaphore(n))
        K.raw = [sb(f"w_raw{i}", [P, 8 * UC]) for i in range(2)]
        K.whi = [sb(f"w_hi{i}", [P, 8 * UC], F32R) for i in range(2)]
        K.wlo = [sb(f"w_lo{i}", [P, 8 * UC], F32R) for i in range(2)]
        K.w_loaded = [sem("w_loaded0"), sem("w_loaded1")]
        K.w_hi_done, K.w_lo_done, K.hilo_free = (sem(n) for n in ("w_hi_done", "w_lo_done", "hilo_free"))
        K.ident, K.ones, K.iota = sb("ident", [P, P]), sb("ones", [P, P]), sb("iota", [P, P])
        K.tri_le, K.tri_gt, K.tri_ge, K.tri_lt = (sb(n, [P, P]) for n in ("tri_le", "tri_gt", "tri_ge", "tri_lt"))
        K.mul1, K.add1, K.mul2, K.add2 = (sb(n, [P, KD, 2]) for n in ("mul1", "add1", "mul2", "add2"))
        K.dt, K.dtA = sb("dt", [P, NT, 64]), sb("dtA", [P, NT, 64])
        K.decay = sb("decay", [P, 6, NT * HEADS])
        with ExitStack() as h_ctx:
            K.hT = [h_ctx.enter_context(nc.sbuf_tensor(f"hT{i}", [P, KD, T], F32R)) for i in range(2)]
            for phase in PHASES:
                run_phase(nc, K, phase)
            with ExitStack() as o:
                K.QT = o.enter_context(nc.sbuf_tensor("QT", [P, KD, T], F32))
                with ExitStack() as kv:
                    K.KT = kv.enter_context(nc.sbuf_tensor("KT", [P, NKV, T + PAST], F32))
                    K.vals = kv.enter_context(nc.sbuf_tensor("vals", [P, NT + 1, NKV * HD], F32))
                    for phase in (phase_qk, phase_attention):
                        run_phase(nc, K, phase)
                run_phase(nc, K, phase_merge)
            run_phase(nc, K, phase_ssd)
        K.so_free, K.g_free = sem("so_free"), sem("g_free")
        with ExitStack() as yc:
            K.yT = [yc.enter_context(nc.sbuf_tensor(f"yT{i}", [P, DI // P, T], F32R)) for i in range(2)]
            for phase in (phase_ssd_norm, phase_ssd_out):
                run_phase(nc, K, phase)
        K.h2T = [sb(f"h2T{i}", [P, KD, T], F32R) for i in range(2)]
        run_phase(nc, K, phase_mix_out)
        with ExitStack() as s:
            K.slotsT = s.enter_context(nc.sbuf_tensor("slotsT", [P, 3, T], F32))
            K.gate_hi = s.enter_context(nc.sbuf_tensor("gate_hi", [P, T], F32R))
            K.gate_lo = s.enter_context(nc.sbuf_tensor("gate_lo", [P, T], F32R))
            for phase in (phase_route, phase_gates):
                run_phase(nc, K, phase)
        K.y = sb("y_peer", [P, NT, D])
        for phase in (phase_experts, phase_final):
            run_phase(nc, K, phase)


def pack_units(w, cols=UC):
    k = w.shape[0] // P
    return w.reshape(k, P, w.shape[1] // cols, cols).transpose(2, 1, 0, 3).reshape(-1, P, k * cols)


def kernel(**inputs):
    import numpy as np
    import concourse.bacc as bacc
    from concourse.bass_utils import run_bass_kernel_spmd

    a = {k: np.asarray(v) for k, v in inputs.items()}
    cols = lambda v, n: np.ascontiguousarray(v.reshape(n, P).T)
    w_in = a["w_in"][0]
    z, xs, bc, cc, dtw, qkv, ga, gb = np.split(w_in, [2048, 4096, 5120, 6144, 6208, 7744, 8768], axis=1)
    tok = pack_units(np.concatenate([z, qkv], 1))
    at = pack_units(a["w_attn_out"][0])
    gbu, gau = pack_units(gb), pack_units(ga)
    merge = np.concatenate([np.stack([gbu, at], 1).reshape(8, P, 2048), gau])
    ssd = np.stack([pack_units(xs), pack_units(np.stack([bc.reshape(D, 8, P), cc.reshape(D, 8, P)], 2).reshape(D, 2048))], 1).reshape(16, P, 2048)
    wso = a["w_ssd_out"][0]
    so = np.stack([pack_units(wso[0:1024]), pack_units(wso[1024:2048])], 1).reshape(8, P, 2048)
    u = a["peer_u"][0].reshape(64, 256, 8, P).transpose(0, 3, 2, 1).reshape(64, P, 2048)
    v = a["peer_v"][0].reshape(64, 2, P, D).transpose(0, 2, 1, 3).reshape(64, P, 2048)
    exp = np.concatenate([u[0:1], np.stack([u[1:], v[:-1]], 1).reshape(126, P, 2048), v[-1:]])
    stream = np.concatenate([tok, merge, ssd, so, pack_units(a["w_o"][0]), pack_units(a["w_pq"][0]), exp])

    pos = np.arange(512)
    inv = np.float32(10000.0) ** (-np.arange(16, dtype=np.float32) / np.float32(16))
    ang = np.stack([(pos // 64).astype(np.float32)[:, None] * inv, (pos % 64).astype(np.float32)[:, None] * inv], 1)
    rope = np.stack([np.cos(ang), np.sin(ang)]).astype(np.float32).reshape(2, 4, P, 32).transpose(2, 0, 1, 3)

    arrays = {
        "x": np.concatenate([a["x_prompt"][0], a["x_sample"][0]]),
        "c_cols": np.stack([a["c_ctx"], a["c"][0]]).reshape(2, KD, P).transpose(2, 1, 0),
        "w_ada": pack_units(a["w_ada"][0]),
        "b_ada": a["b_ada"], "b_ada_cols": cols(a["b_ada"], 48),
        "norm1_cols": cols(a["norm1_w"], KD), "norm2_cols": cols(a["norm2_w"], KD),
        "w_stream": stream,
        "w_dt": pack_units(dtw, 64)[0],
        "dt_bias_f": a["dt_bias_f"], "dt_bias_b": a["dt_bias_b"], "a_log_f": a["a_log_f"], "a_log_b": a["a_log_b"],
        "rope": rope,
        "q_norm_w": a["q_norm_w"], "k_norm_w": a["k_norm_w"],
        "cache_k": a["cache_k"][0, 0].reshape(PAST, NKV * HD), "cache_v": a["cache_v"][0, 0].reshape(PAST, NKV * HD),
        "conv_w_cols": a["conv_w"][0].reshape(5, 32, P).transpose(2, 1, 0), "conv_b_cols": cols(a["conv_b"], 32),
        "d_skip": a["d_skip"],
        "state_f": a["state_ssm_fwd"][0, 0].transpose(2, 0, 1), "state_b": a["state_ssm_bwd"][0, 0].transpose(2, 0, 1),
        "ssd_norm_w": a["ssd_norm_w"],
        "keys_t": a["peer_keys"][0].reshape(16, NKEYS, P).transpose(2, 0, 1),
        "final_norm_w": a["final_norm_w"].reshape(1, D),
    }
    arrays = {k: np.ascontiguousarray(v) for k, v in arrays.items()}
    nc = bacc.Bacc("TRN2", target_bir_lowering=False, num_devices=1)
    K = Shared()
    for name, v in arrays.items():
        setattr(K, name, nc.dram_tensor("in_" + name, v.shape, F32, kind="ExternalInput").ap())
    outs = {"y": (T, D), "new_k": (P, 256), "new_v": (P, 256), "new_sf": (P, HEADS, HP), "new_sb": (P, HEADS, HP)}
    scratch = {"gates": (2, 2 * D), "z_dram": (T, DI), "qkv_dram": (T, 1536), "sga_dram": (KD, P, T), "merged_dram": (KD, P, T), "y_dram": (T, DI), "x2_dram": (T, D),
               "g_dram": (T // 64, P, P, 64)}
    for name, shape in outs.items():
        setattr(K, "out_" + name, nc.dram_tensor("out_" + name, shape, F32, kind="ExternalOutput").ap())
    for name, shape in scratch.items():
        setattr(K, name, nc.dram_tensor(name, shape, F32, kind="Internal").ap())
    build(nc, K)
    r = run_bass_kernel_spmd(nc, [{"in_" + k: v for k, v in arrays.items()}], core_ids=[0]).results[0]
    y = r["out_y"]
    state = lambda s: np.ascontiguousarray(s.transpose(1, 2, 0)).reshape(1, 1, HEADS, HP, NS)
    return (y[0:P].reshape(1, P, D), y[P:].reshape(1, 512, D), r["out_new_k"].reshape(1, 1, P, NKV, HD),
            r["out_new_v"].reshape(1, 1, P, NKV, HD), state(r["out_new_sf"]), state(r["out_new_sb"]))
```

```python
from contextlib import ExitStack

import concourse.bass as bass
from concourse import mybir

F32 = mybir.dt.float32
F32R = mybir.dt.float32r
U32 = mybir.dt.uint32
ALU = mybir.AluOpType
ACT = mybir.ActivationFunctionType
AX = mybir.AxisListType

P = 128
D = 1024
KD = D // P
T = 640
NT = T // P
TH = T // 2
EPS = 1e-6
UC = 256
HEADS, HP, NS, GROUPS = 32, 64, 128, 8
HPG = HEADS // GROUPS
DI = HEADS * HP
NH, NKV, HD = 16, 4, 64
PAST = 128
PH, TOPK, NKEYS = 8, 16, 128
SLOTS = PH * TOPK

N_TOK = 14
N_MERGE = 12
N_SSD = 16
N_SO = 8
N_O = 4
N_PQ = 8
N_EXP = 128
U_TOK = 0
U_MERGE = U_TOK + N_TOK
U_SSD = U_MERGE + N_MERGE
U_SO = U_SSD + N_SSD
U_O = U_SO + N_SO
U_PQ = U_O + N_O
U_EXP = U_PQ + N_PQ
N_UNITS = U_EXP + N_EXP


class Shared:
    pass


def group(t):
    return 0 if t == 0 else 1



class Stream:

    def __init__(self, nc, K):
        self.nc, self.K = nc, K

    def load(self, sp, n, slot):
        K = self.K
        if not (isinstance(n, int) and n < 2):
            sp.wait_ge(K.w_lo_done, n - 1)
        src = K.w_stream[bass.ds(n, 1), :, :].rearrange("o p c -> p (o c)")
        sp.dma_start(K.raw[slot][:, :], src).then_inc(K.w_loaded[slot], 16)

    def hi(self, act, n, slot, tensor_through=True):
        K = self.K
        act.wait_ge(K.w_loaded[slot], (n - slot + 2) * 8)
        if tensor_through:
            act.wait_ge(K.hilo_free, n + 1)
        self.nc.scalar.activation(K.whi[slot][:, :], K.raw[slot][:, :], ACT.Copy).then_inc(K.w_hi_done, 1)

    def lo(self, dve, n, slot):
        K = self.K
        dve.wait_ge(K.w_hi_done, n + 1)
        self.nc.vector.tensor_tensor(K.wlo[slot][:, :], K.raw[slot][:, :], K.whi[slot][:, :].bitcast(F32),
                                     ALU.subtract).then_inc(K.w_lo_done, 1)

    def ready(self, pe, n):
        pe.wait_ge(self.K.w_lo_done, n + 1)


def mm3(nc, out, lhs, rhs, first, last):
    (lh, ll), (rh, rl) = lhs, rhs
    nc.tensor.matmul(out, lh, rh, start=first, stop=False)
    nc.tensor.matmul(out, lh, rl, start=False, stop=False)
    return nc.tensor.matmul(out, ll, rh, start=False, stop=last)



def phase_modulate(nc, K, ctx):
    S = Stream(nc, K)
    sem = K.phase_semaphores(ctx)
    sb = lambda n, s, d=F32: ctx.enter_context(nc.sbuf_tensor(n, s, d))
    ada = [K.raw[0], K.raw[1]]
    cT = sb("cT", [P, KD, 2])
    xt = sb("xt", [P, NT, D])
    xn = sb("xn", [P, 2, D])
    hf = sb("hf", [P, 2, KD, P])
    sq = sb("sq", [P, D])
    ssq = sb("ssq", [P, NT])
    rstd = sb("rstd", [P, NT])
    b_col = sb("b_col", [P, 48])
    n1 = sb("n1", [P, KD])
    modc = sb("modc", [P, 48, 2])
    ps_mod = ctx.enter_context(nc.psum_tensor("ps_mod", [P, 48, 2], F32))
    ps_x = [ctx.enter_context(nc.psum_tensor(f"ps_x{i}", [P, 4, P], F32)) for i in range(2)]

    small = sem("m_small"); c_in = sem("m_c_in"); x_in = sem("m_x_in")
    ada_in = [sem("m_ada_in0"), sem("m_ada_in1")]; ada_used = sem("m_ada_used")
    silu_done = sem("m_silu"); ident_done = sem("m_ident"); iota_done = sem("m_iota"); zeroed = sem("m_zeroed")
    sq_done = sem("m_sq"); ms_done = sem("m_ms"); rt_done = sem("m_rt"); rstd_done = sem("m_rstd")
    xn_done = sem("m_xn"); xT_done = sem("m_xT"); hf_done = sem("m_hf"); hhi_done = sem("m_hhi"); hlo_done = sem("m_hlo")
    modc_done = sem("m_modc"); scale_done = sem("m_scale")

    with nc.Block() as block:
        def split(dve, t):
            dve.wait_ge(hf_done, KD * (t + 1))
            nc.vector.tensor_copy(K.hT[0][:, :, t * P:(t + 1) * P], hf[:, t % 2, :, :]).then_inc(hhi_done, 1)
            dve.wait_ge(hhi_done, t + 1)
            nc.vector.tensor_tensor(K.hT[1][:, :, t * P:(t + 1) * P], hf[:, t % 2, :, :],
                                    K.hT[0][:, :, t * P:(t + 1) * P].bitcast(F32), ALU.subtract).then_inc(hlo_done, 1)

        @block.sync
        def _(sp):
            sp.dma_start(cT[:, :, :], K.c_cols).then_inc(c_in, 16)
            for u in range(2):
                sp.dma_start(ada[u][:, :], K.w_ada[u]).then_inc(ada_in[u], 16)
            sp.dma_start(xt[:, :, :], K.x.rearrange("(t p) d -> p t d", p=P)).then_inc(x_in, 16)
            with sp.Fori(1, 4) as i:
                for s in range(2):
                    sp.wait_ge(ada_used, 2 * i + s - 1)
                    sp.dma_start(ada[s][:, :], K.w_ada[bass.ds(2 * i + s, 1), :, :].rearrange("o p c -> p (o c)")).then_inc(ada_in[s], 16)
            sp.wait_ge(ada_used, 8)
            S.load(sp, 0, 0)
            S.load(sp, 1, 1)
            S.load(sp, 2, 0)

        @block.gpsimd
        def _(pool):
            nc.gpsimd.memset(K.ident[:, :], 0.0).then_inc(zeroed, 1)
            nc.gpsimd.memset(K.ones[:, :], 1.0).then_inc(zeroed, 1)
            pool.wait_ge(zeroed, 2)
            nc.gpsimd.affine_select(out=K.ident[:, :], in_=K.ident[:, :], compare_op=ALU.not_equal, fill=1.0, base=0,
                                    pattern=[[-1, P]], channel_multiplier=1).then_inc(ident_done, 1)
            nc.gpsimd.affine_select(out=K.tri_le[:, :], in_=K.ones[:, :], compare_op=ALU.is_ge, fill=0.0, base=0,
                                    pattern=[[1, P]], channel_multiplier=-1).then_inc(iota_done, 1)
            nc.gpsimd.affine_select(out=K.tri_gt[:, :], in_=K.ones[:, :], compare_op=ALU.is_gt, fill=0.0, base=0,
                                    pattern=[[-1, P]], channel_multiplier=1).then_inc(iota_done, 1)
            nc.gpsimd.affine_select(out=K.tri_ge[:, :], in_=K.ones[:, :], compare_op=ALU.is_ge, fill=0.0, base=0,
                                    pattern=[[-1, P]], channel_multiplier=1).then_inc(iota_done, 1)
            nc.gpsimd.affine_select(out=K.tri_lt[:, :], in_=K.ones[:, :], compare_op=ALU.is_gt, fill=0.0, base=0,
                                    pattern=[[1, P]], channel_multiplier=-1).then_inc(iota_done, 1)
            nc.gpsimd.iota(K.iota[:, :], pattern=[[1, P]], base=0, channel_multiplier=0,
                           allow_small_or_imprecise_dtypes=True).then_inc(iota_done, 1)

        @block.scalar
        def _(act):
            act.dma_start(b_col[:, :], K.b_ada_cols).then_inc(small, 16)
            act.dma_start(n1[:, :], K.norm1_cols).then_inc(small, 16)
            act.wait_ge(c_in, 16)
            nc.scalar.activation(K.silu_c[:, :, :], cT[:, :, :], ACT.Silu).then_inc(silu_done, 1)
            act.wait_ge(x_in, 16)
            for t in range(NT):
                if t:
                    act.wait_ge(sq_done, t)
                nc.scalar.activation(sq[:, :], xt[:, t, :], ACT.Square, accum_out=ssq[:, t:t + 1]).then_inc(sq_done, 1)
            act.wait_ge(ms_done, 1)
            nc.scalar.activation(rstd[:, :], ssq[:, :], ACT.Sqrt).then_inc(rt_done, 1)
            act.wait_ge(scale_done, 4)
            for t in range(NT):
                for h in range(2):
                    act.wait_ge(xT_done, 2 * t + h + 1)
                    if t >= 2 and h == 0:
                        act.wait_ge(hlo_done, t - 1)
                    for k in range(4):
                        kd = 4 * h + k
                        nc.scalar.activation(hf[:, t % 2, kd, :], ps_x[h][:, k, :], ACT.Identity,
                                             scale=K.mul1[:, kd, group(t):group(t) + 1],
                                             bias=K.add1[:, kd, group(t):group(t) + 1]).then_inc(hf_done, 1)
            S.hi(act, 0, 0)

        @block.vector
        def _(dve):
            dve.wait_ge(sq_done, NT)
            nc.vector.tensor_scalar(ssq[:, :], ssq[:, :], 1.0 / D, EPS, ALU.mult, ALU.add).then_inc(ms_done, 1)
            dve.wait_ge(rt_done, 1)
            nc.vector.reciprocal(rstd[:, :], rstd[:, :]).then_inc(rstd_done, 1)
            dve.wait_ge(rstd_done, 1)
            for t in range(NT):
                if t >= 2:
                    dve.wait_ge(xT_done, 2 * t - 2)
                nc.vector.tensor_scalar(xn[:, t % 2, :], xt[:, t, :], rstd[:, t:t + 1], None, ALU.mult).then_inc(xn_done, 1)
                if t == 1:
                    dve.wait_ge(small, 32)
                    dve.wait_ge(ada_used, 8)
                    nc.vector.tensor_tensor(modc[:, 0:16, :], ps_mod[:, 0:16, :],
                                            b_col[:, 0:16].unsqueeze(2).to_broadcast([P, 16, 2]), ALU.add).then_inc(modc_done, 1)
                    dve.wait_ge(modc_done, 1)
                    nc.vector.tensor_copy(K.add1[:, :, :], modc[:, 0:8, :]).then_inc(scale_done, 1)
                    nc.vector.tensor_scalar(K.mul1[:, :, :], modc[:, 8:16, :], 1.0, None, ALU.add).then_inc(scale_done, 1)
                    dve.wait_ge(scale_done, 2)
                    for g in range(2):
                        nc.vector.tensor_tensor(K.mul1[:, :, g], K.mul1[:, :, g], n1[:, :], ALU.mult).then_inc(scale_done, 1)
                if t >= 1:
                    split(dve, t - 1)
            split(dve, NT - 1)
            S.lo(dve, 0, 0)

        @block.tensor
        def _(pe):
            pe.sem_inc(K.hilo_free, 2)
            pe.wait_ge(silu_done, 1)
            with pe.Fori(0, 4) as i:
                for s in range(2):
                    pe.wait_ge(ada_in[s], 16 * i + 16)
                    w = ada[s][:, :].rearrange("p (k c) -> p k c", k=KD)
                    for m in range(2):
                        for k in range(KD):
                            mm = nc.tensor.matmul(ps_mod[:, bass.ds(4 * i + (2 * s + m), 1), :].rearrange("p o c -> p (o c)"),
                                                  w[:, k, m * P:(m + 1) * P], K.silu_c[:, k, :], start=(k == 0), stop=(k == KD - 1))
                    mm.then_inc(ada_used, 1)
            pe.wait_ge(ident_done, 1)
            for t in range(NT):
                pe.wait_ge(xn_done, t + 1)
                for h in range(2):
                    if t:
                        pe.wait_ge(hf_done, KD * (t - 1) + 4 * (h + 1))
                    for k in range(4):
                        kd = 4 * h + k
                        mm = nc.tensor.transpose(ps_x[h][:, k, :], xn[:, t % 2, kd * P:(kd + 1) * P], K.ident[:, :])
                    mm.then_inc(xT_done, 1)


def project_features(nc, pe, w, act, out):
    wh, wl = (x[:, :].rearrange("p (k c) -> p k c", k=KD) for x in w)
    ah, al = act
    for m in range(2):
        for k in range(KD):
            cols = slice(m * P, (m + 1) * P)
            for lhs, rhs, first, last in ((wh, ah, k == 0, False), (wh, al, False, False), (wl, ah, False, k == KD - 1)):
                for h in range(2):
                    mm = nc.tensor.matmul(out[2 * m + h], lhs[:, k, cols], rhs[:, k, h * TH:(h + 1) * TH],
                                          start=first, stop=last)
    return mm



def phase_tokens(nc, K, ctx):
    S = Stream(nc, K)
    sem = K.phase_semaphores(ctx)
    sb = lambda n, s, d=F32: ctx.enter_context(nc.sbuf_tensor(n, s, d))
    ob = [sb(f"t_ob{t}", [P, 2 * UC]) for t in range(NT)]
    ps = [ctx.enter_context(nc.psum_tensor(f"t_ps{t}", [P, 2 * UC], F32)) for t in range(NT)]
    ps_dt = ctx.enter_context(nc.psum_tensor("t_psdt", [P, NT, 64], F32))
    ps_cum = [ctx.enter_context(nc.psum_tensor(f"t_cum{i}", [P, 3, NT * HEADS], F32)) for i in range(2)]
    dtw = sb("dtw", [P, KD * 64])
    dtwh, dtwl = sb("dtwh", [P, KD, 64], F32R), sb("dtwl", [P, KD, 64], F32R)
    bias = sb("dt_bias", [P, 64])
    xdt = sb("xdt", [P, NT, 64]); ax = sb("ax", [P, NT, 64]); ex = sb("ex", [P, NT, 64])
    sr = sb("sr", [P, NT, 64]); s2 = sb("s2", [P, NT, 64]); pl = sb("pl", [P, NT, 64])
    nega = sb("nega", [P, 64])

    dtw_in = sem("t_dtw_in"); par_in = sem("t_par_in"); dtw_hi = sem("t_dtw_hi"); dtw_lo = sem("t_dtw_lo")
    mm_done = sem("t_mm"); ev_done = sem("t_ev"); out_done = [K.pool_dma(t) for t in range(NT)]
    dt_mm = sem("t_dt_mm"); chain = sem("t_chain"); ex_done = sem("t_ex"); ax_done = sem("t_ax")
    na_done = sem("t_na"); dtA_done = sem("t_dtA"); cum_mm = sem("t_cum_mm"); cum_exp = sem("t_cum_exp")

    with nc.Block() as block:
        def one_pair(act, i, func):
            for t in range(NT):
                tile_out(act, i, t, func)
                if t == 0:
                    S.hi(act, 2 * i + 2, 0)
                if t == 2:
                    S.hi(act, 2 * i + 3, 1)

        def tile_out(act, i, t, func):
            act.wait_ge(mm_done, NT * i + (t + 1))
            if not isinstance(i, int):
                act.wait_ge(out_done[t], i * 16)
            nc.scalar.activation(ob[t][:, :], ps[t][:, :], func).then_inc(ev_done, 1)

        @block.sync
        def _(sp):
            sp.dma_start(dtw[:, :], K.w_dt).then_inc(dtw_in, 16)
            sp.dma_start(bias[:, 0:32], K.dt_bias_f.partition_broadcast(P).rearrange("p o h -> p (o h)")).then_inc(par_in, 16)
            sp.dma_start(bias[:, 32:64], K.dt_bias_b.partition_broadcast(P).rearrange("p o h -> p (o h)")).then_inc(par_in, 16)
            sp.dma_start(nega[:, 0:32], K.a_log_f.partition_broadcast(P).rearrange("p o h -> p (o h)")).then_inc(par_in, 16)
            sp.dma_start(nega[:, 32:64], K.a_log_b.partition_broadcast(P).rearrange("p o h -> p (o h)")).then_inc(par_in, 16)
            with sp.Fori(0, N_TOK // 2) as i:
                for s in range(2):
                    S.load(sp, 2 * i + (U_TOK + s + 3), (s + 1) % 2)

        @block.gpsimd
        def _(pool):
            with pool.Fori(0, 4) as i:
                for t in range(NT):
                    pool.wait_ge(ev_done, i * NT + (t + 1))
                    pool.dma_start(K.z_dram[t * P:(t + 1) * P, bass.ds(i * 512, 512)], ob[t][:, :]).then_inc(out_done[t], 16)
            with pool.Fori(0, 3) as i:
                for t in range(NT):
                    pool.wait_ge(ev_done, i * NT + (4 * NT + t + 1))
                    pool.dma_start(K.qkv_dram[t * P:(t + 1) * P, bass.ds(i * 512, 512)], ob[t][:, :]).then_inc(out_done[t], 16)
            for t in range(NT):
                pool.wait_ge(out_done[t], 7 * 16)

        @block.scalar
        def _(act):
            act.wait_ge(dtw_in, 16)
            nc.scalar.activation(dtwh[:, :, :], dtw[:, :].rearrange("p (k c) -> p k c", k=KD), ACT.Copy).then_inc(dtw_hi, 1)
            S.hi(act, 1, 1)
            act.wait_ge(par_in, 64)
            nc.scalar.activation(nega[:, :], nega[:, :], ACT.Exp).then_inc(na_done, 1)
            act.wait_ge(ax_done, 1)
            nc.scalar.activation(ex[:, :, :], ax[:, :, :], ACT.Exp, scale=-1.0).then_inc(ex_done, 1)
            for t in range(NT):
                tile_out(act, 0, t, ACT.Silu)
                if t == 0:
                    S.hi(act, 2, 0)
                if t == 2:
                    S.hi(act, 3, 1)
            act.wait_ge(cum_mm, 2)
            for j in range(2):
                nc.scalar.activation(K.decay[:, 3 * j:3 * j + 3, :], ps_cum[j][:, :, :], ACT.Exp).then_inc(cum_exp, 1)
            with act.Fori(1, 4) as i:
                one_pair(act, i, ACT.Silu)
            with act.Fori(4, 7) as i:
                one_pair(act, i, ACT.Copy)

        @block.vector
        def _(dve):
            dve.wait_ge(dtw_hi, 1)
            nc.vector.tensor_tensor(dtwl[:, :, :], dtw[:, :].rearrange("p (k c) -> p k c", k=KD),
                                    dtwh[:, :, :].bitcast(F32), ALU.subtract).then_inc(dtw_lo, 1)
            S.lo(dve, 1, 1)
            dve.wait_ge(par_in, 64)
            dve.wait_ge(dt_mm, 1)
            k = [0]

            def link(ins):
                k[0] += 1
                ins.then_inc(chain, 1)
                dve.wait_ge(chain, k[0])

            b3 = bias[:, :].unsqueeze(1).to_broadcast([P, NT, 64])
            link(nc.vector.tensor_tensor(xdt[:, :, :], ps_dt[:, :, :], b3, ALU.add))
            nc.vector.scalar_tensor_tensor(ax[:, :, :], xdt[:, :, :], -1.0, xdt[:, :, :], ALU.mult, ALU.max).then_inc(ax_done, 1)
            dve.wait_ge(ex_done, 1)
            link(nc.vector.tensor_scalar(s2[:, :, :], ex[:, :, :], 2.0, None, ALU.add))
            link(nc.vector.reciprocal(pl[:, :, :], s2[:, :, :]))
            link(nc.vector.tensor_tensor(sr[:, :, :], ex[:, :, :], pl[:, :, :], ALU.mult))
            link(nc.vector.tensor_tensor(s2[:, :, :], sr[:, :, :], sr[:, :, :], ALU.mult))
            link(nc.vector.tensor_scalar(pl[:, :, :], s2[:, :, :], 2.0 / 17, None, ALU.mult))
            for c in (15, 13, 11, 9, 7, 5, 3):
                link(nc.vector.scalar_tensor_tensor(pl[:, :, :], pl[:, :, :], 2.0 / c, s2[:, :, :], ALU.add, ALU.mult))
            link(nc.vector.scalar_tensor_tensor(pl[:, :, :], pl[:, :, :], 2.0, sr[:, :, :], ALU.add, ALU.mult))
            link(nc.vector.scalar_tensor_tensor(K.dt[:, :, :], xdt[:, :, :], 0.0, pl[:, :, :], ALU.max, ALU.add))
            dve.wait_ge(na_done, 1)
            link(nc.vector.tensor_scalar(nega[:, :], nega[:, :], -1.0, None, ALU.mult))
            nc.vector.tensor_tensor(K.dtA[:, :, :], K.dt[:, :, :], nega[:, :].unsqueeze(1).to_broadcast([P, NT, 64]),
                                    ALU.mult).then_inc(dtA_done, 1)
            S.lo(dve, 2, 0)
            S.lo(dve, 3, 1)
            dve.wait_ge(cum_exp, 2)
            for row, d in ((1, 0), (4, 1)):
                v = K.decay[:, row, :].rearrange("p (c h) -> p c h", c=NT)
                link(nc.vector.tensor_tensor(v, v, K.dt[:, :, d * 32:(d + 1) * 32], ALU.mult))
            with dve.Fori(1, 7) as i:
                S.lo(dve, 2 * i + 2, 0)
                S.lo(dve, 2 * i + 3, 1)

        @block.tensor
        def _(pe):
            def unit(n, i, s):
                S.ready(pe, n)
                wh, wl = (x[s][:, :].rearrange("p (k c) -> p k c", k=KD) for x in (K.whi, K.wlo))
                for t in range(NT):
                    if s == 0 and not isinstance(i, int):
                        pe.wait_ge(ev_done, NT * i + (t - NT + 1))
                    tc = slice(t * P, (t + 1) * P)
                    for k in range(KD):
                        mm = mm3(nc, ps[t][:, s * UC:(s + 1) * UC], (K.hT[0][:, k, tc], K.hT[1][:, k, tc]),
                                 (wh[:, k, :], wl[:, k, :]), k == 0, k == KD - 1)
                    if s == 1:
                        mm.then_inc(mm_done, 1)
                pe.drain().then_inc(K.hilo_free, 1)

            pe.wait_ge(dtw_lo, 1)
            for t in range(NT):
                tc = slice(t * P, (t + 1) * P)
                for k in range(KD):
                    mm = mm3(nc, ps_dt[:, t, :], (K.hT[0][:, k, tc], K.hT[1][:, k, tc]),
                             (dtwh[:, k, :], dtwl[:, k, :]), k == 0, k == KD - 1)
            mm.then_inc(dt_mm, 1)
            unit(0, 0, 0)
            unit(1, 0, 1)
            pe.wait_ge(dtA_done, 1)
            for j, tris in enumerate(((K.tri_le, K.tri_gt, K.ones), (K.tri_ge, K.tri_lt, K.ones))):
                for r, tri in enumerate(tris):
                    mm = nc.tensor.matmul(ps_cum[j][:, r, :], tri[:, :], K.dtA[:, :, j * 32:(j + 1) * 32],
                                          start=True, stop=True)
                mm.then_inc(cum_mm, 1)
            with pe.Fori(1, 7) as i:
                unit(2 * i, i, 0)
                unit(2 * i + 1, i, 1)



def phase_qk(nc, K, ctx):
    sem = K.phase_semaphores(ctx)
    sb = lambda n, s, d=F32: ctx.enter_context(nc.sbuf_tensor(n, s, d))
    NQ, NK = NH * HD, NKV * HD
    NHK = NH + NKV
    st = [sb(f"q_st{i}", [P, NQ + NK]) for i in range(2)]
    sq = sb("q_sq", [P, NQ + NK])
    qn = sb("q_n", [P, NQ + NK])
    qr = [sb(f"q_r{i}", [P, NQ]) for i in range(2)]
    kd = [sb(f"k_d{i}", [P, NKV, 2, HD]) for i in range(2)]
    ck = sb("q_ck", [P, NK])
    ss = sb("q_ss", [P, NHK]); wq = sb("q_w", [P, HD]); wk = sb("k_w", [P, HD])
    cs = sb("q_cs", [P, 2, 4, 32])
    t1 = sb("q_t1", [P, NHK, 2, 16]); t2 = sb("q_t2", [P, NHK, 2, 16])
    ps = ctx.enter_context(nc.psum_tensor("q_ps", [P, 12, P], F32))
    ADA0, ADA_N = 8, 24
    ada = [sb(f"q_ada{i}", [P, KD, UC]) for i in range(2)]
    b_col = sb("q_bcol", [P, 48]); n2 = sb("q_n2", [P, KD]); modc = sb("q_modc", [P, 16, 2])
    b_row = sb("q_brow", [2, 2 * D])
    ps_mod = ctx.enter_context(nc.psum_tensor("q_pmod", [P, 16, 2], F32))
    ps_gate = ctx.enter_context(nc.psum_tensor("q_pgate", [2, 2 * D], F32))
    st_in = [K.pool_dma(NT + i) for i in range(2)]
    par_in = sem("q_par_in"); ck_in = sem("q_ck_in"); v_in = K.pool_dma(NT + 2)
    chain = sem("q_chain"); ms_done = sem("q_ms"); rt_done = sem("q_rt"); st_read = sem("q_st_read")
    k0_done = sem("q_k0"); src_done = sem("q_src"); tr_done = sem("q_tr"); ev_done = sem("q_ev"); outs = K.pool_dma(NT + 3)
    ada_in = [sem("q_ada_in0"), sem("q_ada_in1")]
    ada_used = sem("q_ada_used"); small = sem("q_small"); modc_done = sem("q_modc_done"); scale_done = sem("q_scale")
    grow_done = sem("q_grow_done"); g_out = sem("q_g_out")
    bc = lambda ap: ap.partition_broadcast(P).rearrange("p o h -> p (o h)")

    with nc.Block() as block:
        @block.sync
        def _(sp):
            sp.dma_start(wq[:, :], bc(K.q_norm_w)).then_inc(par_in, 16)
            sp.dma_start(wk[:, :], bc(K.k_norm_w)).then_inc(par_in, 16)
            sp.dma_start(cs[:, :, :, :], K.rope).then_inc(par_in, 16)
            sp.dma_start(ck[:, :], K.cache_k).then_inc(ck_in, 16)
            sp.dma_start(b_col[:, :], K.b_ada_cols).then_inc(small, 16)
            sp.dma_start(n2[:, :], K.norm2_cols).then_inc(small, 16)
            sp.dma_start(b_row[:, 0:D], K.b_ada[:, 2 * D:3 * D].partition_broadcast(2).rearrange("a o d -> a (o d)")).then_inc(small, 16)
            sp.dma_start(b_row[:, D:2 * D], K.b_ada[:, 5 * D:6 * D].partition_broadcast(2).rearrange("a o d -> a (o d)")).then_inc(small, 16)
            for u in range(ADA0, ADA_N):
                if u >= ADA0 + 2:
                    sp.wait_ge(ada_used, u - ADA0 - 1)
                sp.dma_start(ada[u % 2][:, :, :].rearrange("p k c -> p (k c)"), K.w_ada[u]).then_inc(ada_in[u % 2], 16)
            sp.wait_ge(grow_done, 1)
            sp.dma_start(K.gates, b_row[:, :]).then_inc(g_out, 16)
            sp.wait_ge(g_out, 16)

        @block.gpsimd
        def _(pool):
            def tile_in(t):
                pool.dma_start(st[t % 2][:, :], K.qkv_dram[t * P:(t + 1) * P, 0:NQ + NK]).then_inc(st_in[t % 2], 16)

            tile_in(0)
            tile_in(1)
            pool.dma_start(K.vals[:, 0:NT, :], K.qkv_dram[:, NQ + NK:].rearrange("(t p) c -> p t c", p=P)).then_inc(v_in, 16)
            pool.dma_start(K.vals[:, NT, :], K.cache_v).then_inc(v_in, 16)
            pool.dma_start(K.out_new_v, K.qkv_dram[0:P, NQ + NK:]).then_inc(outs, 16)
            pool.wait_ge(k0_done, 1)
            pool.dma_start(K.out_new_k, qn[:, NQ:]).then_inc(outs, 16)
            for t in range(2, NT):
                pool.wait_ge(st_read, t - 1)
                tile_in(t)
            pool.wait_ge(outs, 32)
            pool.wait_ge(v_in, 32)

        @block.vector
        def _(dve):
            k = [0]

            def link(ins):
                k[0] += 1
                ins.then_inc(chain, 1)
                dve.wait_ge(chain, k[0])

            heads = lambda ap: ap.rearrange("p (h d) -> p h d", d=HD)
            row = lambda w, n: w[:, :].unsqueeze(1).to_broadcast([P, n, HD])
            for t in range(NT):
                s = t % 2
                x = st[s]
                dve.wait_ge(st_in[s], (t // 2 + 1) * 16)
                link(nc.vector.tensor_tensor(sq[:, :], x[:, :], x[:, :], ALU.mult))
                link(nc.vector.tensor_reduce(ss[:, :], heads(sq[:, :]), axis=AX.X, op=ALU.add))
                nc.vector.tensor_scalar(ss[:, :], ss[:, :], 1.0 / HD, EPS, ALU.mult, ALU.add).then_inc(ms_done, 1)
                dve.wait_ge(rt_done, t + 1)
                link(nc.vector.reciprocal(ss[:, :], ss[:, :]))
                if t == 1:
                    dve.wait_ge(outs, 32)
                nc.vector.tensor_tensor(heads(qn[:, :]), heads(x[:, :]), ss[:, :].unsqueeze(2).to_broadcast([P, NHK, HD]),
                                        ALU.mult).then_inc(st_read, 1)
                dve.wait_ge(st_read, t + 1)
                if t == 0:
                    dve.wait_ge(par_in, 48)
                link(nc.vector.tensor_tensor(heads(qn[:, 0:NQ]), heads(qn[:, 0:NQ]), row(wq, NH), ALU.mult))
                ins = nc.vector.tensor_tensor(heads(qn[:, NQ:]), heads(qn[:, NQ:]), row(wk, NKV), ALU.mult)
                if t == 0:
                    ins.then_inc(k0_done, 1)
                    dve.wait_ge(k0_done, 1)
                    link(nc.vector.tensor_copy(qr[0][:, :], qn[:, 0:NQ]))
                    for c in range(2):
                        nc.vector.tensor_copy(kd[0][:, :, c, :], heads(qn[:, NQ:])).then_inc(src_done, 1)
                else:
                    link(ins)
                    if t >= 2:
                        dve.wait_ge(tr_done, t - 1)
                    axes = qn[:, :].rearrange("p (h a f d) -> p h a f d", h=NHK, a=2, f=2)
                    a, b = axes[:, :, :, 0, :], axes[:, :, :, 1, :]
                    cos, sin = (cs[:, j, t - 1, :].rearrange("p (a d) -> p a d", a=2).unsqueeze(1).to_broadcast([P, NHK, 2, 16])
                                for j in range(2))
                    qo = qr[s][:, :].rearrange("p (h a f d) -> p h a f d", h=NH, a=2, f=2)
                    for f, (c1, c2, op) in enumerate(((cos, sin, ALU.subtract), (sin, cos, ALU.add))):
                        link(nc.vector.tensor_tensor(t1[:, :, :, :], a, c1, ALU.mult))
                        link(nc.vector.tensor_tensor(t2[:, :, :, :], b, c2, ALU.mult))
                        link(nc.vector.tensor_tensor(qo[:, :, :, f, :], t1[:, 0:NH], t2[:, 0:NH], op))
                        for c in range(2):
                            ko = kd[s][:, :, c, :].rearrange("p h (a f d) -> p h a f d", a=2, f=2)
                            link(nc.vector.tensor_tensor(ko[:, :, :, f, :], t1[:, NH:], t2[:, NH:], op))
                    nc.vector.tensor_copy(ss[:, 0:1], ss[:, 0:1]).then_inc(src_done, 2)
            dve.wait_ge(ck_in, 16)
            dve.wait_ge(tr_done, NT - 1)
            for c in range(2):
                nc.vector.tensor_copy(kd[1][:, :, c, :], heads(ck[:, :])).then_inc(src_done, 1)
            dve.wait_ge(small, 64)
            dve.wait_ge(ada_used, ADA_N - ADA0)
            nc.vector.tensor_tensor(modc[:, :, :], ps_mod[:, :, :],
                                    b_col[:, 24:40].unsqueeze(2).to_broadcast([P, 16, 2]), ALU.add).then_inc(modc_done, 1)
            nc.vector.tensor_tensor(b_row[:, :], ps_gate[:, :], b_row[:, :], ALU.add).then_inc(grow_done, 1)
            dve.wait_ge(modc_done, 1)
            nc.vector.tensor_copy(K.add2[:, :, :], modc[:, 0:8, :]).then_inc(scale_done, 1)
            nc.vector.tensor_scalar(K.mul2[:, :, :], modc[:, 8:16, :], 1.0, None, ALU.add).then_inc(scale_done, 1)
            dve.wait_ge(scale_done, 2)
            for g in range(2):
                nc.vector.tensor_tensor(K.mul2[:, :, g], K.mul2[:, :, g], n2[:, :], ALU.mult).then_inc(scale_done, 1)

        @block.scalar
        def _(act):
            def evacuate(t):
                act.wait_ge(tr_done, t + 1)
                cols = slice(t * P, (t + 1) * P)
                if t < NT:
                    nc.scalar.activation(K.QT[:, :, cols], ps[:, 0:8, :], ACT.Copy).then_inc(ev_done, 1)
                nc.scalar.activation(K.KT[:, :, cols], ps[:, 8:12, :], ACT.Copy).then_inc(ev_done, 1)

            for t in range(NT):
                act.wait_ge(ms_done, t + 1)
                nc.scalar.activation(ss[:, :], ss[:, :], ACT.Sqrt).then_inc(rt_done, 1)
                if t:
                    evacuate(t - 1)
            evacuate(NT - 1)
            evacuate(NT)

        @block.tensor
        def _(pe):
            def modulation(u):
                part, col = u // 4, u % 4 * UC
                pe.wait_ge(ada_in[u % 2], 16 * ((u - ADA0) // 2 + 1))
                if part in (2, 5):
                    col += 0 if part == 2 else D
                    for k in range(KD):
                        mm = nc.tensor.matmul(ps_gate[:, col:col + UC], K.silu_c[:, k, :], ada[u % 2][:, k, :],
                                              start=(k == 0), stop=(k == KD - 1))
                else:
                    for m in range(2):
                        for k in range(KD):
                            mm = nc.tensor.matmul(ps_mod[:, 2 * (u - 12) + m, :], ada[u % 2][:, k, m * P:(m + 1) * P], K.silu_c[:, k, :],
                                                  start=(k == 0), stop=(k == KD - 1))
                mm.then_inc(ada_used, 1)

            todo = list(range(ADA0, ADA_N))
            for t in range(NT + 1):
                for u in todo[:3]:
                    modulation(u)
                todo = todo[3:]
                s = t % 2
                pe.wait_ge(src_done, 2 * (t + 1))
                if t:
                    pe.wait_ge(ev_done, 2 * t)
                if t < NT:
                    for i in range(8):
                        nc.tensor.transpose(ps[:, i, :], qr[s][:, i * P:(i + 1) * P], K.ident[:, :])
                for i in range(NKV):
                    mm = nc.tensor.transpose(ps[:, 8 + i, :], kd[s][:, i, :, :].rearrange("p c d -> p (c d)"), K.ident[:, :])
                mm.then_inc(tr_done, 1)
            for u in todo:
                modulation(u)



def phase_attention(nc, K, ctx):
    sem = K.phase_semaphores(ctx)
    sb = lambda n, s, d=F32: ctx.enter_context(nc.sbuf_tensor(n, s, d))
    SCALE = float(HD) ** -0.5
    STEPS = [(h, qt) for h in range(NH) for qt in range(NT)]
    J = len(STEPS)
    KW = TH
    prob = [sb(f"a_p{i}", [P, 2 * KW]) for i in range(3)]
    PT = [sb(f"a_pT{i}", [P, NT, T]) for i in range(2)]
    nb = sb("a_nb", [P, J]); nmax = sb("a_nmax", [P, J]); sm = sb("a_sum", [P, J]); rc = sb("a_rc", [P, J])
    ps_s = [ctx.enter_context(nc.psum_tensor(f"a_ps{i}", [P, 2, 512], F32)) for i in range(2)]
    ps_t = ctx.enter_context(nc.psum_tensor("a_pst", [P, 8, P], F32))
    ps_o = ctx.enter_context(nc.psum_tensor("a_pso", [P, 2, 512], F32))
    sc_done = sem("a_sc"); mx_done = sem("a_mx"); nb_done = sem("a_nb"); exp_done = sem("a_exp"); rc_done = sem("a_rc")
    pn_done = sem("a_pn"); pT_done = sem("a_pT"); ptev = sem("a_ptev"); pv_done = sem("a_pv"); oev = sem("a_oev")

    def scores(j):
        return ps_s[j % 2][:, :, 0:KW] if STEPS[j][1] else ps_s[j % 2][:, 0, 0:P]

    def probs(j):
        return prob[j % 3][:, :].rearrange("p (a c) -> p a c", a=2) if STEPS[j][1] else prob[j % 3][:, 0:P]

    with nc.Block() as block:
        @block.tensor
        def _(pe):
            def qk(j):
                h, qt = STEPS[j]
                rows = slice(64 * (h % 2), 64 * (h % 2) + 64)
                if j >= 2:
                    pe.wait_ge(exp_done, j - 1)
                q = K.QT[rows, h // 2, qt * P:(qt + 1) * P]
                if qt == 0:
                    mm = nc.tensor.matmul(ps_s[j % 2][:, 0, 0:P], q, K.KT[rows, h // 4, 0:P], start=True, stop=True)
                else:
                    for a in range(2):
                        mm = nc.tensor.matmul(ps_s[j % 2][:, a, 0:KW], q, K.KT[rows, h // 4, P + a * KW:P + (a + 1) * KW],
                                              start=True, stop=True)
                mm.then_inc(sc_done, 1)

            def transposes(j):
                pe.wait_ge(pn_done, j + 1)
                if j:
                    pe.wait_ge(ptev, j)
                for kt in range(NT if STEPS[j][1] else 1):
                    mm = nc.tensor.transpose(ps_t[:, kt, :], prob[j % 3][:, kt * P:(kt + 1) * P], K.ident[:, :])
                mm.then_inc(pT_done, 1)

            def pv(h):
                rows = slice(64 * (h % 2), 64 * (h % 2) + 64)
                kv = slice((h // 4) * HD, (h // 4 + 1) * HD)
                pe.wait_ge(ptev, NT * (h + 1))
                if h:
                    pe.wait_ge(oev, 2 * h)
                nc.tensor.matmul(ps_o[rows, 0, 0:P], K.vals[:, 0, kv], PT[h % 2][:, 0, 0:P], start=True, stop=True)
                for kt in range(NT):
                    mm = nc.tensor.matmul(ps_o[rows, 1, 0:4 * P], K.vals[:, kt + 1, kv], PT[h % 2][:, kt, P:T],
                                          start=(kt == 0), stop=(kt == NT - 1))
                mm.then_inc(pv_done, 1)

            for j in range(J + 2):
                if j < J:
                    qk(j)
                if j >= 2:
                    transposes(j - 2)
                    if STEPS[j - 2][1] == NT - 1:
                        pv(STEPS[j - 2][0])

        @block.vector
        def _(dve):
            def normalise(j):
                dve.wait_ge(exp_done, j + 1)
                nc.vector.reciprocal(rc[:, j:j + 1], sm[:, j:j + 1]).then_inc(rc_done, 1)
                dve.wait_ge(rc_done, j + 1)
                nc.vector.tensor_scalar(probs(j), probs(j), rc[:, j:j + 1], None, ALU.mult).then_inc(pn_done, 1)

            def output(h):
                rows = slice(64 * (h % 2), 64 * (h % 2) + 64)
                dve.wait_ge(pv_done, h + 1)
                nc.vector.tensor_copy(K.QT[rows, h // 2, 0:P], ps_o[rows, 0, 0:P]).then_inc(oev, 1)
                nc.vector.tensor_copy(K.QT[rows, h // 2, P:T], ps_o[rows, 1, 0:4 * P]).then_inc(oev, 1)

            for j in range(J):
                dve.wait_ge(sc_done, j + 1)
                nc.vector.tensor_reduce(nmax[:, j:j + 1], scores(j), axis=AX.XY if STEPS[j][1] else AX.X, op=ALU.max,
                                        negate=True).then_inc(mx_done, 1)
                dve.wait_ge(mx_done, j + 1)
                nc.vector.tensor_scalar(nb[:, j:j + 1], nmax[:, j:j + 1], SCALE, None, ALU.mult).then_inc(nb_done, 1)
                if j:
                    normalise(j - 1)
                if j >= NT + 3 and (j - 3) % NT == 0:
                    output((j - 3) // NT - 1)
            normalise(J - 1)
            output(NH - 1)

        @block.scalar
        def _(act):
            def evacuate(j):
                h, qt = STEPS[j]
                act.wait_ge(pT_done, j + 1)
                if h >= 2 and qt == 0:
                    act.wait_ge(pv_done, h - 1)
                n = NT if qt else 1
                nc.scalar.activation(PT[h % 2][:, 0:n, qt * P:(qt + 1) * P], ps_t[:, 0:n, :], ACT.Copy).then_inc(ptev, 1)

            for j in range(J):
                act.wait_ge(nb_done, j + 1)
                if j >= 3:
                    act.wait_ge(pT_done, j - 2)
                nc.scalar.activation(probs(j), scores(j), ACT.Exp, bias=nb[:, j:j + 1], scale=SCALE,
                                     accum_out=sm[:, j:j + 1]).then_inc(exp_done, 1)
                if j >= 2:
                    evacuate(j - 2)
            evacuate(J - 2)
            evacuate(J - 1)



def phase_merge(nc, K, ctx):
    S = Stream(nc, K)
    sem = K.phase_semaphores(ctx)
    sb = lambda n, s, d=F32: ctx.enter_context(nc.sbuf_tensor(n, s, d))
    oT = [sb(f"g_oT{i}", [P, KD, T], F32R) for i in range(2)]
    mergedT = sb("mergedT", [P, KD, T])
    merged_out = K.pool_dma(NT + 6)
    sg = [sb(f"g_sg{i}", [P, 4, TH]) for i in range(2)]
    ps = [[ctx.enter_context(nc.psum_tensor(f"g_ps{s}{i}", [P, TH], F32)) for i in range(4)] for s in range(2)]
    oh_done = sem("g_oh"); ol_done = sem("g_ol")
    mm_done = [sem("g_mm0"), sem("g_mm1")]
    bank_read = [sem("g_read0"), sem("g_read1")]
    out_done = [K.pool_dma(NT + 4 + i) for i in range(2)]

    with nc.Block() as block:
        @block.sync
        def _(sp):
            with sp.Fori(0, N_MERGE // 2) as i:
                for s in range(2):
                    S.load(sp, 2 * i + (U_MERGE + s + 3), (s + 1) % 2)

        @block.gpsimd
        def _(pool):
            for i in range(4, 6):
                for s in range(2):
                    pool.wait_ge(bank_read[s], 4 * (i + 1))
                    pool.dma_start(K.sga_dram[2 * (2 * (i - 4) + s):2 * (2 * (i - 4) + s) + 2, :, :].rearrange("m p t -> p m t"),
                                   sg[s][:, :, :].rearrange("p (m a) t -> p m (a t)", a=2)).then_inc(out_done[s], 16)
                if i == 4:
                    pool.wait_ge(bank_read[1], 16)
                    pool.dma_start(K.merged_dram.rearrange("m p t -> p m t"), mergedT[:, :, :]).then_inc(merged_out, 16)
            for s in range(2):
                pool.wait_ge(out_done[s], 32)
            pool.wait_ge(merged_out, 16)

        @block.tensor
        def _(pe):
            def unit(i, s, act):
                n = 2 * i + (U_MERGE + s)
                S.ready(pe, n)
                if not isinstance(i, int):
                    pe.wait_ge(bank_read[s], 4 * i)
                project_features(nc, pe, (K.whi[s], K.wlo[s]), act, [p[:, :] for p in ps[s]]).then_inc(mm_done[s], 1)
                pe.drain().then_inc(K.hilo_free, 1)

            unit(0, 0, K.hT)
            pe.wait_ge(ol_done, 4)
            unit(0, 1, oT)
            with pe.Fori(1, 4) as i:
                unit(i, 0, K.hT)
                unit(i, 1, oT)
            with pe.Fori(4, 6) as i:
                unit(i, 0, K.hT)
                unit(i, 1, K.hT)

        @block.scalar
        def _(act):
            for q in range(4):
                nc.scalar.activation(oT[0][:, 2 * q:2 * q + 2, :], K.QT[:, 2 * q:2 * q + 2, :], ACT.Copy).then_inc(oh_done, 1)

            def sigmoids(i, s):
                act.wait_ge(mm_done[s], i + 1)
                for b in range(4):
                    nc.scalar.activation(sg[s][:, b, :], ps[s][b][:, :], ACT.Sigmoid).then_inc(bank_read[s], 1)

            def pair(i):
                if not isinstance(i, int):
                    act.wait_ge(bank_read[1], 4 * i)
                sigmoids(i, 0)
                S.hi(act, 2 * i + (U_MERGE + 2), 0)
                S.hi(act, 2 * i + (U_MERGE + 3), 1)

            pair(0)
            with act.Fori(1, 4) as i:
                pair(i)
            for i in range(4, 6):
                for s in range(2):
                    if i == 4:
                        act.wait_ge(bank_read[1], 16)
                    else:
                        act.wait_ge(out_done[s], 16)
                    sigmoids(i, s)
                    S.hi(act, 2 * i + (U_MERGE + 2 + s), s)

        @block.vector
        def _(dve):
            for q in range(4):
                dve.wait_ge(oh_done, q + 1)
                nc.vector.tensor_tensor(oT[1][:, 2 * q:2 * q + 2, :], K.QT[:, 2 * q:2 * q + 2, :],
                                        oT[0][:, 2 * q:2 * q + 2, :].bitcast(F32), ALU.subtract).then_inc(ol_done, 1)
            with dve.Fori(0, 4) as i:
                S.lo(dve, 2 * i + (U_MERGE + 2), 0)
                dve.wait_ge(mm_done[1], i + 1)
                dve.wait_ge(bank_read[0], 4 * i + 4)
                for b in range(4):
                    nc.vector.tensor_tensor(mergedT[:, bass.ds(2 * i + b // 2, 1), (b % 2) * TH:(b % 2 + 1) * TH],
                                            ps[1][b][:, :].unsqueeze(1), sg[0][:, b, :].unsqueeze(1), ALU.mult).then_inc(bank_read[1], 1)
                S.lo(dve, 2 * i + (U_MERGE + 3), 1)
            with dve.Fori(4, 6) as i:
                for s in range(2):
                    S.lo(dve, 2 * i + (U_MERGE + 2 + s), s)



def phase_ssd(nc, K, ctx):
    S = Stream(nc, K)
    sem = K.phase_semaphores(ctx)
    sb = lambda n, s, d=F32: ctx.enter_context(nc.sbuf_tensor(n, s, d))
    pb = lambda n, s: ctx.enter_context(nc.psum_tensor(n, s, F32))
    CW = 5
    PAD = CW // 2
    WC = P + PAD + 4 * P
    WI = WC + 2 * PAD
    XW = HPG * HP
    c0 = lambda c: 0 if c == 0 else P + PAD + (c - 1) * P
    ORDER = [4, 3, 2, 1, 0]
    cin = sb("s_cin", [P, 4, WI])
    xc = [sb(f"s_xc{i}", [P, 4, WC]) for i in range(2)]
    xb = sb("s_xb", [P, NT, XW + NS])
    xs = [sb(f"s_xs{i}", [P, 2, XW]) for i in range(2)]
    st = sb("s_st", [P, NT, 2, XW])
    pv = sb("s_pv", [P, 4, 2, XW])
    rT = [sb(f"s_rT{i}", [P, 2, HPG, P]) for i in range(2)]
    E = sb("s_E", [P, HPG, P])
    stl = sb("s_stl", [P, P]); stu = sb("s_stu", [P, P])
    A = sb("s_A", [P, HPG, P]); B = sb("s_B", [P, HPG, P])
    M = [sb(f"s_M{i}", [P, HPG, P]) for i in range(2)]
    t3 = sb("s_t3", [P, 2, XW]); xd = sb("s_xd", [P, XW])
    yb = [sb(f"s_yb{i}", [P, XW]) for i in range(2)]
    cw = sb("s_cw", [P, 32, CW]); cb = sb("s_cb", [P, 32]); dsk = sb("s_dsk", [P, HEADS])
    ps_p = [pb(f"s_pp{i}", [P, TH]) for i in range(4)]
    ps_tr = pb("s_ptr", [P, XW + NS]); ps_T = pb("s_pT", [P, HPG, P]); ps_so = pb("s_pso", [P, 2, XW])
    ps_y = pb("s_py", [P, XW])
    ps_sc = ps_tr[:, 0:P]

    par_in = sem("s_par"); zero = sem("s_zero")
    pj_mm, cin_done, conv_done, silu_done = sem("s_pj"), sem("s_cin_done"), sem("s_conv"), sem("s_silu")
    tr_mm, xb_done, xs_done, st_mm, st_done = sem("s_tr"), sem("s_xb_done"), sem("s_xs_done"), sem("s_stmm"), sem("s_st_done")
    pv_in, pv_done, pv_step, s_out = sem("s_pv_in"), sem("s_pv_done"), sem("s_pv_step"), sem("s_s_out")
    rT_done, T_mm, sc_mm, E_done, ml_done = sem("s_rT_done"), sem("s_T"), sem("s_sc"), sem("s_E_done"), sem("s_ml")
    A_done, B_done, PM, M_done = sem("s_A_done"), sem("s_B_done"), sem("s_PM"), sem("s_M_done")
    y_mm, xd_done, t3_done, y_step, y_done = sem("s_y"), sem("s_xd_done"), sem("s_t3_done"), sem("s_y_step"), sem("s_y_done")
    y_out = [sem("s_y_out0"), sem("s_y_out1")]
    cv = sem("s_cv")
    first = lambda g: isinstance(g, int) and g == 0

    heads = lambda ap: ap.rearrange("p (h d) -> p h d", d=HP)

    def per_head(ap, n):
        return ap.unsqueeze(len(ap.shape)).to_broadcast(list(ap.shape) + [n])

    def decay(row, c, g):
        return K.decay[:, row, bass.ds(4 * g + c * HEADS, HPG)]

    with nc.Block() as block:
        @block.sync
        def _(sp):
            sp.dma_start(cw[:, :, :], K.conv_w_cols).then_inc(par_in, 16)
            sp.dma_start(cb[:, :], K.conv_b_cols).then_inc(par_in, 16)
            sp.dma_start(dsk[:, :], K.d_skip.partition_broadcast(P).rearrange("p o h -> p (o h)")).then_inc(par_in, 16)

            def group_dmas(g, loads):
                if not first(g):
                    sp.wait_ge(y_mm, 5 * g)
                sp.dma_start(pv[:, 0, 0, :], K.state_f[:, bass.ds(4 * g, HPG), :].rearrange("p h d -> p (h d)")).then_inc(pv_in, 16)
                sp.dma_start(pv[:, 3, 1, :], K.state_b[:, bass.ds(4 * g, HPG), :].rearrange("p h d -> p (h d)")).then_inc(pv_in, 16)
                if loads:
                    S.load(sp, 2 * g + (U_SSD + 5), 1)
                sp.wait_ge(st_done, 5 * g + 5)
                sp.dma_start(K.out_new_sf[:, bass.ds(4 * g, HPG), :], heads(st[:, 0, 0, :])).then_inc(s_out, 16)
                sp.dma_start(K.out_new_sb[:, bass.ds(4 * g, HPG), :], heads(st[:, 0, 1, :])).then_inc(s_out, 16)
                for c in range(NT):
                    sp.wait_ge(y_done, 5 * g + (c + 1))
                    sp.dma_start(K.y_dram[c * P:(c + 1) * P, bass.ds(g * XW, XW)], yb[c % 2][:, :]).then_inc(y_out[c % 2], 16)
                    if c == 2 and loads:
                        S.load(sp, 2 * g + (U_SSD + 6), 0)

            S.load(sp, U_SSD + 3, 1)
            S.load(sp, U_SSD + 4, 0)
            with sp.Fori(0, 7) as g:
                group_dmas(g, True)
            group_dmas(7, False)
            sp.wait_ge(s_out, 8 * 32)
            sp.wait_ge(y_out[0], 24 * 16)
            sp.wait_ge(y_out[1], 16 * 16)

        @block.gpsimd
        def _(pool):
            nc.gpsimd.memset(cin[:, :, :], 0.0).then_inc(zero, 1)
            pool.wait_ge(par_in, 48)

            def build_rT(g, c):
                if c >= 2:
                    pool.wait_ge(T_mm, 5 * g + c - 1)
                elif not first(g):
                    pool.wait_ge(T_mm, 5 * g)
                for d, tri in ((0, K.tri_le), (1, K.tri_ge)):
                    ins = nc.gpsimd.tensor_tensor(rT[c % 2][:, d], per_head(K.dtA[:, c, bass.ds(4 * g + d * HEADS, HPG)], P),
                                                  tri[:, :].unsqueeze(1).to_broadcast([P, HPG, P]), ALU.mult)
                ins.then_inc(rT_done, 1)

            def carry(g, n, to, frm, d, c):
                pool.wait_ge(st_done, 5 * g + (ORDER.index(c) + 1))
                if n:
                    pool.wait_ge(pv_done, 6 * g + n)
                row = 2 if d == 0 else 5
                nc.gpsimd.tensor_tensor(heads(pv[:, to - 1, d, :]), heads(pv[:, frm - 1, d, :]), per_head(decay(row, c, g), HP),
                                        ALU.mult).then_inc(pv_step, 1)
                pool.wait_ge(pv_step, 6 * g + (n + 1))
                nc.gpsimd.tensor_tensor(pv[:, to - 1, d, :], pv[:, to - 1, d, :], st[:, c, d, :], ALU.add).then_inc(pv_done, 1)

            def skip(g, c):
                if c == 0:
                    pool.wait_ge(xb_done, 5 * g + 5)
                if not (first(g) and c == 0):
                    pool.wait_ge(y_done, 5 * g + c)
                nc.gpsimd.tensor_tensor(heads(xd[:, :]), heads(xb[:, c, 0:XW]), per_head(dsk[:, bass.ds(4 * g, HPG)], HP),
                                        ALU.mult).then_inc(xd_done, 1)

            def forward_part(g, c):
                pool.wait_ge(ml_done, 5 * g + (c + 1))
                if not (first(g) and c == 0):
                    pool.wait_ge(M_done, 5 * g + c)
                nc.gpsimd.tensor_tensor(A[:, :, :], stl[:, :].unsqueeze(1).to_broadcast([P, HPG, P]),
                                        per_head(K.dt[:, c, bass.ds(4 * g, HPG)], P), ALU.mult).then_inc(A_done, 1)

            def group_work(g):
                build_rT(g, 0)
                pool.wait_ge(pv_in, 32 * g + 32)
                carry(g, 0, 3, 4, 1, 4)
                carry(g, 1, 2, 3, 1, 3)
                carry(g, 2, 1, 2, 1, 2)
                carry(g, 3, 2, 1, 0, 1)
                build_rT(g, 1)
                skip(g, 0)
                forward_part(g, 0)
                build_rT(g, 2)
                carry(g, 4, 3, 2, 0, 2)
                carry(g, 5, 4, 3, 0, 3)
                for c in range(1, NT):
                    forward_part(g, c)
                    if c + 2 < NT:
                        build_rT(g, c + 2)
                    skip(g, c)

            for g in range(GROUPS):
                group_work(g)

        def piece(pe, g, p):
            m, half = p // 2, p % 2
            unit = m // 2
            n = 2 * g + (U_SSD + unit)
            if p % 4 == 0:
                S.ready(pe, n)
            if half == 0 and not (first(g) and m < 2):
                pe.wait_ge(cin_done, 4 * g + (m - 1))
            wh, wl = (x[unit][:, :].rearrange("p (k c) -> p k c", k=KD) for x in (K.whi, K.wlo))
            ah, al = K.hT
            cols = slice((m % 2) * P, (m % 2 + 1) * P)
            for k in range(4 * half, 4 * half + 4):
                for lhs, rhs, f, l in ((wh, ah, k == 0, False), (wh, al, False, False), (wl, ah, False, k == KD - 1)):
                    for h in range(2):
                        mm = nc.tensor.matmul(ps_p[2 * (m % 2) + h][:, :], lhs[:, k, cols], rhs[:, k, h * TH:(h + 1) * TH],
                                              start=f, stop=l)
            if half:
                mm.then_inc(pj_mm, 1)

        @block.tensor
        def _(pe):
            def transposes(g, s, a):
                c = ORDER[a]
                if a == 0:
                    pe.wait_ge(silu_done, 2 * g + 2)
                    if not first(g):
                        pe.wait_ge(ml_done, 5 * g)
                if not (first(g) and a == 0):
                    pe.wait_ge(xb_done, 5 * g + a)
                for m in range(3):
                    mm = nc.tensor.transpose(ps_tr[:, m * P:(m + 1) * P], xc[s][:, m, c0(c):c0(c) + P], K.ident[:, :])
                mm.then_inc(tr_mm, 1)

            def states(g, a):
                c = ORDER[a]
                pe.wait_ge(xs_done, 5 * g + (a + 1))
                if a:
                    pe.wait_ge(st_done, 5 * g + a)
                elif not first(g):
                    pe.wait_ge(t3_done, 4 * g)
                nc.tensor.matmul(ps_so[:, :, :], xb[:, c, XW:], xs[a % 2][:, :, :], start=True, stop=True).then_inc(st_mm, 1)

            def between(g, s, c):
                if not (first(g) and c == 0):
                    pe.wait_ge(ml_done, 5 * g + c)
                if c == 0:
                    pe.wait_ge(xb_done, 5 * g + 5)
                nc.tensor.matmul(ps_sc, xc[s][:, 2, c0(c):c0(c) + P], xc[s][:, 3, c0(c):c0(c) + P],
                                 start=True, stop=True).then_inc(sc_mm, 1)
                if not (first(g) and c == 0):
                    pe.wait_ge(E_done, 5 * g + c)
                pe.wait_ge(rT_done, 5 * g + (c + 1))
                nc.tensor.matmul(ps_T[:, :, :], K.tri_gt[:, :], rT[c % 2][:, 0], start=True, stop=False)
                nc.tensor.matmul(ps_T[:, :, :], K.tri_lt[:, :], rT[c % 2][:, 1], start=False, stop=True).then_inc(T_mm, 1)

            def outputs(g, s, c):
                if not (first(g) and c == 0):
                    pe.wait_ge(y_done, 5 * g + c)
                if c:
                    if c == 1:
                        pe.wait_ge(st_done, 5 * g + 5)
                    else:
                        pe.wait_ge(t3_done, 4 * g + (c - 1))
                    pe.wait_ge(pv_done, 6 * g + (c + 2))
                    nc.tensor.matmul(ps_so[:, :, :], xc[s][:, 3, c0(c):c0(c) + P], pv[:, c - 1], start=True, stop=True)
                pe.wait_ge(M_done, 5 * g + (c + 1))
                for h in range(HPG):
                    mm = nc.tensor.matmul(ps_y[:, h * HP:(h + 1) * HP], M[c % 2][:, h, :], xb[:, c, h * HP:(h + 1) * HP],
                                          start=True, stop=True)
                mm.then_inc(y_mm, 1)

            def group_work(g, s, ahead):
                for k in range(11):
                    if k < NT:
                        transposes(g, s, k)
                    if 1 <= k <= NT:
                        states(g, k - 1)
                    if NT <= k < 2 * NT:
                        between(g, s, k - NT)
                    if k > NT:
                        outputs(g, s, k - NT - 1)
                    if ahead and k < 8:
                        piece(pe, g + 1, k)

            for p in range(8):
                piece(pe, 0, p)
            with pe.Fori(0, 3) as i:
                group_work(2 * i, 0, True)
                group_work(2 * i + 1, 1, True)
            group_work(6, 0, True)
            group_work(7, 1, False)

        @block.scalar
        def _(act):
            act.wait_ge(zero, 1)

            def conv_input(g, m):
                act.wait_ge(pj_mm, 4 * g + (m + 1))
                if m % 2:
                    act.sem_inc(K.hilo_free, 1)
                if not first(g):
                    act.wait_ge(conv_done, 4 * g + (m - 3))
                b = ps_p[2 * (m % 2):2 * (m % 2) + 2]
                nc.scalar.activation(cin[:, m, PAD:PAD + P], b[0][:, 0:P], ACT.Copy)
                nc.scalar.activation(cin[:, m, 2 * PAD + P:2 * PAD + TH], b[0][:, P:TH], ACT.Copy)
                nc.scalar.activation(cin[:, m, 2 * PAD + TH:2 * PAD + T], b[1][:, :], ACT.Copy).then_inc(cin_done, 1)

            def silus(g, s, half):
                act.wait_ge(conv_done, 4 * g + 2 * half + 2)
                rows = xc[s][:, 2 * half:2 * half + 2, :]
                nc.scalar.activation(rows, rows, ACT.Silu).then_inc(silu_done, 1)

            def token_major(g, a):
                act.wait_ge(tr_mm, 5 * g + (a + 1))
                if a == 0 and not first(g):
                    act.wait_ge(y_mm, 5 * g)
                    act.wait_ge(xd_done, 5 * g)
                nc.scalar.activation(xb[:, ORDER[a], :], ps_tr[:, :], ACT.Copy).then_inc(xb_done, 1)

            def chunk_states(g, a):
                act.wait_ge(st_mm, 5 * g + (a + 1))
                if a == 0 and not first(g):
                    act.wait_ge(pv_done, 6 * g)
                if a == 4 and not first(g):
                    act.wait_ge(s_out, 32 * g)
                nc.scalar.activation(st[:, ORDER[a]], ps_so[:, :, :], ACT.Copy).then_inc(st_done, 1)

            def exps(g, c):
                act.wait_ge(T_mm, 5 * g + (c + 1))
                if not (first(g) and c == 0):
                    act.wait_ge(M_done, 5 * g + c)
                nc.scalar.activation(E[:, :, :], ps_T[:, :, :], ACT.Exp).then_inc(E_done, 1)

            def group_work(g, s, ahead, split):
                token_major(g, 0)
                token_major(g, 1)
                chunk_states(g, 0)
                if ahead:
                    conv_input(g + 1, 0)
                token_major(g, 2)
                chunk_states(g, 1)
                token_major(g, 3)
                chunk_states(g, 2)
                if ahead:
                    conv_input(g + 1, 1)
                if split:
                    S.hi(act, 2 * g + (U_SSD + 4), 0)
                token_major(g, 4)
                chunk_states(g, 3)
                chunk_states(g, 4)
                if ahead:
                    silus(g + 1, 1 - s, 0)
                exps(g, 0)
                if ahead:
                    conv_input(g + 1, 2)
                exps(g, 1)
                exps(g, 2)
                if ahead:
                    conv_input(g + 1, 3)
                if split:
                    S.hi(act, 2 * g + (U_SSD + 5), 1)
                exps(g, 3)
                exps(g, 4)
                if ahead:
                    silus(g + 1, 1 - s, 1)

            for m in range(4):
                conv_input(0, m)
            S.hi(act, U_SSD + 2, 0)
            S.hi(act, U_SSD + 3, 1)
            silus(0, 0, 0)
            silus(0, 0, 1)
            with act.Fori(0, 3) as i:
                group_work(2 * i, 0, True, True)
                group_work(2 * i + 1, 1, True, True)
            group_work(6, 0, True, True)
            group_work(7, 1, False, False)

        @block.vector
        def _(dve):
            dve.wait_ge(par_in, 48)
            n_cv = 4 * (CW - 1)

            def convolve(g, s, m):
                tile = bass.ds(2 * g + m, 1) if m < 2 else bass.ds(g + (16 if m == 2 else 24), 1)
                dve.wait_ge(cin_done, 4 * g + (m + 1))
                if m == 0 and not (isinstance(g, int) and g < 2):
                    dve.wait_ge(y_mm, 5 * g - 5)
                tap = lambda w: cw[:, tile, w:w + 1].rearrange("p o w -> p (o w)")
                out = xc[s][:, m, :]
                nc.vector.tensor_scalar(out, cin[:, m, 0:WC], tap(0), cb[:, tile], ALU.mult, ALU.add).then_inc(cv, 1)
                for w in range(1, CW):
                    dve.wait_ge(cv, n_cv * g + (4 * m + w))
                    nc.vector.scalar_tensor_tensor(out, cin[:, m, w:w + WC], tap(w), out, ALU.mult,
                                                   ALU.add).then_inc(cv if w < CW - 1 else conv_done, 1)

            def weighted(g, a):
                c = ORDER[a]
                dve.wait_ge(xb_done, 5 * g + (a + 1))
                if a >= 2:
                    dve.wait_ge(st_mm, 5 * g + (a - 1))
                elif not first(g):
                    dve.wait_ge(st_mm, 5 * g)
                for d, row in ((0, 1), (1, 4)):
                    ins = nc.vector.tensor_tensor(heads(xs[a % 2][:, d, :]), heads(xb[:, c, 0:XW]), per_head(decay(row, c, g), HP), ALU.mult)
                ins.then_inc(xs_done, 1)

            def mix(g, c):
                dve.wait_ge(sc_mm, 5 * g + (c + 1))
                if not (first(g) and c == 0):
                    dve.wait_ge(A_done, 5 * g + c)
                nc.vector.tensor_tensor(stl[:, :], ps_sc, K.tri_le[:, :], ALU.mult)
                nc.vector.tensor_tensor(stu[:, :], ps_sc, K.tri_ge[:, :], ALU.mult).then_inc(ml_done, 1)
                dve.wait_ge(ml_done, 5 * g + (c + 1))
                nc.vector.tensor_tensor(B[:, :, :], stu[:, :].unsqueeze(1).to_broadcast([P, HPG, P]),
                                        per_head(K.dt[:, c, bass.ds(4 * g + HEADS, HPG)], P), ALU.mult).then_inc(B_done, 1)
                dve.wait_ge(B_done, 5 * g + (c + 1))
                dve.wait_ge(A_done, 5 * g + (c + 1))
                nc.vector.tensor_tensor(B[:, :, :], B[:, :, :], A[:, :, :], ALU.add).then_inc(PM, 1)
                dve.wait_ge(PM, 5 * g + (c + 1))
                dve.wait_ge(E_done, 5 * g + (c + 1))
                if c >= 2:
                    dve.wait_ge(y_mm, 5 * g + (c - 1))
                elif not first(g):
                    dve.wait_ge(y_mm, 5 * g)
                nc.vector.tensor_tensor(M[c % 2][:, :, :], B[:, :, :], E[:, :, :], ALU.mult).then_inc(M_done, 1)

            def finish(g, c):
                dve.wait_ge(y_mm, 5 * g + (c + 1))
                dve.wait_ge(xd_done, 5 * g + (c + 1))
                per, before = (3, c // 2) if c % 2 == 0 else (2, c // 2)
                if not (first(g) and before == 0):
                    dve.wait_ge(y_out[c % 2], 16 * per * g + 16 * before)
                y = yb[c % 2]
                if c:
                    nc.vector.tensor_tensor(t3[:, :, :].rearrange("p a (h d) -> p a h d", h=HPG),
                                            ps_so[:, :, :].rearrange("p a (h d) -> p a h d", h=HPG),
                                            per_head(K.decay[:, 0:4:3, bass.ds(4 * g + c * HEADS, HPG)], HP), ALU.mult).then_inc(t3_done, 1)
                    nc.vector.tensor_tensor(y[:, :], ps_y[:, 0:XW], xd[:, :], ALU.add).then_inc(y_step, 1)
                    dve.wait_ge(t3_done, 4 * g + c)
                    dve.wait_ge(y_step, 8 * g + (2 * c - 1))
                    nc.vector.tensor_tensor(y[:, :], y[:, :], t3[:, 0, :], ALU.add).then_inc(y_step, 1)
                    dve.wait_ge(y_step, 8 * g + 2 * c)
                    nc.vector.tensor_tensor(y[:, :], y[:, :], t3[:, 1, :], ALU.add).then_inc(y_done, 1)
                    dve.wait_ge(y_done, 5 * g + (c + 1))
                else:
                    nc.vector.tensor_tensor(y[:, :], ps_y[:, 0:XW], xd[:, :], ALU.add).then_inc(y_done, 1)

            def group_work(g, s, ahead, split):
                weighted(g, 0)
                weighted(g, 1)
                if ahead:
                    convolve(g + 1, 1 - s, 0)
                weighted(g, 2)
                weighted(g, 3)
                if ahead:
                    convolve(g + 1, 1 - s, 1)
                if split:
                    S.lo(dve, 2 * g + (U_SSD + 4), 0)
                weighted(g, 4)
                mix(g, 0)
                if ahead:
                    convolve(g + 1, 1 - s, 2)
                mix(g, 1)
                finish(g, 0)
                mix(g, 2)
                finish(g, 1)
                if ahead:
                    convolve(g + 1, 1 - s, 3)
                if split:
                    S.lo(dve, 2 * g + (U_SSD + 5), 1)
                mix(g, 3)
                finish(g, 2)
                mix(g, 4)
                finish(g, 3)
                finish(g, 4)

            for m in range(4):
                convolve(0, 0, m)
            S.lo(dve, U_SSD + 2, 0)
            S.lo(dve, U_SSD + 3, 1)
            with dve.Fori(0, 3) as i:
                group_work(2 * i, 0, True, True)
                group_work(2 * i + 1, 1, True, True)
            group_work(6, 0, True, True)
            group_work(7, 1, False, False)



def phase_ssd_norm(nc, K, ctx):
    sem = K.phase_semaphores(ctx)
    sb = lambda n, s, d=F32: ctx.enter_context(nc.sbuf_tensor(n, s, d))
    KI = DI // P
    y = [sb(f"n_y{i}", [P, DI]) for i in range(2)]
    z = [sb(f"n_z{i}", [P, DI]) for i in range(2)]
    w = sb("n_w", [P, DI]); ss = sb("n_ss", [P, NT])
    ps = [ctx.enter_context(nc.psum_tensor(f"n_ps{i}", [P, 4, P], F32)) for i in range(4)]
    y_in = [sem(f"n_y_in{i}") for i in range(2)]
    w_in = sem("n_w_in"); gz_done = sem("n_gz"); sq_done = sem("n_sq"); ms_done = sem("n_ms"); rt_done = sem("n_rt")
    r_done = sem("n_r"); yn_done = sem("n_yn"); tr_done = sem("n_tr"); hi_done = sem("n_hi"); lo_done = sem("n_lo")

    with nc.Block() as block:
        @block.sync
        def _(sp):
            for t in range(NT):
                if t >= 2:
                    sp.wait_ge(tr_done, 4 * (t - 1))
                sp.dma_start(y[t % 2][:, :], K.y_dram[t * P:(t + 1) * P, :]).then_inc(y_in[t % 2], 16)
                sp.dma_start(z[t % 2][:, :], K.z_dram[t * P:(t + 1) * P, :]).then_inc(y_in[t % 2], 16)
                if t == 0:
                    sp.dma_start(w[:, :], K.ssd_norm_w.partition_broadcast(P).rearrange("p o d -> p (o d)")).then_inc(w_in, 16)

        @block.vector
        def _(dve):
            def lows(t):
                for b in range(4):
                    dve.wait_ge(hi_done, 4 * t + b + 1)
                    nc.vector.tensor_tensor(K.yT[1][:, 4 * b:4 * b + 4, t * P:(t + 1) * P], ps[b][:, :, :],
                                            K.yT[0][:, 4 * b:4 * b + 4, t * P:(t + 1) * P].bitcast(F32), ALU.subtract).then_inc(lo_done, 1)

            for t in range(NT):
                s = t % 2
                dve.wait_ge(y_in[s], 32 * (t // 2 + 1))
                nc.vector.tensor_tensor(y[s][:, :], y[s][:, :], z[s][:, :], ALU.mult).then_inc(gz_done, 1)
                dve.wait_ge(sq_done, t + 1)
                nc.vector.tensor_scalar(ss[:, t:t + 1], ss[:, t:t + 1], 1.0 / DI, EPS, ALU.mult, ALU.add).then_inc(ms_done, 1)
                if t:
                    lows(t - 1)
                dve.wait_ge(rt_done, t + 1)
                nc.vector.reciprocal(ss[:, t:t + 1], ss[:, t:t + 1]).then_inc(r_done, 1)
                dve.wait_ge(r_done, t + 1)
                if t == 0:
                    dve.wait_ge(w_in, 16)
                nc.vector.scalar_tensor_tensor(y[s][:, :], y[s][:, :], ss[:, t:t + 1], w[:, :], ALU.mult, ALU.mult).then_inc(yn_done, 1)
            lows(NT - 1)

        @block.scalar
        def _(act):
            def highs(t):
                for b in range(4):
                    act.wait_ge(tr_done, 4 * t + b + 1)
                    nc.scalar.activation(K.yT[0][:, 4 * b:4 * b + 4, t * P:(t + 1) * P], ps[b][:, :, :], ACT.Copy).then_inc(hi_done, 1)

            for t in range(NT):
                act.wait_ge(gz_done, t + 1)
                nc.scalar.activation(z[t % 2][:, :], y[t % 2][:, :], ACT.Square, accum_out=ss[:, t:t + 1]).then_inc(sq_done, 1)
                act.wait_ge(ms_done, t + 1)
                nc.scalar.activation(ss[:, t:t + 1], ss[:, t:t + 1], ACT.Sqrt).then_inc(rt_done, 1)
                if t:
                    highs(t - 1)
            highs(NT - 1)

        @block.tensor
        def _(pe):
            for t in range(NT):
                pe.wait_ge(yn_done, t + 1)
                for b in range(4):
                    if t:
                        pe.wait_ge(lo_done, 4 * (t - 1) + b + 1)
                    for i in range(4):
                        k = 4 * b + i
                        mm = nc.tensor.transpose(ps[b][:, i, :], y[t % 2][:, k * P:(k + 1) * P], K.ident[:, :])
                    mm.then_inc(tr_done, 1)



def phase_ssd_out(nc, K, ctx):
    S = Stream(nc, K)
    sem = K.phase_semaphores(ctx)
    sb = lambda n, s, d=F32: ctx.enter_context(nc.sbuf_tensor(n, s, d))
    sg = [sb(f"o_sg{i}", [P, 2, T]) for i in range(2)]
    mb = [sb(f"o_mb{i}", [P, 2, T]) for i in range(2)]
    ps = [[ctx.enter_context(nc.psum_tensor(f"o_ps{s}{i}", [P, TH], F32)) for i in range(4)] for s in range(2)]
    ld = [sem("o_ld0"), sem("o_ld1")]
    mm_done = sem("o_mm"); gated = sem("o_gated"); added = sem("o_added"); out = [sem("o_out0"), sem("o_out1")]

    def columns(c):
        return bass.ds(2 * c, 2)

    with nc.Block() as block:
        @block.sync
        def _(sp):
            def block_dmas(c, s):
                sp.dma_start(sg[s][:, :, :], K.sga_dram[columns(c), :, :].rearrange("m p t -> p m t")).then_inc(ld[s], 16)
                sp.dma_start(mb[s][:, :, :], K.merged_dram[columns(c), :, :].rearrange("m p t -> p m t")).then_inc(ld[s], 16)

            block_dmas(0, 0)
            block_dmas(1, 1)
            for c in range(4):
                S.load(sp, U_SO + 2 * c + 3, 1)
                S.load(sp, U_SO + 2 * c + 4, 0)
                sp.wait_ge(added, 4 * (c + 1))
                sp.dma_start(K.merged_dram[2 * c:2 * c + 2, :, :].rearrange("m p t -> p m t"), mb[c % 2][:, :, :]).then_inc(out[c % 2], 16)
                if c + 2 < 4:
                    sp.wait_ge(out[c % 2], 16)
                    block_dmas(c + 2, c % 2)
            for s in range(2):
                sp.wait_ge(out[s], 32)

        @block.tensor
        def _(pe):
            pe.sem_inc(K.so_free, 8)

            def unit(c, s, half):
                S.ready(pe, 2 * c + (U_SO + half))
                wh, wl = (x[half][:, :].rearrange("p (k c) -> p k c", k=KD) for x in (K.whi, K.wlo))
                for m in range(2):
                    for k in range(KD):
                        cols, kk = slice(m * P, (m + 1) * P), half * KD + k
                        for lhs, rhs, f, l in ((wh, K.yT[0], kk == 0, False), (wh, K.yT[1], False, False),
                                               (wl, K.yT[0], False, kk == 2 * KD - 1)):
                            for h in range(2):
                                mm = nc.tensor.matmul(ps[s][2 * m + h][:, :], lhs[:, k, cols], rhs[:, kk, h * TH:(h + 1) * TH],
                                                      start=f, stop=l)
                if half:
                    mm.then_inc(mm_done, 1)
                pe.drain().then_inc(K.hilo_free, 1)

            with pe.Fori(0, 2) as i:
                for s in range(2):
                    c = 2 * i + s
                    pe.wait_ge(K.so_free, 4 * c + 4)
                    unit(c, s, 0)
                    unit(c, s, 1)

        @block.scalar
        def _(act):
            with act.Fori(0, 4) as c:
                S.hi(act, 2 * c + (U_SO + 2), 0)
                S.hi(act, 2 * c + (U_SO + 3), 1)

        @block.vector
        def _(dve):
            with dve.Fori(0, 2) as i:
                for s in range(2):
                    c = 2 * i + s
                    S.lo(dve, 2 * c + (U_SO + 2), 0)
                    dve.wait_ge(mm_done, c + 1)
                    dve.wait_ge(ld[s], 32 * i + 32)
                    for b in range(4):
                        v = sg[s][:, b // 2, (b % 2) * TH:(b % 2 + 1) * TH]
                        nc.vector.tensor_tensor(v, v, ps[s][b][:, :], ALU.mult).then_inc(K.so_free, 1)
                    dve.wait_ge(K.so_free, 4 * c + 12)
                    for b in range(4):
                        v = mb[s][:, b // 2, (b % 2) * TH:(b % 2 + 1) * TH]
                        nc.vector.tensor_tensor(v, v, sg[s][:, b // 2, (b % 2) * TH:(b % 2 + 1) * TH], ALU.add).then_inc(added, 1)
                    S.lo(dve, 2 * c + (U_SO + 3), 1)



def phase_mix_out(nc, K, ctx):
    S = Stream(nc, K)
    sem = K.phase_semaphores(ctx)
    sb = lambda n, s, d=F32: ctx.enter_context(nc.sbuf_tensor(n, s, d))
    m32 = sb("x_m32", [P, KD, T])
    mT = [sb(f"x_mT{i}", [P, KD, T], F32R) for i in range(2)]
    x = sb("x_x", [P, NT, D]); g1 = sb("x_g1", [P, 2, D]); tmp = sb("x_tmp", [P, 2 * UC])
    xn = sb("x_n", [P, D]); hf = sb("x_hf", [P, KD, P]); ss = sb("x_ss", [P, NT])
    ps = [ctx.enter_context(nc.psum_tensor(f"x_ps{t}", [P, 2 * UC], F32)) for t in range(NT)]
    ps_x = [ctx.enter_context(nc.psum_tensor(f"x_px{i}", [P, 4, P], F32)) for i in range(2)]
    m_in = sem("x_m_in"); x_in = sem("x_x_in"); mh = sem("x_mh"); ml = sem("x_ml"); mm_done = sem("x_mm")
    scaled = sem("x_scaled"); res = sem("x_res"); sq_done = sem("x_sq"); ms_done = sem("x_ms"); rt_done = sem("x_rt")
    r_done = sem("x_r"); xn_done = sem("x_xn"); tr_done = sem("x_tr"); hf_done = sem("x_hf_done"); hh = sem("x_hh"); hl = sem("x_hl")
    x_out = sem("x_out")

    with nc.Block() as block:
        @block.sync
        def _(sp):
            sp.dma_start(m32[:, :, :], K.merged_dram.rearrange("m p t -> p m t")).then_inc(m_in, 16)
            sp.dma_start(x[:, :, :], K.x.rearrange("(t p) d -> p t d", p=P)).then_inc(x_in, 16)
            for g in range(2):
                sp.dma_start(g1[:, g, :], K.gates[g:g + 1, 0:D].partition_broadcast(P).rearrange("p o d -> p (o d)")).then_inc(x_in, 16)
            for n in range(U_O, U_PQ):
                S.load(sp, n + 3, (n + 3) % 2)
            sp.wait_ge(res, 2 * NT)
            sp.dma_start(K.x2_dram.rearrange("(t p) d -> p t d", p=P), x[:, :, :]).then_inc(x_out, 16)
            sp.wait_ge(x_out, 16)

        @block.tensor
        def _(pe):
            pe.wait_ge(ml, 4)
            for n in range(U_O, U_PQ):
                i, s = (n - U_O) // 2, n % 2
                S.ready(pe, n)
                wh, wl = (w[s][:, :].rearrange("p (k c) -> p k c", k=KD) for w in (K.whi, K.wlo))
                for t in range(NT):
                    if i and s == 0:
                        pe.wait_ge(scaled, t + 1)
                    tc = slice(t * P, (t + 1) * P)
                    for k in range(KD):
                        mm = mm3(nc, ps[t][:, s * UC:(s + 1) * UC], (mT[0][:, k, tc], mT[1][:, k, tc]),
                                 (wh[:, k, :], wl[:, k, :]), k == 0, k == KD - 1)
                    if s == 1:
                        mm.then_inc(mm_done, 1)
                pe.drain().then_inc(K.hilo_free, 1)
            for t in range(NT):
                pe.wait_ge(xn_done, t + 1)
                for h in range(2):
                    if t:
                        pe.wait_ge(hf_done, KD * (t - 1) + 4 * (h + 1))
                    for k in range(4):
                        mm = nc.tensor.transpose(ps_x[h][:, k, :], xn[:, (4 * h + k) * P:(4 * h + k + 1) * P], K.ident[:, :])
                    mm.then_inc(tr_done, 1)

        @block.scalar
        def _(act):
            act.wait_ge(m_in, 16)
            for q in range(4):
                nc.scalar.activation(mT[0][:, 2 * q:2 * q + 2, :], m32[:, 2 * q:2 * q + 2, :], ACT.Copy).then_inc(mh, 1)
            for n in range(U_O, U_PQ):
                S.hi(act, n + 2, n % 2)
            for t in range(NT):
                act.wait_ge(res, NT + t + 1)
                if t:
                    act.wait_ge(tr_done, 2 * t)
                nc.scalar.activation(xn[:, :], x[:, t, :], ACT.Square, accum_out=ss[:, t:t + 1]).then_inc(sq_done, 1)
                act.wait_ge(ms_done, t + 1)
                nc.scalar.activation(ss[:, t:t + 1], ss[:, t:t + 1], ACT.Sqrt).then_inc(rt_done, 1)
                for h in range(2):
                    act.wait_ge(tr_done, 2 * t + h + 1)
                    if t and h == 0:
                        act.wait_ge(hl, t)
                    for k in range(4):
                        kd = 4 * h + k
                        nc.scalar.activation(hf[:, kd, :], ps_x[h][:, k, :], ACT.Identity,
                                             scale=K.mul2[:, kd, group(t):group(t) + 1],
                                             bias=K.add2[:, kd, group(t):group(t) + 1]).then_inc(hf_done, 1)

        @block.vector
        def _(dve):
            for q in range(4):
                dve.wait_ge(mh, q + 1)
                nc.vector.tensor_tensor(mT[1][:, 2 * q:2 * q + 2, :], m32[:, 2 * q:2 * q + 2, :],
                                        mT[0][:, 2 * q:2 * q + 2, :].bitcast(F32), ALU.subtract).then_inc(ml, 1)
            dve.wait_ge(x_in, 48)
            for i in range(2):
                for t in range(NT):
                    n = NT * i + t
                    dve.wait_ge(mm_done, n + 1)
                    cols = slice(i * 512, (i + 1) * 512)
                    if n:
                        dve.wait_ge(res, n)
                    nc.vector.tensor_tensor(tmp[:, :], ps[t][:, :], g1[:, group(t), cols], ALU.mult).then_inc(scaled, 1)
                    dve.wait_ge(scaled, n + 1)
                    nc.vector.tensor_tensor(x[:, t, cols], x[:, t, cols], tmp[:, :], ALU.add).then_inc(res, 1)
                S.lo(dve, U_O + 2 * i + 2, 0)
                S.lo(dve, U_O + 2 * i + 3, 1)
            for t in range(NT):
                dve.wait_ge(sq_done, t + 1)
                nc.vector.tensor_scalar(ss[:, t:t + 1], ss[:, t:t + 1], 1.0 / D, EPS, ALU.mult, ALU.add).then_inc(ms_done, 1)
                dve.wait_ge(rt_done, t + 1)
                nc.vector.reciprocal(ss[:, t:t + 1], ss[:, t:t + 1]).then_inc(r_done, 1)
                dve.wait_ge(r_done, t + 1)
                nc.vector.tensor_scalar(xn[:, :], x[:, t, :], ss[:, t:t + 1], None, ALU.mult).then_inc(xn_done, 1)
                dve.wait_ge(hf_done, KD * (t + 1))
                tc = slice(t * P, (t + 1) * P)
                nc.vector.tensor_copy(K.h2T[0][:, :, tc], hf[:, :, :]).then_inc(hh, 1)
                dve.wait_ge(hh, t + 1)
                nc.vector.tensor_tensor(K.h2T[1][:, :, tc], hf[:, :, :], K.h2T[0][:, :, tc].bitcast(F32), ALU.subtract).then_inc(hl, 1)



def phase_route(nc, K, ctx):
    S = Stream(nc, K)
    sem = K.phase_semaphores(ctx)
    sb = lambda n, s, d=F32: ctx.enter_context(nc.sbuf_tensor(n, s, d))
    LOW = -3.0e38
    keys = sb("r_keys", [P, 2 * PH, NKEYS])
    q = [sb(f"r_q{i}", [P, 2, T]) for i in range(2)]
    sc = [sb(f"r_sc{i}", [P, NT, 2, NKEYS]) for i in range(2)]
    v16 = sb("r_v16", [P, NT, 2, TOPK]); i16 = sb("r_i16", [P, NT, 2, TOPK], U32); f16 = sb("r_f16", [P, NT, 2, TOPK])
    cand = sb("r_cand", [P, NT, TOPK, TOPK])
    bv = sb("r_bv", [P, NT, TOPK]); bi = sb("r_bi", [P, NT, TOPK], U32)
    ki = sb("r_ki", [P, 2, NT, TOPK], U32); kf = sb("r_kf", [P, 2, NT * TOPK])
    eq = [sb(f"r_eq{i}", [P, NT * TOPK, TOPK]) for i in range(2)]; bs = sb("r_bs", [P, NT, TOPK]); be = sb("r_be", [P, NT, TOPK])
    sm = sb("r_sm", [P, NT])
    slots = sb("r_slots", [P, 3, NT, SLOTS])
    ps = [ctx.enter_context(nc.psum_tensor(f"r_ps{i}", [P, TH], F32)) for i in range(4)]
    ps_k = [ctx.enter_context(nc.psum_tensor(f"r_pk{i}", [P, 2, 2, NKEYS], F32)) for i in range(3)]
    ps_t = ctx.enter_context(nc.psum_tensor("r_pt", [P, 3, P], F32))
    k_in = sem("r_k_in"); mm_done = sem("r_mm"); q_done = sem("r_q_done"); sc_mm = sem("r_sc_mm"); sc_done = sem("r_sc_done")
    chain = sem("r_chain"); top_done = sem("r_top"); sub_done = sem("r_sub"); be_done = sem("r_be_done"); slot_done = sem("r_slot")
    tr_done = sem("r_tr"); ev_done = sem("r_ev")

    with nc.Block() as block:
        @block.sync
        def _(sp):
            sp.dma_start(keys[:, :, :], K.keys_t).then_inc(k_in, 16)
            with sp.Fori(0, PH // 2) as i:
                for s in range(2):
                    S.load(sp, 2 * i + (U_PQ + s + 3), (s + 1) % 2)

        @block.tensor
        def _(pe):
            pe.wait_ge(k_in, 16)

            def queries(h, s):
                S.ready(pe, h + U_PQ)
                if not (isinstance(h, int) and h == 0):
                    pe.wait_ge(q_done, 4 * h)
                project_features(nc, pe, (K.whi[s], K.wlo[s]), K.h2T, [p[:, :] for p in ps]).then_inc(mm_done, 1)

            def scores(h, s):
                pe.wait_ge(q_done, 4 * h + 4)
                if not (isinstance(h, int) and h == 0):
                    pe.wait_ge(sc_done, 3 * h)
                for t in range(NT):
                    for c in range(2):
                        mm = nc.tensor.matmul(ps_k[t // 2][:, t % 2, c, :], q[s][:, c, t * P:(t + 1) * P],
                                              keys[:, bass.ds(2 * h + c, 1), :].rearrange("p o k -> p (o k)"), start=True, stop=True)
                mm.then_inc(sc_mm, 1)

            queries(0, 0)
            with pe.Fori(0, 3) as i:
                queries(2 * i + 1, 1)
                scores(2 * i, 0)
                queries(2 * i + 2, 0)
                scores(2 * i + 1, 1)
            queries(7, 1)
            scores(6, 0)
            scores(7, 1)
            pe.wait_ge(slot_done, PH)
            for t in range(NT):
                if t:
                    pe.wait_ge(ev_done, t)
                for r in range(3):
                    mm = nc.tensor.transpose(ps_t[:, r, :], slots[:, r, t, :], K.ident[:, :])
                mm.then_inc(tr_done, 1)

        @block.scalar
        def _(act):
            def copies(h, s):
                act.wait_ge(mm_done, h + 1)
                act.sem_inc(K.hilo_free, 1)
                if not (isinstance(h, int) and h < 2):
                    act.wait_ge(sc_mm, h - 1)
                for m in range(2):
                    for a in range(2):
                        nc.scalar.activation(q[s][:, m, a * TH:(a + 1) * TH], ps[2 * m + a][:, :], ACT.Copy).then_inc(q_done, 1)
                S.hi(act, h + (U_PQ + 2), s)

            def score_copies(h, s):
                act.wait_ge(sc_mm, h + 1)
                if not (isinstance(h, int) and h < 2):
                    act.wait_ge(top_done, h - 1)
                for b in range(3):
                    n = 2 if b < 2 else 1
                    nc.scalar.activation(sc[s][:, 2 * b:2 * b + n, :, :], ps_k[b][:, 0:n, :, :], ACT.Copy).then_inc(sc_done, 1)

            def gate_exp(h):
                act.wait_ge(sub_done, h + 1)
                nc.scalar.activation(be[:, :, :], bs[:, :, :], ACT.Exp).then_inc(be_done, 1)

            copies(0, 0)
            copies(1, 1)
            score_copies(0, 0)
            with act.Fori(0, 3) as i:
                copies(2 * i + 2, 0)
                score_copies(2 * i + 1, 1)
                gate_exp(2 * i)
                copies(2 * i + 3, 1)
                score_copies(2 * i + 2, 0)
                gate_exp(2 * i + 1)
            score_copies(7, 1)
            gate_exp(6)
            gate_exp(7)
            for t in range(NT):
                act.wait_ge(tr_done, t + 1)
                nc.scalar.activation(K.slotsT[:, :, t * P:(t + 1) * P], ps_t[:, :, :], ACT.Copy).then_inc(ev_done, 1)

        @block.vector
        def _(dve):
            done = [0]

            def stage(instructions):
                for ins in instructions:
                    done[0] += 1
                    ins.then_inc(chain, 1)
                dve.wait_ge(chain, done[0])

            def top16(rows):
                stage(nc.vector.max(best[:, 0:8], values) for values, best, _ in rows)
                stage(nc.vector.max_index(index[:, 0:8], best[:, 0:8], values) for values, best, index in rows)
                stage(nc.vector.match_replace(out=values, in_to_replace=best[:, 0:8], in_values=values, imm_value=LOW)
                      for values, best, _ in rows)
                stage(nc.vector.max(best[:, 8:16], values) for values, best, _ in rows)
                stage(nc.vector.max_index(index[:, 8:16], best[:, 8:16], values) for values, best, index in rows)

            def search(h, s):
                dve.wait_ge(sc_done, 3 * h + 3)
                top16([(sc[s][:, t, c, :], v16[:, t, c, :], i16[:, t, c, :]) for t in range(NT) for c in range(2)])
                for t in range(NT):
                    ins = nc.vector.tensor_tensor(cand[:, t], v16[:, t, 0, :].unsqueeze(2).to_broadcast([P, TOPK, TOPK]),
                                                  v16[:, t, 1, :].unsqueeze(1).to_broadcast([P, TOPK, TOPK]), ALU.add)
                ins.then_inc(top_done, 1)
                stage([nc.vector.tensor_copy(f16[:, :, :, :], i16[:, :, :, :])])
                dve.wait_ge(top_done, h + 1)
                top16([(cand[:, t].rearrange("p a b -> p (a b)"), bv[:, t, :], bi[:, t, :]) for t in range(NT)])
                nc.vector.tensor_tensor(bs[:, :, :], bv[:, :, :], bv[:, :, 0:1].to_broadcast([P, NT, TOPK]), ALU.subtract).then_inc(sub_done, 1)
                stage([nc.vector.tensor_scalar(ki[:, 0], bi[:, :, :], 4, None, ALU.logical_shift_right),
                       nc.vector.tensor_scalar(ki[:, 1], bi[:, :, :], 15, None, ALU.bitwise_and)])
                stage([nc.vector.tensor_copy(kf[:, :, :], ki[:, :, :, :].rearrange("p c t k -> p c (t k)"))])
                slot = slice(TOPK * h, TOPK * (h + 1))
                e4 = [eq[c][:, :, :].rearrange("p (t k) e -> p t k e", t=NT) for c in range(2)]
                stage([nc.vector.tensor_tensor(eq[c][:, :, :], kf[:, c, :].unsqueeze(2).to_broadcast([P, NT * TOPK, TOPK]),
                                               K.iota[:, 0:TOPK].unsqueeze(1).to_broadcast([P, NT * TOPK, TOPK]), ALU.is_equal)
                       for c in range(2)])
                stage([nc.vector.tensor_tensor(e4[c], e4[c], f16[:, :, c, :].unsqueeze(2).to_broadcast([P, NT, TOPK, TOPK]), ALU.mult)
                       for c in range(2)])
                dve.wait_ge(be_done, h + 1)
                stage([nc.vector.tensor_reduce(sm[:, :], be[:, :, :], axis=AX.X, op=ALU.add)]
                      + [nc.vector.tensor_reduce(slots[:, c, :, slot], e4[c], axis=AX.X, op=ALU.add) for c in range(2)])
                stage([nc.vector.reciprocal(sm[:, :], sm[:, :])])
                nc.vector.tensor_tensor(slots[:, 2, :, slot], be[:, :, :], sm[:, :].unsqueeze(2).to_broadcast([P, NT, TOPK]),
                                        ALU.mult).then_inc(slot_done, 1)
                dve.wait_ge(slot_done, h + 1)

            S.lo(dve, U_PQ + 2, 0)
            S.lo(dve, U_PQ + 3, 1)
            for h in range(PH):
                search(h, h % 2)
                if h < PH - 2:
                    S.lo(dve, h + U_PQ + 4, h % 2)



def phase_gates(nc, K, ctx):
    sem = K.phase_semaphores(ctx)
    sb = lambda n, s, d=F32: ctx.enter_context(nc.sbuf_tensor(n, s, d))
    TB, Q = 64, 8
    STEPS = TB // Q
    stage = [sb(f"e_st{i}", [P, P, TB]) for i in range(2)]
    gate = [sb(f"e_gate{i}", [P, Q]) for i in range(2)]
    oj = [sb(f"e_oj{i}", [P, Q, P]) for i in range(2)]
    oi = [sb(f"e_oi{i}", [P, Q, P]) for i in range(2)]
    ps = [[ctx.enter_context(nc.psum_tensor(f"e_ps{u}{i}", [P, Q // 2, P], F32)) for i in range(2)] for u in range(2)]
    hot_done = sem("e_hot"); weighted = sem("e_weighted"); mm_done = sem("e_mm")
    bank_free = sem("e_bank_free"); ev_done = sem("e_ev")
    out = [sem("e_out0"), sem("e_out1")]

    with nc.Block() as block:
        @block.sync
        def _(sp):
            with sp.Fori(0, T // TB // 2) as b:
                for s in range(2):
                    sp.wait_ge(ev_done, 4 * STEPS * b + (2 * STEPS * (s + 1)))
                    sp.dma_start(K.g_dram[bass.ds(2 * b + s, 1)].rearrange("o j i t -> j (o i t)"),
                                 stage[s][:, :, :].rearrange("p i t -> p (i t)")).then_inc(out[s], 16)
            for s in range(2):
                sp.wait_ge(out[s], 16 * (T // TB // 2))

        @block.vector
        def _(dve):
            def one_hots(g, u):
                dve.wait_ge(mm_done, 2 * g + 2)
                tok = bass.ds(Q * g, Q)
                iota = K.iota[:, :].unsqueeze(1).to_broadcast([P, Q, P])
                key = lambda r: K.slotsT[:, r, tok].unsqueeze(2).to_broadcast([P, Q, P])
                nc.vector.tensor_copy(gate[u][:, :], K.slotsT[:, 2, tok])
                nc.vector.tensor_tensor(oi[u][:, :, :], iota, key(0), ALU.is_equal).then_inc(hot_done, 1)
                nc.vector.tensor_tensor(oj[u][:, :, :], iota, key(1), ALU.is_equal).then_inc(hot_done, 1)

            with dve.Fori(0, T // Q // 2) as i:
                for u in range(2):
                    one_hots(2 * i + u, u)

        @block.gpsimd
        def _(pool):
            with pool.Fori(0, T // Q // 2) as i:
                for u in range(2):
                    pool.wait_ge(hot_done, 4 * i + (2 * u + 1))
                    nc.gpsimd.tensor_tensor(oi[u][:, :, :], oi[u][:, :, :], gate[u][:, :].unsqueeze(2).to_broadcast([P, Q, P]),
                                            ALU.mult).then_inc(weighted, 1)

        @block.tensor
        def _(pe):
            pe.sem_inc(bank_free, 4)
            pe.sem_inc(mm_done, 4)

            def products(g, u):
                pe.wait_ge(hot_done, 2 * g + 2)
                pe.wait_ge(weighted, g + 1)
                for h in range(2):
                    pe.wait_ge(bank_free, 2 * g + (h + 1))
                    for t in range(Q // 2):
                        mm = nc.tensor.matmul(ps[u][h][:, t, :], oj[u][:, h * Q // 2 + t, :], oi[u][:, h * Q // 2 + t, :], start=True, stop=True)
                    mm.then_inc(mm_done, 1)

            with pe.Fori(0, T // Q // 2) as i:
                for u in range(2):
                    products(2 * i + u, u)

        @block.scalar
        def _(act):
            def fill(b, s):
                with act.Fori(0, STEPS // 2) as i:
                    for u in range(2):
                        for h in range(2):
                            done = 4 * STEPS * b + 4 * i + (2 * STEPS * s + 2 * u + h)
                            act.wait_ge(mm_done, done + 5)
                            nc.scalar.activation(stage[s][:, :, bass.ds(2 * Q * i + (Q * u + Q // 2 * h), Q // 2)].rearrange("p i t -> p t i"),
                                                 ps[u][h][:, :, :], ACT.Copy).then_inc(ev_done, 1)
                            act.wait_ge(ev_done, done + 1)
                            act.sem_inc(bank_free, 1)

            fill(0, 0)
            fill(0, 1)
            with act.Fori(1, T // TB // 2) as b:
                for s in range(2):
                    act.wait_ge(out[s], 16 * b)
                    fill(b, s)



def phase_experts(nc, K, ctx):
    S = Stream(nc, K)
    sem = K.phase_semaphores(ctx)
    sb = lambda n, s, d=F32: ctx.enter_context(nc.sbuf_tensor(n, s, d))
    PAIRS = NKEYS // 2
    TB = 64
    NB = 4
    OUTS = [(t, d) for t in range(NT) for d in range(2)]
    NO = len(OUTS)
    G = [sb(f"p_g{i}", [P, T // TB, 2, TB]) for i in range(2)]
    A = sb("p_a", [P, 2, T]); W = sb("p_w", [P, 2, T])
    Wh = [sb(f"p_wh{i}", [P, 2, T], F32R) for i in range(2)]
    Wl = [sb(f"p_wl{i}", [P, 2, T], F32R) for i in range(2)]
    ps_a = [ctx.enter_context(nc.psum_tensor(f"p_pa{i}", [P, TH], F32)) for i in range(4)]
    ps_y = [ctx.enter_context(nc.psum_tensor(f"p_py{i}", [P, 512], F32)) for i in range(NB)]
    g_in = [sem("p_g_in0"), sem("p_g_in1")]
    a_mm = sem("p_a_mm"); a_done = sem("p_a_done"); w_done = sem("p_w_done"); wh_done = sem("p_wh_done"); wl_done = sem("p_wl_done")
    y_mm = sem("p_y_mm"); y_added = sem("p_y_added"); zeroed = sem("p_zero")
    is0 = lambda n: isinstance(n, int) and n == 0

    with nc.Block() as block:
        @block.sync
        def _(sp):
            def load_g(n, s):
                sp.dma_start(G[s][:, :, :, :], K.g_dram[:, :, bass.ds(2 * n, 2), :].rearrange("b j i t -> j b i t")).then_inc(g_in[s], 16)

            def pair(n, s, stream, gates):
                if stream:
                    S.load(sp, 2 * n + (U_EXP + 4), 0)
                if gates:
                    sp.wait_ge(w_done, n + 1)
                    load_g(n + 2, s)
                if stream:
                    S.load(sp, 2 * n + (U_EXP + 5), 1)

            load_g(0, 0)
            load_g(1, 1)
            S.load(sp, U_EXP + 3, 1)
            sp.dma_start(K.res[:, :, :], K.x2_dram.rearrange("(t p) d -> p t d", p=P)).then_inc(K.final_in, 16)
            for g in range(2):
                sp.dma_start(K.gate2[:, g, :], K.gates[g:g + 1, D:2 * D].partition_broadcast(P).rearrange("p o d -> p (o d)")).then_inc(K.final_in, 16)
            sp.dma_start(K.norm_w[:, :], K.final_norm_w.partition_broadcast(P).rearrange("p o d -> p (o d)")).then_inc(K.final_in, 16)
            with sp.Fori(0, 30) as i:
                pair(2 * i, 0, True, True)
                pair(2 * i + 1, 1, True, True)
            pair(60, 0, True, True)
            pair(61, 1, False, True)
            S.load(sp, U_EXP + 126, 0)
            S.load(sp, U_EXP + 127, 1)

        @block.tensor
        def _(pe):
            def hidden(n, slot):
                S.ready(pe, U_EXP if is0(n) else 2 * n + (U_EXP - 1))
                if not is0(n):
                    pe.wait_ge(a_done, 4 * n)
                project_features(nc, pe, (K.whi[slot], K.wlo[slot]), K.h2T, [p[:, :] for p in ps_a]).then_inc(a_mm, 1)

            def output(n, s, slot, unit):
                S.ready(pe, unit)
                pe.wait_ge(wl_done, n + 1)
                vh, vl = (x[slot][:, :].rearrange("p (c d) -> p c d", c=2) for x in (K.whi, K.wlo))
                for o, (t, d) in enumerate(OUTS):
                    last = o - NB if o >= NB else max(x for x in range(NO) if x % NB == o) - NO
                    pe.wait_ge(y_added, NO * n + (NO + last + 1))
                    tc, dc = slice(t * P, (t + 1) * P), slice(d * 512, (d + 1) * 512)
                    for c in range(2):
                        mm = mm3(nc, ps_y[o % NB][:, :], (Wh[s][:, c, tc], Wl[s][:, c, tc]), (vh[:, c, dc], vl[:, c, dc]), c == 0, c == 1)
                    mm.then_inc(y_mm, 1)

            hidden(0, 0)
            with pe.Fori(0, 31) as i:
                for s in range(2):
                    n = 2 * i + s
                    hidden(n + 1, 1)
                    output(n, s, 0, 2 * n + (U_EXP + 2))
            hidden(63, 1)
            output(62, 0, 0, U_EXP + 126)
            output(63, 1, 1, U_EXP + 127)

        @block.scalar
        def _(act):
            def gelu(n, s):
                act.wait_ge(a_mm, n + 1)
                if not is0(n):
                    act.wait_ge(w_done, n)
                for m in range(2):
                    for h in range(2):
                        nc.scalar.activation(A[:, m, h * TH:(h + 1) * TH], ps_a[2 * m + h][:, :], ACT.Gelu_apprx_tanh).then_inc(a_done, 1)

            def w_hi(n, s):
                act.wait_ge(w_done, n + 1)
                if not (isinstance(n, int) and n < 2):
                    act.wait_ge(y_mm, NO * n - NO)
                nc.scalar.activation(Wh[s][:, :, :], W[:, :, :], ACT.Copy).then_inc(wh_done, 1)

            def hi_u(n, slot):
                S.hi(act, n, slot, False)

            def hi_v(pair, n, slot):
                act.wait_ge(y_mm, NO * pair)
                S.hi(act, n, slot, False)

            gelu(0, 0)
            hi_u(U_EXP + 2, 0)
            w_hi(0, 0)
            gelu(1, 1)
            hi_u(U_EXP + 3, 1)
            w_hi(1, 1)
            hi_v(1, U_EXP + 4, 0)
            with act.Fori(1, 31) as i:
                for s in range(2):
                    n = 2 * i + s
                    gelu(n, s)
                    hi_u(2 * n + (U_EXP + 1), 1)
                    w_hi(n, s)
                    hi_v(n, 2 * n + (U_EXP + 2), 0)
            gelu(62, 0)
            hi_u(U_EXP + 125, 1)
            w_hi(62, 0)
            hi_v(62, U_EXP + 126, 0)
            gelu(63, 1)
            hi_u(U_EXP + 127, 1)
            w_hi(63, 1)

        @block.vector
        def _(dve):
            dve.sem_inc(y_added, NO)
            nc.vector.memset(K.y[:, :, :], 0.0).then_inc(zeroed, 1)
            dve.wait_ge(zeroed, 1)

            def weight(n, s):
                dve.wait_ge(a_done, 4 * n + 4)
                dve.wait_ge(g_in[s], 8 * (n - s) + 16)
                if not is0(n):
                    dve.wait_ge(wh_done, n)
                    dve.wait_ge(wl_done, n)
                for c in range(2):
                    ins = nc.vector.tensor_tensor(W[:, c, :].rearrange("p (b t) -> p b t", t=TB),
                                                  A[:, c, :].rearrange("p (b t) -> p b t", t=TB), G[s][:, :, c, :], ALU.mult)
                ins.then_inc(w_done, 1)

            def w_lo(n, s):
                dve.wait_ge(wh_done, n + 1)
                nc.vector.tensor_tensor(Wl[s][:, :, :], W[:, :, :], Wh[s][:, :, :].bitcast(F32), ALU.subtract).then_inc(wl_done, 1)

            def add(n, lo, hi):
                for o in range(lo, hi):
                    t, d = OUTS[o]
                    dve.wait_ge(y_mm, NO * n + (o + 1))
                    v = K.y[:, t, d * 512:(d + 1) * 512]
                    nc.vector.tensor_tensor(v, v, ps_y[o % NB][:, :], ALU.add).then_inc(y_added, 1)

            def step(n, s, first_unit, second_unit):
                add(n, 0, 1)
                weight(n + 1, 1 - s)
                add(n, 1, 2)
                S.lo(dve, first_unit, 1)
                add(n, 2, 3)
                w_lo(n + 1, 1 - s)
                add(n, 3, NO)
                if second_unit is not None:
                    S.lo(dve, second_unit, 0)

            weight(0, 0)
            S.lo(dve, U_EXP + 2, 0)
            w_lo(0, 0)
            with dve.Fori(0, 31) as i:
                for s in range(2):
                    n = 2 * i + s
                    step(n, s, 2 * n + (U_EXP + 3), 2 * n + (U_EXP + 4))
            step(62, 0, U_EXP + 127, None)
            add(63, 0, NO)



def phase_final(nc, K, ctx):
    sem = K.phase_semaphores(ctx)
    sb = lambda n, s, d=F32: ctx.enter_context(nc.sbuf_tensor(n, s, d))
    x, g2, w = K.res, K.gate2, K.norm_w
    sq = sb("f_sq", [P, D]); ss = sb("f_ss", [P, NT])
    scaled = sem("f_scaled"); res = sem("f_res"); sq_done = sem("f_sq_done"); ms_done = sem("f_ms"); rt_done = sem("f_rt")
    r_done = sem("f_r"); o_done = sem("f_o"); out = sem("f_out")

    with nc.Block() as block:
        @block.sync
        def _(sp):
            for t in range(NT):
                sp.wait_ge(o_done, t + 1)
                sp.dma_start(K.out_y[t * P:(t + 1) * P, :], x[:, t, :]).then_inc(out, 16)
            sp.wait_ge(out, 16 * NT)

        @block.vector
        def _(dve):
            def residual(t):
                nc.vector.tensor_tensor(K.y[:, t, :], K.y[:, t, :], g2[:, group(t), :], ALU.mult).then_inc(scaled, 1)
                dve.wait_ge(scaled, t + 1)
                nc.vector.tensor_tensor(x[:, t, :], x[:, t, :], K.y[:, t, :], ALU.add).then_inc(res, 1)

            def mean_square(t):
                dve.wait_ge(sq_done, t + 1)
                nc.vector.tensor_scalar(ss[:, t:t + 1], ss[:, t:t + 1], 1.0 / D, EPS, ALU.mult, ALU.add).then_inc(ms_done, 1)

            def norm(t):
                dve.wait_ge(rt_done, t + 1)
                nc.vector.reciprocal(ss[:, t:t + 1], ss[:, t:t + 1]).then_inc(r_done, 1)
                dve.wait_ge(r_done, t + 1)
                nc.vector.scalar_tensor_tensor(x[:, t, :], x[:, t, :], ss[:, t:t + 1], w[:, :], ALU.mult, ALU.mult).then_inc(o_done, 1)

            dve.wait_ge(K.final_in, 64)
            for t in range(NT + 2):
                if t < NT:
                    residual(t)
                if 1 <= t <= NT:
                    mean_square(t - 1)
                if t >= 2:
                    norm(t - 2)

        @block.scalar
        def _(act):
            for t in range(NT + 1):
                if t < NT:
                    act.wait_ge(res, t + 1)
                    if t:
                        act.wait_ge(sq_done, t)
                    nc.scalar.activation(sq[:, :], x[:, t, :], ACT.Square, accum_out=ss[:, t:t + 1]).then_inc(sq_done, 1)
                if t:
                    act.wait_ge(ms_done, t)
                    nc.scalar.activation(ss[:, t - 1:t], ss[:, t - 1:t], ACT.Sqrt).then_inc(rt_done, 1)



PHASES = [phase_modulate, phase_tokens]


def run_phase(nc, K, phase):
    K.sems = []

    def phase_semaphores(ctx):
        def sem(name):
            K.sems.append(ctx.enter_context(nc.semaphore(name)))
            return K.sems[-1]
        return sem

    def pool_dma(i):
        return K.pool_dma_sems[i]

    K.phase_semaphores, K.pool_dma = phase_semaphores, pool_dma
    with ExitStack() as ctx:
        phase(nc, K, ctx)
        with nc.Block() as block:
            @block.gpsimd
            def _(pool):
                for s in K.sems:
                    pool.sem_clear(s)


def build(nc, K):
    ctx = ExitStack()
    with ctx:
        sb = lambda n, s, d=F32: ctx.enter_context(nc.sbuf_tensor(n, s, d))
        sem = lambda n: ctx.enter_context(nc.semaphore(n))
        K.raw = [sb(f"w_raw{i}", [P, 8 * UC]) for i in range(2)]
        K.whi = [sb(f"w_hi{i}", [P, 8 * UC], F32R) for i in range(2)]
        K.wlo = [sb(f"w_lo{i}", [P, 8 * UC], F32R) for i in range(2)]
        K.w_loaded = [sem("w_loaded0"), sem("w_loaded1")]
        K.pool_dma_sems = [sem(f"pool_dma{i}") for i in range(NT + 7)]
        K.w_hi_done, K.w_lo_done, K.hilo_free = (sem(n) for n in ("w_hi_done", "w_lo_done", "hilo_free"))
        K.ident, K.ones, K.iota = sb("ident", [P, P]), sb("ones", [P, P]), sb("iota", [P, P])
        K.tri_le, K.tri_gt, K.tri_ge, K.tri_lt = (sb(n, [P, P]) for n in ("tri_le", "tri_gt", "tri_ge", "tri_lt"))
        K.mul1, K.add1, K.mul2, K.add2 = (sb(n, [P, KD, 2]) for n in ("mul1", "add1", "mul2", "add2"))
        K.silu_c = sb("silu_c", [P, KD, 2])
        K.dt, K.dtA = sb("dt", [P, NT, 64]), sb("dtA", [P, NT, 64])
        K.decay = sb("decay", [P, 6, NT * HEADS])
        with ExitStack() as h_ctx:
            K.hT = [h_ctx.enter_context(nc.sbuf_tensor(f"hT{i}", [P, KD, T], F32R)) for i in range(2)]
            for phase in PHASES:
                run_phase(nc, K, phase)
            with ExitStack() as o:
                K.QT = o.enter_context(nc.sbuf_tensor("QT", [P, KD, T], F32))
                with ExitStack() as kv:
                    K.KT = kv.enter_context(nc.sbuf_tensor("KT", [P, NKV, T + PAST], F32))
                    K.vals = kv.enter_context(nc.sbuf_tensor("vals", [P, NT + 1, NKV * HD], F32))
                    for phase in (phase_qk, phase_attention):
                        run_phase(nc, K, phase)
                run_phase(nc, K, phase_merge)
            run_phase(nc, K, phase_ssd)
        K.so_free = sem("so_free")
        with ExitStack() as yc:
            K.yT = [yc.enter_context(nc.sbuf_tensor(f"yT{i}", [P, DI // P, T], F32R)) for i in range(2)]
            for phase in (phase_ssd_norm, phase_ssd_out):
                run_phase(nc, K, phase)
        K.h2T = [sb(f"h2T{i}", [P, KD, T], F32R) for i in range(2)]
        run_phase(nc, K, phase_mix_out)
        with ExitStack() as s:
            K.slotsT = s.enter_context(nc.sbuf_tensor("slotsT", [P, 3, T], F32))
            for phase in (phase_route, phase_gates):
                run_phase(nc, K, phase)
        K.y = sb("y_peer", [P, NT, D])
        K.res, K.gate2, K.norm_w = sb("f_x", [P, NT, D]), sb("f_g2", [P, 2, D]), sb("f_w", [P, D])
        K.final_in = sem("f_in")
        for phase in (phase_experts, phase_final):
            run_phase(nc, K, phase)


def pack_units(w, cols=UC):
    k = w.shape[0] // P
    return w.reshape(k, P, w.shape[1] // cols, cols).transpose(2, 1, 0, 3).reshape(-1, P, k * cols)


def kernel(**inputs):
    import numpy as np
    import concourse.bacc as bacc
    from concourse.bass_utils import run_bass_kernel_spmd

    a = {k: np.asarray(v) for k, v in inputs.items()}
    cols = lambda v, n: np.ascontiguousarray(v.reshape(n, P).T)
    w_in = a["w_in"][0]
    z, xs, bc, cc, dtw, qkv, ga, gb = np.split(w_in, [2048, 4096, 5120, 6144, 6208, 7744, 8768], axis=1)
    tok = pack_units(np.concatenate([z, qkv], 1))
    at = pack_units(a["w_attn_out"][0])
    gbu, gau = pack_units(gb), pack_units(ga)
    merge = np.concatenate([np.stack([gbu, at], 1).reshape(8, P, 2048), gau])
    ssd = np.stack([pack_units(xs), pack_units(np.stack([bc.reshape(D, 8, P), cc.reshape(D, 8, P)], 2).reshape(D, 2048))], 1).reshape(16, P, 2048)
    wso = a["w_ssd_out"][0]
    so = np.stack([pack_units(wso[0:1024]), pack_units(wso[1024:2048])], 1).reshape(8, P, 2048)
    u = a["peer_u"][0].reshape(64, 256, 8, P).transpose(0, 3, 2, 1).reshape(64, P, 2048)
    v = a["peer_v"][0].reshape(64, 2, P, D).transpose(0, 2, 1, 3).reshape(64, P, 2048)
    exp = np.concatenate([u[0:1], np.stack([u[1:], v[:-1]], 1).reshape(126, P, 2048), v[-1:]])
    stream = np.concatenate([tok, merge, ssd, so, pack_units(a["w_o"][0]), pack_units(a["w_pq"][0]), exp])

    pos = np.arange(512)
    inv = np.float32(10000.0) ** (-np.arange(16, dtype=np.float32) / np.float32(16))
    ang = np.stack([(pos // 64).astype(np.float32)[:, None] * inv, (pos % 64).astype(np.float32)[:, None] * inv], 1)
    rope = np.stack([np.cos(ang), np.sin(ang)]).astype(np.float32).reshape(2, 4, P, 32).transpose(2, 0, 1, 3)

    arrays = {
        "x": np.concatenate([a["x_prompt"][0], a["x_sample"][0]]),
        "c_cols": np.stack([a["c_ctx"], a["c"][0]]).reshape(2, KD, P).transpose(2, 1, 0),
        "w_ada": pack_units(a["w_ada"][0]),
        "b_ada": a["b_ada"], "b_ada_cols": cols(a["b_ada"], 48),
        "norm1_cols": cols(a["norm1_w"], KD), "norm2_cols": cols(a["norm2_w"], KD),
        "w_stream": stream,
        "w_dt": pack_units(dtw, 64)[0],
        "dt_bias_f": a["dt_bias_f"], "dt_bias_b": a["dt_bias_b"], "a_log_f": a["a_log_f"], "a_log_b": a["a_log_b"],
        "rope": rope,
        "q_norm_w": a["q_norm_w"], "k_norm_w": a["k_norm_w"],
        "cache_k": a["cache_k"][0, 0].reshape(PAST, NKV * HD), "cache_v": a["cache_v"][0, 0].reshape(PAST, NKV * HD),
        "conv_w_cols": a["conv_w"][0].reshape(5, 32, P).transpose(2, 1, 0), "conv_b_cols": cols(a["conv_b"], 32),
        "d_skip": a["d_skip"],
        "state_f": a["state_ssm_fwd"][0, 0].transpose(2, 0, 1), "state_b": a["state_ssm_bwd"][0, 0].transpose(2, 0, 1),
        "ssd_norm_w": a["ssd_norm_w"],
        "keys_t": a["peer_keys"][0].reshape(16, NKEYS, P).transpose(2, 0, 1),
        "final_norm_w": a["final_norm_w"].reshape(1, D),
    }
    arrays = {k: np.ascontiguousarray(v) for k, v in arrays.items()}
    nc = bacc.Bacc("TRN2", target_bir_lowering=False, num_devices=1)
    K = Shared()
    for name, v in arrays.items():
        setattr(K, name, nc.dram_tensor("in_" + name, v.shape, F32, kind="ExternalInput").ap())
    outs = {"y": (T, D), "new_k": (P, 256), "new_v": (P, 256), "new_sf": (P, HEADS, HP), "new_sb": (P, HEADS, HP)}
    scratch = {"gates": (2, 2 * D), "z_dram": (T, DI), "qkv_dram": (T, 1536), "sga_dram": (KD, P, T), "merged_dram": (KD, P, T), "y_dram": (T, DI), "x2_dram": (T, D),
               "g_dram": (T // 64, P, P, 64)}
    for name, shape in outs.items():
        setattr(K, "out_" + name, nc.dram_tensor("out_" + name, shape, F32, kind="ExternalOutput").ap())
    for name, shape in scratch.items():
        setattr(K, name, nc.dram_tensor(name, shape, F32, kind="Internal").ap())
    build(nc, K)
    r = run_bass_kernel_spmd(nc, [{"in_" + k: v for k, v in arrays.items()}], core_ids=[0]).results[0]
    y = r["out_y"]
    state = lambda s: np.ascontiguousarray(s.transpose(1, 2, 0)).reshape(1, 1, HEADS, HP, NS)
    return (y[0:P].reshape(1, P, D), y[P:].reshape(1, 512, D), r["out_new_k"].reshape(1, 1, P, NKV, HD),
            r["out_new_v"].reshape(1, 1, P, NKV, HD), state(r["out_new_sf"]), state(r["out_new_sb"]))
```
